# Optimizing a Trainium2 kernel written in Bass

```python
import jax, jax.numpy as jnp
from jax import lax
import numpy as np

D_MODEL = 1024
BATCH = 1
SEQ = 256
DEPTH = 1
DEC_BATCH = 1
DEC_SEQ = 256
PAST_LEN = 128

GRID_W = 64
NA_HEADS = 8
NA_HEAD_DIM = 64
NA_WIDTH = NA_HEADS * NA_HEAD_DIM
NA_ROWS = 8
NA_COLS = 16
NA_KEY_COLS = 2 * NA_COLS
SG_WIDTH = 512
SG_GROUPS = 4
SG_GROUP_DIM = SG_WIDTH // SG_GROUPS
SG_CHUNK = 128
CV_WIDTH = 512
CV_KERNEL = 31
IN_WIDTH = 3 * NA_WIDTH + 2 * SG_WIDTH + 2 * CV_WIDTH
SPLIT_POINTS = (NA_WIDTH, 2 * NA_WIDTH, 3 * NA_WIDTH, 3 * NA_WIDTH + SG_WIDTH,
                3 * NA_WIDTH + 2 * SG_WIDTH, 3 * NA_WIDTH + 2 * SG_WIDTH + CV_WIDTH)
N_BRANCH = 3
N_EXPERTS = 16
N_GROUPS = 4
EXPERTS_PER_GROUP = N_EXPERTS // N_GROUPS
TOP_K = 2
EXPERT_FF = 512
ALPHA = (2 * DEPTH) ** 0.25
BETA = (8 * DEPTH) ** -0.25
LN_EPS = 1e-5
NEG_INF = -1e30

kernel_name = "hybrid_na_sgmlp_conv_moe_encoder"

def layer_norm(x, g, b):
    xf = x.astype(jnp.float32)
    mu = jnp.mean(xf, axis=-1, keepdims=True)
    var = jnp.mean(jnp.square(xf - mu), axis=-1, keepdims=True)
    y = (xf - mu) * lax.rsqrt(var + LN_EPS) * g.astype(jnp.float32) + b.astype(jnp.float32)
    return y.astype(x.dtype)

def neighbourhood_attention(q, k, v, rpb):
    B, L, H, Dh = q.shape
    rows = L // GRID_W
    wr = min(NA_ROWS, rows)
    n_cb = GRID_W // NA_COLS
    r = np.arange(rows)
    key_rows = np.clip(r - wr // 2, 0, rows - wr)[:, None] + np.arange(wr)
    q_cols = np.arange(GRID_W).reshape(n_cb, NA_COLS)
    key_cols = (np.clip(q_cols[:, 0] - NA_COLS // 2, 0, GRID_W - NA_KEY_COLS)[:, None]
                + np.arange(NA_KEY_COLS))
    col_start = np.clip(q_cols - NA_COLS // 2, 0, GRID_W - NA_COLS)
    kc = key_cols[:, None, :]
    col_valid = (kc >= col_start[:, :, None]) & (kc < col_start[:, :, None] + NA_COLS)
    row_off = key_rows - r[:, None] + NA_ROWS - 1
    col_off = np.clip(kc - q_cols[:, :, None] + NA_COLS - 1, 0, 2 * NA_COLS - 2)
    bias = rpb.astype(jnp.float32)[:, row_off[:, None, None, :, None], col_off[None, :, :, None, :]]
    qg = q.reshape(B, rows, n_cb, NA_COLS, H, Dh)
    kg = k.reshape(B, rows, GRID_W, H, Dh)[:, key_rows[:, None, :, None], key_cols[None, :, None, :]]
    vg = v.reshape(B, rows, GRID_W, H, Dh)[:, key_rows[:, None, :, None], key_cols[None, :, None, :]]
    s = jnp.einsum('brjqhd,brjwkhd->bhrjqwk', qg * (Dh ** -0.5), kg).astype(jnp.float32) + bias
    s = jnp.where(col_valid[:, :, None, :], s, NEG_INF)
    p = jax.nn.softmax(s, axis=(-2, -1)).astype(v.dtype)
    o = jnp.einsum('bhrjqwk,brjwkhd->brjqhd', p, vg)
    return o.reshape(B, L, H * Dh)

def token_mixer(x, w_in, b_in, w_gate, b_gate, rpb, w_a_o, sg_ln_g, sg_ln_b, w_s, b_s, w_b_o,
                conv_w, conv_b, cv_ln_g, cv_ln_b, w_c_o, w_o, b_o):
    B, L, D = x.shape
    z = x @ w_in + b_in
    q, k, v, u_sg, v_sg, glu_a, glu_g = jnp.split(z, SPLIT_POINTS, axis=-1)
    hd = (B, L, NA_HEADS, NA_HEAD_DIM)
    a = neighbourhood_attention(q.reshape(hd), k.reshape(hd), v.reshape(hd), rpb) @ w_a_o
    u = jax.nn.gelu(u_sg)
    vs = layer_norm(jax.nn.gelu(v_sg), sg_ln_g, sg_ln_b)
    vs = vs.reshape(B, L // SG_CHUNK, SG_CHUNK, SG_GROUPS, SG_GROUP_DIM)
    sv = jnp.einsum('gts,bnsgc->bntgc', w_s, vs) + b_s.T[:, :, None]
    bb = (u * sv.reshape(B, L, SG_WIDTH)) @ w_b_o
    h = glu_a * jax.nn.sigmoid(glu_g)
    h = lax.conv_general_dilated(h, conv_w[:, None, :], window_strides=(1,), padding='SAME',
                                 dimension_numbers=('NWC', 'WIO', 'NWC'),
                                 feature_group_count=CV_WIDTH) + conv_b
    c = jax.nn.silu(layer_norm(h, cv_ln_g, cv_ln_b)) @ w_c_o
    g = jax.nn.sigmoid((x @ w_gate + b_gate).astype(jnp.float32)).astype(x.dtype)
    g = g.reshape(B, L, N_BRANCH, D)
    merged = g[:, :, 0] * a + g[:, :, 1] * bb + g[:, :, 2] * c
    return merged @ w_o + b_o

def grouped_moe(x, w_router, b_router, w_e1, w_e3, w_e2):
    B, L, D = x.shape
    xt = x.reshape(B * L, D)
    s = jax.nn.sigmoid((xt @ w_router).astype(jnp.float32))
    sb = (s + b_router.astype(jnp.float32)).reshape(-1, N_GROUPS, EXPERTS_PER_GROUP)
    group_score = lax.top_k(sb, TOP_K)[0].sum(-1)
    gmask = jnp.argmax(group_score, axis=-1)[:, None] == jnp.arange(N_GROUPS)
    masked = jnp.where(gmask[:, :, None], sb, -jnp.inf).reshape(-1, N_EXPERTS)
    _, idx = lax.top_k(masked, TOP_K)
    w = jnp.take_along_axis(s, idx, axis=-1)
    w = w / jnp.sum(w, axis=-1, keepdims=True)
    gates = jnp.sum(jax.nn.one_hot(idx, N_EXPERTS, dtype=jnp.float32) * w[..., None], axis=1).astype(x.dtype)
    y = jnp.zeros_like(xt)
    for e in range(N_EXPERTS):
        h = jax.nn.silu(xt @ w_e1[e]) * (xt @ w_e3[e])
        y = y + gates[:, e:e + 1] * (h @ w_e2[e])
    return y.reshape(B, L, D)

def run_trunk(x, emb_ln_g, emb_ln_b, w_in, b_in, w_gate, b_gate, rpb, w_a_o, sg_ln_g, sg_ln_b,
              w_s, b_s, w_b_o, conv_w, conv_b, cv_ln_g, cv_ln_b, w_c_o, w_o, b_o, ln1_g, ln1_b,
              w_router, b_router, w_e1, w_e3, w_e2, ln2_g, ln2_b):
    x = layer_norm(x, emb_ln_g, emb_ln_b)
    for l in range(DEPTH):
        m = token_mixer(x, w_in[l], b_in[l], w_gate[l], b_gate[l], rpb[l], w_a_o[l], sg_ln_g[l], sg_ln_b[l],
                        w_s[l], b_s[l], w_b_o[l], conv_w[l], conv_b[l], cv_ln_g[l], cv_ln_b[l], w_c_o[l],
                        w_o[l], b_o[l])
        x = layer_norm(ALPHA * x + m, ln1_g[l], ln1_b[l])
        f = grouped_moe(x, w_router, b_router, w_e1[l], w_e3[l], w_e2[l])
        x = layer_norm(ALPHA * x + f, ln2_g[l], ln2_b[l])
    return x

def setup_inputs(seed: int = 0) -> dict:
    key = jax.random.key(seed)
    ks = iter(jax.random.split(key, 40))

    def nrm(shape, scale):
        return jax.random.normal(next(ks), shape, jnp.float32) * scale

    D = D_MODEL
    x_prompt = nrm((BATCH, SEQ, D), 1.0)
    x_sample = nrm((DEC_BATCH, DEC_SEQ, D), 1.0)
    emb_ln_g = 1.0 + nrm((D,), 0.02)
    emb_ln_b = nrm((D,), 0.02)
    col_scale = jnp.concatenate([jnp.ones((2 * NA_WIDTH,), jnp.float32),
                                 jnp.full((NA_WIDTH,), BETA, jnp.float32),
                                 jnp.ones((2 * SG_WIDTH + 2 * CV_WIDTH,), jnp.float32)])
    w_in = nrm((DEPTH, D, IN_WIDTH), D ** -0.5) * col_scale
    b_in = nrm((DEPTH, IN_WIDTH), 0.02)
    w_gate = nrm((DEPTH, D, N_BRANCH * D), D ** -0.5)
    b_gate = nrm((DEPTH, N_BRANCH * D), 0.02)
    rpb = nrm((DEPTH, NA_HEADS, 2 * NA_ROWS - 1, 2 * NA_COLS - 1), 0.1)
    w_a_o = nrm((DEPTH, NA_WIDTH, D), NA_WIDTH ** -0.5)
    sg_ln_g = 1.0 + nrm((DEPTH, SG_WIDTH), 0.02)
    sg_ln_b = nrm((DEPTH, SG_WIDTH), 0.02)
    w_s = nrm((DEPTH, SG_GROUPS, SG_CHUNK, SG_CHUNK), 0.5 * SG_CHUNK ** -0.5)
    b_s = 1.0 + nrm((DEPTH, SG_GROUPS, SG_CHUNK), 0.01)
    w_b_o = nrm((DEPTH, SG_WIDTH, D), SG_WIDTH ** -0.5)
    conv_w = nrm((DEPTH, CV_KERNEL, CV_WIDTH), CV_KERNEL ** -0.5)
    conv_b = nrm((DEPTH, CV_WIDTH), 0.02)
    cv_ln_g = 1.0 + nrm((DEPTH, CV_WIDTH), 0.02)
    cv_ln_b = nrm((DEPTH, CV_WIDTH), 0.02)
    w_c_o = nrm((DEPTH, CV_WIDTH, D), CV_WIDTH ** -0.5)
    w_o = nrm((DEPTH, D, D), BETA * D ** -0.5)
    b_o = nrm((DEPTH, D), 0.02)
    ln1_g = 1.0 + nrm((DEPTH, D), 0.02)
    ln1_b = nrm((DEPTH, D), 0.02)
    w_router = nrm((D, N_EXPERTS), D ** -0.5)
    b_router = nrm((N_EXPERTS,), 0.01)
    w_e1 = nrm((DEPTH, N_EXPERTS, D, EXPERT_FF), D ** -0.5)
    w_e3 = nrm((DEPTH, N_EXPERTS, D, EXPERT_FF), D ** -0.5)
    w_e2 = nrm((DEPTH, N_EXPERTS, EXPERT_FF, D), BETA * EXPERT_FF ** -0.5)
    ln2_g = 1.0 + nrm((DEPTH, D), 0.02)
    ln2_b = nrm((DEPTH, D), 0.02)
    return {"x_prompt": x_prompt, "x_sample": x_sample, "emb_ln_g": emb_ln_g, "emb_ln_b": emb_ln_b,
            "w_in": w_in, "b_in": b_in, "w_gate": w_gate, "b_gate": b_gate, "rpb": rpb, "w_a_o": w_a_o,
            "sg_ln_g": sg_ln_g, "sg_ln_b": sg_ln_b, "w_s": w_s, "b_s": b_s, "w_b_o": w_b_o,
            "conv_w": conv_w, "conv_b": conv_b, "cv_ln_g": cv_ln_g, "cv_ln_b": cv_ln_b, "w_c_o": w_c_o,
            "w_o": w_o, "b_o": b_o, "ln1_g": ln1_g, "ln1_b": ln1_b, "w_router": w_router,
            "b_router": b_router, "w_e1": w_e1, "w_e3": w_e3, "w_e2": w_e2, "ln2_g": ln2_g, "ln2_b": ln2_b}

def reference(x_prompt, x_sample, emb_ln_g, emb_ln_b, w_in, b_in, w_gate, b_gate, rpb, w_a_o,
              sg_ln_g, sg_ln_b, w_s, b_s, w_b_o, conv_w, conv_b, cv_ln_g, cv_ln_b, w_c_o, w_o, b_o,
              ln1_g, ln1_b, w_router, b_router, w_e1, w_e3, w_e2, ln2_g, ln2_b):
    weights = (emb_ln_g, emb_ln_b, w_in, b_in, w_gate, b_gate, rpb, w_a_o, sg_ln_g, sg_ln_b,
               w_s, b_s, w_b_o, conv_w, conv_b, cv_ln_g, cv_ln_b, w_c_o, w_o, b_o, ln1_g, ln1_b,
               w_router, b_router, w_e1, w_e3, w_e2, ln2_g, ln2_b)
    y_prompt = run_trunk(x_prompt, *weights)
    y_sample = run_trunk(x_sample, *weights)
    return (y_prompt, y_sample)


_drawn_inputs = setup_inputs


def setup_inputs(seed=0):
    import zlib

    import numpy as np

    out = dict(_drawn_inputs(seed))
    spreads = {}
    factors = {'b_gate': 4.28,
     'rpb': 3.386,
     'sg_ln_g': 8.0,
     'sg_ln_b': 6.225,
     'b_s': 4.319,
     'cv_ln_g': 3.726,
     'cv_ln_b': 3.226,
     'ln2_g': 2.932,
     'ln2_b': 2.769}
    for name, (base, spread) in spreads.items():
        noise = np.random.default_rng([zlib.crc32(name.encode()), seed]).standard_normal(out[name].shape)
        drawn = base * np.exp(spread * noise) if base else spread * noise
        out[name] = __import__('jax').numpy.asarray(drawn.astype(out[name].dtype))
    for name, factor in factors.items():
        out[name] = (out[name] * factor).astype(out[name].dtype)
    return out
```

```python
from contextlib import ExitStack

import concourse.bass as bass
from concourse import mybir

P = 128
F32 = mybir.dt.float32
F32R = mybir.dt.float32r
I32 = mybir.dt.int32
ALU = mybir.AluOpType
ACT = mybir.ActivationFunctionType
AX = mybir.AxisListType

D = 1024
DC = D // P
T = 512
TT = T // P
SEQ = 256
W = 512
WC = W // P
GRID = 64
ROWS = SEQ // GRID
QCOLS = 16
KCOLS = 32
WINDOW = (0, 8, 24, 32)
PATTERN = (0, 1, 1, 2)
SHIFT = (0, -8, -16)
TAPS = 31
HALO = TAPS // 2
EXPERTS = 16
SLOTS = 128
FF = 512
ALPHA = 2.0 ** 0.25
EPS = 1e-5
QSCALE = 64 ** -0.5

RAW = 6
SPLIT = 3
UNIT = 1024

C_IDENT, C_BEFORE, C_IOTA, C_ONES = 0, 128, 256, 384
C_TOKEN = 512
C_HIGHER = 516
C_MASK = 532
C_ALL = C_MASK + 3 * KCOLS

V_IN, V_GATE, V_CONVB, V_CVG, V_CVB, V_ALL = 0, 28, 52, 56, 60, 64

U_GLU, U_V, U_VSG, U_QK, U_USG = 0, 8, 12, 16, 24
U_MERGE = 28
U_WO = U_MERGE + 36
U_MOE = U_WO + 8
U_OVER = U_MOE + 12 * EXPERTS


class Banks:

    def __init__(self):
        self.used, self.full, self.at = [0] * 8, [0] * 8, {}

    def use(self, name, bank, unit=None):
        self.loop(1, 0, [(name, bank, unit)])

    def loop(self, times, units, uses):
        used, full = list(self.used), list(self.full)
        for name, bank, unit in uses:
            self.at[name] = [bank, used[bank], full[bank], unit, units]
            used[bank] += 1
            full[bank] += unit is None
        for name, bank, _ in uses:
            self.at[name] += [used[bank] - self.used[bank], full[bank] - self.full[bank]]
        self.used = [a + (b - a) * times for a, b in zip(self.used, used)]
        self.full = [a + (b - a) * times for a, b in zip(self.full, full)]


def plan_banks():
    b = Banks()
    b.use("vectors", 6)
    b.use("w_s", 7)
    for t in range(TT):
        for h in range(2):
            b.use(("x0T", t, h), 2 * (t % 2) + h)
    for c in range(WC):
        b.use(("glu_a", c), 4 + 2 * (c % 2), U_GLU + 2 * c)
        b.use(("glu_g", c), 5 + 2 * (c % 2), U_GLU + 2 * c + 1)
    for t in range(TT):
        b.use(("v", t), t, U_V + 3)
    for t in range(TT):
        b.use(("vsg", t), 4 + t, U_VSG + 3)
    for c in range(WC):
        b.use(("q", c), 4 + 2 * (c % 2), U_QK + 2 * c)
        b.use(("k", c), 5 + 2 * (c % 2), U_QK + 2 * c + 1)
    for g in range(8):
        b.use(("scores", g), g % 2)
        b.use(("probsT", g), 2)
        b.use(("attended", g), 3)
    for c in range(WC):
        b.use(("usg", c), 4 + c % 2, U_USG + c)
        b.use(("spatial", c), 6 + c % 2)
    b.use("conv_mean", 0)
    b.use("conv_var", 1)
    uses = []
    for r in range(2):
        for d in range(2):
            uses += [(("gate", r, d, n), 3 * d + n, U_MERGE + 9 * r + 3 * d + n) for n in range(3)]
        for n, bank in enumerate((6, 0, 2)):
            uses += [(("branch", r, d, n), bank + d, U_MERGE + 9 * r + 6 + n) for d in range(2)]
    b.loop(2, 18, uses)
    for n in range(2):
        for t in range(TT):
            b.use(("mixed", n, t), 4 * n + t, U_WO + 4 * n + 3)
    for t in range(TT):
        for h in range(2):
            b.use(("x1T", t, h), 2 * t + h)
    b.use("router", 0)
    b.use("position", 1)
    return b


M_H1, M_H3, M_Y, M_XT, M_HT, M_INFO = 0, 1, 2, 4, 6, 7


def encoder_layer(nc, A, out_prompt, out_sample):
    banks = plan_banks()
    ctx = ExitStack()
    m_used, m_full = list(banks.used), list(banks.full)

    def sem(name):
        return ctx.enter_context(nc.semaphore(name))

    x0_dram = nc.dram_tensor("x0_scratch", (T, D), F32).ap()
    v_dram = nc.dram_tensor("v_scratch", (T, W), F32).ap()
    rpb_dram = nc.dram_tensor("rpb_scratch", (QCOLS, A["rpb"].shape[1] * A["rpb"].shape[2] * A["rpb"].shape[3]),
                              F32).ap()
    x1_dram = nc.dram_tensor("x1_scratch", (T, D), F32).ap()
    y_dram = nc.dram_tensor("y_scratch", (2 * T, D), F32).ap()

    def sb(stack, name, shape, dt=F32):
        return stack.enter_context(nc.sbuf_tensor(name, [P] + shape, dt))

    raw = sb(ctx, "raw", [RAW, UNIT])
    w_hi = sb(ctx, "w_hi", [SPLIT, UNIT], F32R)
    w_lo = sb(ctx, "w_lo", [SPLIT, UNIT], F32R)
    const = sb(ctx, "const", [C_ALL])
    vec = sb(ctx, "vec", [V_ALL])
    conv_col = sb(ctx, "conv_col", [TAPS, WC])
    stats = sb(ctx, "stats", [TT, 2, 6])
    mv = sb(ctx, "mv", [TT, 2])
    rstd = sb(ctx, "rstd", [TT])
    var_eps = sb(ctx, "var_eps", [TT])
    minus_half = sb(ctx, "minus_half", [TT])
    neg_max = sb(ctx, "neg_max", [2, 4])
    exp_sum = sb(ctx, "exp_sum", [2, 4])
    exp_inv = sb(ctx, "exp_inv", [2, 4])
    ident = const[:, C_IDENT:C_IDENT + P]
    before = const[:, C_BEFORE:C_BEFORE + P]
    iota = const[:, C_IOTA:C_IOTA + P]
    ones = const[:, C_ONES:C_ONES + P]
    token = const[:, C_TOKEN:C_TOKEN + TT]

    mix = ExitStack()
    xT_hi = sb(mix, "xT_hi", [DC, T], F32R)
    xT_lo = sb(mix, "xT_lo", [DC, T], F32R)
    branch_hi = [sb(mix, f"branch{n}_hi", [WC, T], F32R) for n in range(2)]
    branch_lo = [sb(mix, f"branch{n}_lo", [WC, T], F32R) for n in range(2)]
    conv_in = sb(mix, "conv_in", [WC, 2, SEQ + 2 * HALO])
    conv = sb(mix, "conv", [WC, T])
    early = ExitStack()
    qT = sb(early, "qT", [WC, T])
    kT = sb(early, "kT", [WC, T])
    v_win = sb(early, "v_win", [2, 4, W])
    bias = sb(early, "bias", [WC, 4, P])
    probs = sb(early, "probs", [2, W])
    probsT = sb(early, "probsT", [W])
    vs = sb(early, "vs", [TT, W])
    w_sT = sb(early, "w_sT", [4, P])
    b_s = sb(early, "b_s", [4, P])
    sg_g = sb(early, "sg_g", [W])
    sg_b = sb(early, "sg_b", [W])
    bv = sb(early, "bv", [W])
    bvs = sb(early, "bvs", [W])
    tmp = sb(early, "tmp", [2, W])
    conv_odd = sb(early, "conv_odd", [W])
    tap = sb(early, "tap", [W])
    early.close()
    first = ExitStack()
    x_in = sb(first, "x_in", [TT, D])
    emb_g = sb(first, "emb_g", [D])
    emb_b = sb(first, "emb_b", [D])
    rows_v = sb(first, "rows_v", [P])
    rows_c = sb(first, "rows_c", [P])
    w_s = sb(first, "w_s_in", [4, P])
    first.close()
    late = ExitStack()
    branch_hi.append(sb(late, "branch2_hi", [WC, T], F32R))
    branch_lo.append(sb(late, "branch2_lo", [WC, T], F32R))
    mT_hi = sb(late, "mT_hi", [DC, T], F32R)
    mT_lo = sb(late, "mT_lo", [DC, T], F32R)
    gate = sb(late, "gate", [2, 3, T])
    part = sb(late, "part", [2, T])
    merged = sb(late, "merged", [2, T])
    late.close()
    mix.close()

    x1 = sb(ctx, "x1", [TT, D])
    ln1_g = sb(ctx, "ln1_g", [D])
    ln1_b = sb(ctx, "ln1_b", [D])
    b_o = sb(ctx, "b_o", [D])
    moe = ExitStack()
    ln2_g = sb(moe, "ln2_g", [D])
    ln2_b = sb(moe, "ln2_b", [D])
    x1T = sb(moe, "x1T", [DC, T])
    w_router = sb(moe, "w_router_in", [DC, EXPERTS])
    b_router = sb(moe, "b_router_in", [EXPERTS])
    r_s = sb(moe, "r_s", [TT, 4, 4])
    r_sb = sb(moe, "r_sb", [TT, 4, 4])
    r_ge = sb(moe, "r_ge", [TT, 4, 4])
    r_rank = sb(moe, "r_rank", [TT, 4, 4])
    r_sel = sb(moe, "r_sel", [TT, 4, 4])
    r_tmp = sb(moe, "r_tmp", [TT, 4, 4])
    r_kth = sb(moe, "r_kth", [TT, 4, 4])
    g_sum = sb(moe, "g_sum", [TT, 4])
    g_ge = sb(moe, "g_ge", [TT, 4])
    g_rank = sb(moe, "g_rank", [TT, 4])
    w_sum = sb(moe, "w_sum", [TT])
    w_inv = sb(moe, "w_inv", [TT])
    position = sb(moe, "position", [TT, EXPERTS])
    info = sb(moe, "info", [TT, EXPERTS, 4])
    most = sb(moe, "most", [1])
    overflow = sb(moe, "overflow", [1], I32)
    onehot = sb(moe, "onehot", [TT, SLOTS])
    slot_token = sb(moe, "slot_token", [2], I32)
    slot_row = sb(moe, "slot_row", [2], I32)
    slot_gate = sb(moe, "slot_gate", [2])
    slot_none = sb(moe, "slot_none", [1])
    xg = sb(moe, "xg", [2, D])
    xgT_hi = sb(moe, "xgT_hi", [2, DC, SLOTS], F32R)
    xgT_lo = sb(moe, "xgT_lo", [2, DC, SLOTS], F32R)
    h_silu = sb(moe, "h_silu", [FF])
    h = sb(moe, "h", [FF])
    hT_hi = sb(moe, "hT_hi", [4, SLOTS], F32R)
    hT_lo = sb(moe, "hT_lo", [4, SLOTS], F32R)
    y = sb(moe, "y", [2, D])
    y_in = sb(moe, "y_in", [2, 2, D])

    psum = [ctx.enter_context(nc.psum_tensor(f"bank{b}", [P, 512], F32)) for b in range(8)]

    const_loaded = sem("const_loaded")
    rows_loaded = sem("rows_loaded")
    emb_loaded = sem("emb_loaded")
    x_loaded = [sem(f"x_loaded{t}") for t in range(TT)]
    early_loaded = sem("early_loaded")
    rpb_copied = sem("rpb_copied")
    bias_loaded = sem("bias_loaded")
    raw_loaded = [sem(f"raw_loaded{s}") for s in range(RAW)]
    hi_cast = sem("hi_cast")
    lo_cast = sem("lo_cast")
    unit_used = sem("unit_used")
    psum_full = [sem(f"psum_full{b}") for b in range(8)]
    psum_free = [sem(f"psum_free{b}") for b in range(8)]
    dve_step = sem("dve_step")
    pool_step = sem("pool_step")
    pool_go = sem("pool_go")
    halo_zero = sem("halo_zero")
    var_ready = sem("var_ready")
    rstd_ready = sem("rstd_ready")
    x0_ready = sem("x0_ready")
    x0_stored = sem("x0_stored")
    x0T_hi_done = sem("x0T_hi_done")
    pool_conv = sem("pool_conv")
    v_stored = sem("v_stored")
    v_windows = sem("v_windows")
    bias_ready = sem("bias_ready")
    max_ready = sem("max_ready")
    exp_done = sem("exp_done")
    probs_ready = sem("probs_ready")
    attn_hi = sem("attn_hi")
    vsg_gelu = sem("vsg_gelu")
    vs_ready = sem("vs_ready")
    gated = sem("gated")
    gated_hi = sem("gated_hi")
    gated_lo = sem("gated_lo")
    conv_ready = sem("conv_ready")
    centred = sem("centred")
    squared = sem("squared")
    conv_root = sem("conv_root")
    conv_scaled = sem("conv_scaled")
    conv_silu = sem("conv_silu")
    conv_hi = sem("conv_hi")
    conv_lo = sem("conv_lo")
    merged_ready = sem("merged_ready")
    merged_hi = sem("merged_hi")
    merged_lo = sem("merged_lo")
    x0_reloaded = sem("x0_reloaded")
    late_loaded = sem("late_loaded")
    x1_ready = sem("x1_ready")
    x1_stored = sem("x1_stored")
    selected = sem("selected")
    routed = sem("routed")
    flag_ready = sem("flag_ready")
    onehot_ready = sem("onehot_ready")
    token_ready = sem("token_ready")
    gathered = [sem(f"gathered{q}") for q in range(2)]
    xg_hi = sem("xg_hi")
    hT_hi_done = sem("hT_hi_done")
    y_stored = [sem(f"y_stored{q}") for q in range(2)]
    all_stored = sem("all_stored")
    y_loaded = [sem(f"y_loaded{q}") for q in range(2)]
    y_summed = sem("y_summed")
    final_step = sem("final_step")
    out_ready = sem("out_ready")
    out_stored = sem("out_stored")

    def nth(j, per=0, i=None):
        return j if i is None or not per else i * per + j

    def bank(name):
        return psum[banks.at[name][0]]

    def filled(name, i=None):
        b, _, full, unit, units, _, more = banks.at[name]
        if unit is None:
            return psum_full[b], nth(full + 1, more, i)
        return unit_used, nth(unit + 1, units, i)

    def empty(name, i=None):
        b, used, _, _, _, more, _ = banks.at[name]
        return psum_free[b], nth(used, more, i)

    def drained(name, i=None):
        b, used, _, _, _, more, _ = banks.at[name]
        return psum_free[b], nth(used + 1, more, i)

    def frees(name):
        return psum_free[banks.at[name][0]]

    def fills(name):
        return psum_full[banks.at[name][0]]

    def m_filled(b, n):
        return psum_full[b], n + (m_full[b] + 1)

    def m_empty(b, n):
        return psum_free[b], n + m_used[b]

    def m_drained(b, n):
        return psum_free[b], n + (m_used[b] + 1)

    def tokens_of(t):
        return slice(t * P, (t + 1) * P)

    def grid(row, seq, col, cols):
        return row[:, seq * SEQ:(seq + 1) * SEQ].rearrange("p (r c) -> p r c", c=GRID)[:, :, col:col + cols]

    def column(at):
        return vec[:, at:at + 1]

    def unit_of(tile, j, cols):
        return tile[:, j % SPLIT, :].rearrange("p (c n) -> p c n", n=cols)

    def attended_out(g, h2, rows):
        return bank(("attended", g))[rows, :].rearrange(
            "p (j q) -> p j q", j=4)[:, :, 64 * h2:64 * h2 + 64].rearrange("p j (r c) -> p j r c", r=ROWS)

    def attended_in(tile, g, rows):
        seq = g % 2
        return tile[rows, g // 2, seq * SEQ:(seq + 1) * SEQ].rearrange("p (r j c) -> p j r c", r=ROWS, j=4)

    w_in = A["w_in"][0].rearrange("(c p) n -> p c n", p=P)
    w_gate = A["w_gate"][0].rearrange("(c p) n -> p c n", p=P)
    w_branch = [A[n][0].rearrange("(c p) n -> p c n", p=P) for n in ("w_a_o", "w_b_o", "w_c_o")]
    w_o = A["w_o"][0].rearrange("(c p) n -> p c n", p=P)
    w_e1 = A["w_e1"][0].rearrange("e (c p) n -> p e c n", p=P)
    w_e3 = A["w_e3"][0].rearrange("e (c p) n -> p e c n", p=P)
    w_e2 = A["w_e2"][0].rearrange("e (c p) n -> p e c n", p=P)

    in_chunk = {}
    for c in range(WC):
        in_chunk |= {U_GLU + 2 * c: 20 + c, U_GLU + 2 * c + 1: 24 + c,
                     U_QK + 2 * c: c, U_QK + 2 * c + 1: 4 + c, U_USG + c: 12 + c}

    block = ctx.enter_context(nc.Block())

    @block.sync
    def _(sp):
        def load(j, source, n, per=0, i=None):
            if j >= RAW:
                sp.wait_ge(lo_cast, nth(j - RAW + 1, per, i))
            sp.dma_start(raw[:, j % RAW, :].rearrange("p (c n) -> p c n", n=n), source).then_inc(
                raw_loaded[j % RAW], 16)

        for t in range(TT):
            x = (A["x_prompt"], A["x_sample"])[t // 2][0]
            sp.dma_start(x_in[:, t, :], x[tokens_of(t % 2), :]).then_inc(x_loaded[t], 16)
        copy, heads, table_row = rpb_dram.shape[1], A["rpb"].shape[2] * A["rpb"].shape[3], A["rpb"].shape[3]

        def load_bias(h2, hp, qr):
            for pat, j in ((0, 0), (1, 1), (2, 3)):
                at = (2 * hp + h2) * heads + (7 - qr) * table_row + 15 + SHIFT[pat]
                source = bass.AP(tensor=rpb_dram.tensor, offset=rpb_dram.offset + at,
                                 ap=[[copy - 1, QCOLS], [table_row, ROWS], [1, KCOLS]])
                rows = slice(64 * h2 + QCOLS * qr, 64 * h2 + QCOLS * (qr + 1))
                sp.dma_start(bias[rows, hp, j, :].rearrange("p (r c) -> p r c", r=ROWS), source).then_inc(
                    bias_loaded, 16)

        for u in range(U_MERGE):
            if u == 6:
                sp.wait_ge(x0_stored, 16 * TT)
                sp.wait_ge(*drained("w_s"))
                sp.wait_ge(rpb_copied, 16)
            if 6 <= u < 14:
                for qr in range(ROWS):
                    load_bias((u - 6) % 2, (u - 6) // 2, qr)
            if u == 18:
                sp.wait_ge(v_stored, 16 * TT)
                for seq in range(2):
                    for j in range(4):
                        for r in range(ROWS):
                            at = seq * SEQ + r * GRID + WINDOW[j]
                            sp.dma_start(v_win[KCOLS * r:KCOLS * (r + 1), seq, j, :],
                                         v_dram[at:at + KCOLS, :]).then_inc(v_windows, 16)
            if u in in_chunk:
                f = in_chunk[u]
                load(u, w_in[:, :, f * P:(f + 1) * P], P)
            else:
                k, col = (u - U_V, 1024) if u < U_VSG else (u - U_VSG, 2048)
                load(u, w_in[:, 2 * k:2 * k + 2, col:col + W], W)
        with sp.Fori(0, 2) as i:
            for r in range(2):
                u = U_MERGE + 9 * r
                for d in range(2):
                    for n in range(3):
                        load(u, w_gate[:, :, bass.ds(i * 512 + (n * D + (2 * r + d) * P), P)], P, 18, i)
                        u += 1
                for n in range(3):
                    load(u, w_branch[n][:, :, bass.ds(i * 512 + 2 * r * P, 2 * P)], 2 * P, 18, i)
                    u += 1
        for n in range(2):
            for k in range(4):
                load(U_WO + 4 * n + k, w_o[:, 2 * k:2 * k + 2, n * 512:(n + 1) * 512], 512)

        def load_expert(kind, j, e, per=0, i=None):
            for k in range(4):
                if kind == 2:
                    source = w_e2[:, e, 2 * (k % 2):2 * (k % 2) + 2, (k // 2) * 512:(k // 2 + 1) * 512]
                else:
                    source = (w_e1 if kind == 1 else w_e3)[:, e, 2 * k:2 * k + 2, :]
                if i is not None:
                    source = source.rearrange("p e c n -> p (e c) n")
                load(j + k, source, 512, per, i)

        load_expert(1, U_MOE, 0)
        with sp.Fori(0, 7) as i:
            for q in range(2):
                j = U_MOE + 4 + 12 * q
                load_expert(3, j, bass.ds(i * 2 + q, 1), 24, i)
                load_expert(1, j + 4, bass.ds(i * 2 + (q + 1), 1), 24, i)
                load_expert(2, j + 8, bass.ds(i * 2 + q, 1), 24, i)
        j = U_MOE + 4 + 12 * 14
        load_expert(3, j, 14)
        load_expert(1, j + 4, 15)
        load_expert(2, j + 8, 14)
        load_expert(3, j + 12, 15)
        load_expert(2, j + 16, 15)

        sp.wait_ge(flag_ready, 1)
        with sp.register("over_sp") as reg:
            sp.reg_load(reg, overflow[0:1, 0:1])
            with sp.If(sp.snap(reg) > 0):
                with sp.Fori(0, EXPERTS) as e:
                    for b in range(3):
                        j = U_OVER + 12 * b
                        load_expert(1, j, bass.ds(e, 1), 36, e)
                        load_expert(3, j + 4, bass.ds(e, 1), 36, e)
                        load_expert(2, j + 8, bass.ds(e, 1), 36, e)
                sp.nop()
            with sp.Else():
                sp.nop()

        sp.wait_ge(all_stored, 1)
        for t in range(TT):
            if t >= 2:
                sp.wait_ge(y_summed, t - 1)
            for k in range(2):
                sp.dma_start(y_in[:, t % 2, k, :], y_dram[k * T + t * P:k * T + (t + 1) * P, :]).then_inc(
                    y_loaded[t % 2], 16)
        for t in range(TT):
            sp.wait_ge(out_ready, t + 1)
            o = (out_prompt, out_sample)[t // 2][0]
            sp.dma_start(o[tokens_of(t % 2), :], x1[:, t, :]).then_inc(out_stored, 16)
        sp.wait_ge(out_stored, 16 * TT)

    @block.scalar
    def _(act):
        act.dma_start(const[:], A["consts"]).then_inc(const_loaded, 16)
        act.dma_start(emb_g[:], A["emb_ln_g"].partition_broadcast(P)).then_inc(emb_loaded, 16)
        act.dma_start(emb_b[:], A["emb_ln_b"].partition_broadcast(P)).then_inc(emb_loaded, 16)
        for at, n, a in ((V_IN, 28, "b_in"), (V_GATE, 24, "b_gate"), (V_CONVB, 4, "conv_b"),
                         (V_CVG, 4, "cv_ln_g"), (V_CVB, 4, "cv_ln_b")):
            act.dma_start(rows_v[at:at + n, :], A[a][0].rearrange("(r c) -> r c", c=P)).then_inc(rows_loaded, 16)
        act.dma_start(rows_c[0:TAPS * WC, :], A["conv_w"][0].rearrange("t (c p) -> (t c) p", p=P)).then_inc(
            rows_loaded, 16)
        act.dma_start(w_s[:], A["w_s"][0].rearrange("g t s -> t g s")).then_inc(rows_loaded, 16)

        def cast_hi(j, per=0, i=None):
            act.wait_ge(raw_loaded[j % RAW], nth(16 * (j // RAW + 1), 16 * per // RAW, i))
            if j >= SPLIT:
                act.wait_ge(unit_used, nth(j - SPLIT + 1, per, i))
            act.copy(w_hi[:, j % SPLIT, :], raw[:, j % RAW, :]).then_inc(hi_cast, 1)

        cast_hi(0)
        cast_hi(1)
        for t in range(TT):
            for half in range(2):
                name = ("x0T", t, half)
                act.wait_ge(*filled(name))
                act.copy(xT_hi[:, 4 * half:4 * half + 4, tokens_of(t)],
                         bank(name)[:].rearrange("p (c n) -> p c n", c=4)).then_inc(x0T_hi_done, 1)
        act.wait_ge(*drained("vectors"))
        act.wait_ge(x0_stored, 16 * TT)

        def glu(c):
            if c:
                act.wait_ge(*drained(("glu_a", c - 1)))
            act.wait_ge(*filled(("glu_g", c)))
            act.activation(tmp[:, 0, :], bank(("glu_g", c))[:], ACT.Sigmoid,
                           bias=column(V_IN + 24 + c)).then_inc(frees(("glu_g", c)), 1)

        def keys(c):
            act.wait_ge(*filled(("k", c)))
            act.activation(kT[:, c, :], bank(("k", c))[:], ACT.Identity,
                           bias=column(V_IN + 4 + c)).then_inc(frees(("k", c)), 1)

        def queries(c):
            act.wait_ge(*filled(("q", c)))
            for s in range(2):
                tokens = slice(s * SEQ, (s + 1) * SEQ)
                o = act.activation(qT[:, c, tokens].rearrange("p (j r c) -> p r j c", j=4, r=ROWS),
                                   bank(("q", c))[:, tokens].rearrange("p (r j c) -> p r j c", j=4, r=ROWS),
                                   ACT.Identity, bias=column(V_IN + c))
            o.then_inc(frees(("q", c)), 1)

        def exp_rows(g):
            act.wait_ge(max_ready, g + 1)
            for j in range(4):
                key = probs[:, g % 2, j * P:(j + 1) * P]
                o = act.activation(key, key, ACT.Exp, bias=neg_max[:, g % 2, j:j + 1],
                                   accum_out=exp_sum[:, g % 2, j:j + 1])
            o.then_inc(exp_done, 1)

        def copy_probsT(g):
            act.wait_ge(*filled(("probsT", g)))
            if g:
                act.wait_ge(*filled(("attended", g - 1)))
            act.copy(probsT[:], bank(("probsT", g))[:]).then_inc(frees(("probsT", g)), 1)

        def split_attended(g):
            act.wait_ge(*filled(("attended", g)))
            for h2 in range(2):
                rows = slice(64 * h2, 64 * h2 + 64)
                o = act.copy(attended_in(branch_hi[0], g, rows), attended_out(g, h2, rows))
            o.then_inc(attn_hi, 1)

        for u in range(U_MERGE):
            cast_hi(u + 2)
            if u < U_V and u % 2:
                glu(u // 2)
            if U_QK <= u < U_USG:
                c = (u - U_QK) // 2
                keys(c) if u % 2 else queries(c)
            if 20 <= u < 28:
                split_attended(u - 20)
            if 19 <= u < 27:
                copy_probsT(u - 19)
            if 18 <= u < 26:
                exp_rows(u - 18)
            if u == U_VSG + 3:
                for t in range(TT):
                    act.wait_ge(*drained(("vsg", t)))
                    act.activation(vs[:, t, :], vs[:, t, :], ACT.Gelu_apprx_tanh).then_inc(vsg_gelu, 1)
            if u >= U_USG:
                c = u - U_USG
                if c >= 2:
                    act.wait_ge(gated_lo, c - 1)
                act.wait_ge(*filled(("usg", c)))
                act.activation(tmp[:, c % 2, :], bank(("usg", c))[:], ACT.Gelu_apprx_tanh,
                               bias=column(V_IN + 12 + c)).then_inc(frees(("usg", c)), 1)
                act.wait_ge(gated, c + 1)
                act.copy(branch_hi[1][:, c, :], tmp[:, c % 2, :]).then_inc(gated_hi, 1)

        for c in range(WC):
            act.wait_ge(centred, c + 1)
            act.activation(gate[:, c // 2, c % 2, :], conv[:, c, :], ACT.Square).then_inc(squared, 1)
        act.wait_ge(*drained("conv_var"))
        act.activation(part[:, 1, :], part[:, 0, :], ACT.Sqrt).then_inc(conv_root, 1)
        for c in range(WC):
            act.wait_ge(conv_scaled, c + 1)
            act.activation(conv[:, c, :], conv[:, c, :], ACT.Silu, bias=column(V_CVB + c),
                           scale=column(V_CVG + c)).then_inc(conv_silu, 1)
        for c in range(WC):
            act.wait_ge(conv_silu, c + 1)
            act.copy(branch_hi[2][:, c, :], conv[:, c, :]).then_inc(conv_hi, 1)

        with act.Fori(0, 2) as i:
            for r in range(2):
                u = U_MERGE + 9 * r
                for d in range(2):
                    for n in range(3):
                        cast_hi(u + 2, 18, i)
                        name = ("gate", r, d, n)
                        if r:
                            act.wait_ge(*drained(("branch", r - 1, d, n), i))
                        else:
                            act.wait_ge(*drained(("branch", 1, d, n), i - 1))
                        act.wait_ge(*filled(name, i))
                        act.activation(gate[:, d, n, :], bank(name)[:], ACT.Sigmoid,
                                       bias=vec[:, bass.ds(i * 4 + (V_GATE + n * DC + 2 * r + d), 1)]).then_inc(
                            frees(name), 1)
                        u += 1
                for n in range(3):
                    cast_hi(u + 2, 18, i)
                    u += 1
                for d in range(2):
                    act.wait_ge(merged_ready, i * 4 + (2 * r + d + 1))
                    act.copy(mT_hi[:, bass.ds(i * 4 + (2 * r + d), 1), :].rearrange("p o n -> p (o n)"),
                             merged[:, d, :]).then_inc(merged_hi, 1)
        for u in range(U_WO, U_MOE):
            cast_hi(u + 2)

        for t in range(TT):
            for half in range(2):
                name = ("x1T", t, half)
                act.wait_ge(*filled(name))
                act.copy(x1T[:, 4 * half:4 * half + 4, tokens_of(t)],
                         bank(name)[:].rearrange("p (c n) -> p c n", c=4)).then_inc(frees(name), 1)
        act.wait_ge(*filled("router"))
        act.activation(r_s[:].rearrange("p t g e -> p (t g e)"), bank("router")[:, 0:TT * EXPERTS],
                       ACT.Sigmoid).then_inc(frees("router"), 1)

        def split_xg(n, q):
            for half in range(2):
                act.wait_ge(*m_filled(M_XT + half, n))
                act.copy(xgT_hi[:, q, 4 * half:4 * half + 4, :],
                         psum[M_XT + half][:].rearrange("p (c n) -> p c n", c=4)).then_inc(xg_hi, 1)

        def silu(unit, n, h_before=None):
            act.wait_ge(unit_used, unit + 1)
            if h_before is not None:
                act.wait_ge(*m_drained(M_H3, h_before))
            act.activation(h_silu[:], psum[M_H1][:], ACT.Silu).then_inc(psum_free[M_H1], 1)

        def split_hT(n):
            act.wait_ge(*m_filled(M_HT, n))
            act.copy(hT_hi[:].rearrange("p c n -> p (c n)"), psum[M_HT][:]).then_inc(hT_hi_done, 1)

        def scale_y(unit, n, q, half):
            act.wait_ge(unit_used, unit + 1)
            act.wait_ge(*m_drained(M_INFO, n))
            act.activation(y[:, q, half * 512:(half + 1) * 512], psum[M_Y + half][:], ACT.Copy,
                           scale=slot_gate[:, q:q + 1]).then_inc(psum_free[M_Y + half], 1)

        def expert(n, q, j, per=0, i=None):
            for k in range(12):
                if j + k + 2 < U_OVER:
                    cast_hi(j + k + 2, per, i)
                if k == 1:
                    split_xg(n + 1, 1 - q)
                if k == 5:
                    split_hT(n)
                if k == 7:
                    silu(nth(j + 7, per, i), n + 1, n)
                if k == 9:
                    scale_y(nth(j + 9, per, i), n, q, 0)
                if k == 11:
                    scale_y(nth(j + 11, per, i), n, q, 1)

        split_xg(0, 0)
        for k in range(4):
            cast_hi(U_MOE + k + 2)
        silu(U_MOE + 3, 0)
        with act.Fori(0, 7) as i:
            for q in range(2):
                expert(i * 2 + q, q, U_MOE + 4 + 12 * q, 24, i)
        expert(14, 0, U_MOE + 4 + 12 * 14)
        j = U_MOE + 4 + 12 * 15
        for k in range(8):
            if j + k + 2 < U_OVER:
                cast_hi(j + k + 2)
            if k == 3:
                split_hT(15)
            if k == 5:
                scale_y(j + 5, 15, 1, 0)
            if k == 7:
                scale_y(j + 7, 15, 1, 1)

        act.wait_ge(flag_ready, 1)
        with act.register("over_act") as reg:
            act.reg_load(reg, overflow[0:1, 0:1])
            with act.If(act.snap(reg) > 0):
                with act.Fori(0, EXPERTS) as e:
                    for b in range(3):
                        n, j = e * 3 + (EXPERTS + b), U_OVER + 12 * b
                        split_xg(n, 0)
                        for k in range(4):
                            cast_hi(j + k, 36, e)
                        silu(nth(j + 3, 36, e), n)
                        for k in range(4, 8):
                            cast_hi(j + k, 36, e)
                        split_hT(n)
                        for k in range(8, 12):
                            cast_hi(j + k, 36, e)
                            if k % 2:
                                scale_y(nth(j + k, 36, e), n, 0, (k - 8) // 2)
                act.nop()
            with act.Else():
                act.nop()

    @block.vector
    def _(dve):
        steps = [0, 0, None]

        def step(k=1):
            steps[0] += k
            return steps[0] if steps[2] is None else steps[2] * steps[1] + steps[0]

        def cast_lo(j, per=0, i=None):
            dve.wait_ge(hi_cast, nth(j + 1, per, i))
            dve.tensor_tensor(w_lo[:, j % SPLIT, :], raw[:, j % RAW, :], w_hi[:, j % SPLIT, :].bitcast(F32),
                              ALU.subtract).then_inc(lo_cast, 1)

        def row_stats(x, t):
            halves = x.shape[-1] // 512
            for k in range(halves):
                dve.bn_stats(stats[:, t, k, :], x[:, k * 512:(k + 1) * 512]).then_inc(dve_step, 1)
            dve.wait_ge(dve_step, step(halves))
            dve.bn_aggr(mv[:, t, :], stats[:, t, 0:halves, :].rearrange("p k s -> p (k s)")).then_inc(dve_step, 1)
            dve.wait_ge(dve_step, step())
            return dve.tensor_scalar(var_eps[:, t:t + 1], mv[:, t, 1:2], EPS, None, ALU.add)

        def normalise(x, t, g, b):
            dve.tensor_scalar(x, x, mv[:, t, 0:1], rstd[:, t:t + 1], ALU.subtract, ALU.mult).then_inc(dve_step, 1)
            dve.wait_ge(dve_step, step())
            dve.tensor_tensor(x, x, g, ALU.mult).then_inc(dve_step, 1)
            dve.wait_ge(dve_step, step())
            return dve.tensor_tensor(x, x, b, ALU.add)

        for t in range(TT):
            dve.wait_ge(x_loaded[t], 16)
            row_stats(x_in[:, t, :], t).then_inc(var_ready, 1)
        dve.wait_ge(rstd_ready, 1)
        dve.wait_ge(emb_loaded, 32)
        for t in range(TT):
            normalise(x_in[:, t, :], t, emb_g[:], emb_b[:]).then_inc(x0_ready, 1)
        cast_lo(0)
        cast_lo(1)
        for t in range(TT):
            for half in range(2):
                name = ("x0T", t, half)
                dve.wait_ge(x0T_hi_done, 2 * t + half + 1)
                part_of = (slice(None), slice(4 * half, 4 * half + 4), tokens_of(t))
                dve.tensor_tensor(xT_lo[part_of], bank(name)[:].rearrange("p (c n) -> p c n", c=4),
                                  xT_hi[part_of].bitcast(F32), ALU.subtract).then_inc(frees(name), 1)
        dve.wait_ge(*filled("vectors"))
        dve.tensor_copy(conv_col[:].rearrange("p t c -> p (t c)"), bank("vectors")[:, V_ALL:V_ALL + TAPS * WC])
        dve.tensor_copy(vec[:], bank("vectors")[:, 0:V_ALL]).then_inc(frees("vectors"), 1)
        dve.wait_ge(*filled("w_s"))
        dve.wait_ge(x0_stored, 16 * TT)
        dve.tensor_copy(w_sT[:].rearrange("p g t -> p (g t)"), bank("w_s")[:]).then_inc(frees("w_s"), 1)
        dve.wait_ge(*drained("vectors"))

        taps = [(c, k) for c in range(WC - 1) for k in range(TAPS + 1)]
        last = {0: 0, 1: 0}

        def convolve(count):
            for _ in range(min(count, len(taps))):
                c, k = taps.pop(0)
                shifted = None if k == TAPS else conv_in[:, c, :, k:k + SEQ]
                even = conv[:, c, :].rearrange("p (s t) -> p s t", s=2)
                odd = conv_odd[:].rearrange("p (s t) -> p s t", s=2)
                if k == 0:
                    dve.wait_ge(*drained(("glu_a", c)))
                    o = dve.tensor_scalar(even, shifted, conv_col[:, k, c:c + 1], column(V_CONVB + c),
                                          ALU.mult, ALU.add)
                elif k == TAPS:
                    dve.wait_ge(dve_step, steps[0])
                    dve.tensor_tensor(even, even, odd, ALU.add).then_inc(conv_ready, 1)
                    continue
                elif k == 1:
                    if c:
                        dve.wait_ge(conv_ready, c)
                    o = dve.tensor_scalar(odd, shifted, conv_col[:, k, c:c + 1], None, ALU.mult)
                else:
                    dve.wait_ge(dve_step, last[k % 2])
                    sum_ = odd if k % 2 else even
                    o = dve.scalar_tensor_tensor(out=sum_, in0=shifted, scalar=conv_col[:, k, c:c + 1], in1=sum_,
                                                 op0=ALU.mult, op1=ALU.add)
                o.then_inc(dve_step, 1)
                last[k % 2] = step()

        def glu(c):
            dve.wait_ge(*filled(("glu_a", c)))
            dve.wait_ge(*drained(("glu_g", c)))
            if c == 0:
                dve.wait_ge(halo_zero, 1)
            dve.scalar_tensor_tensor(
                out=conv_in[:, c, :, HALO:HALO + SEQ], in0=bank(("glu_a", c))[:].rearrange("p (s t) -> p s t", s=2),
                scalar=column(V_IN + 20 + c), in1=tmp[:, 0, :].rearrange("p (s t) -> p s t", s=2),
                op0=ALU.add, op1=ALU.mult).then_inc(frees(("glu_a", c)), 1)

        def mask_scores(g):
            dve.wait_ge(*filled(("scores", g)))
            if g == 0:
                dve.wait_ge(bias_ready, 4)
            if g >= 2:
                dve.wait_ge(*filled(("probsT", g - 2)))
            row = probs[:, g % 2, :]
            dve.scalar_tensor_tensor(out=row, in0=bank(("scores", g))[:], scalar=QSCALE,
                                     in1=bias[:, g // 2, :, :].rearrange("p j k -> p (j k)"),
                                     op0=ALU.mult, op1=ALU.add).then_inc(frees(("scores", g)), 1)
            dve.wait_ge(*drained(("scores", g)))
            dve.tensor_reduce(neg_max[:, g % 2, :], row.rearrange("p (j k) -> p j k", j=4), AX.X,
                              ALU.max).then_inc(dve_step, 1)
            dve.wait_ge(dve_step, step())
            dve.tensor_scalar(neg_max[:, g % 2, :], neg_max[:, g % 2, :], -1.0, None, ALU.mult).then_inc(max_ready, 1)

        def divide_probs(g):
            dve.wait_ge(exp_done, g + 1)
            dve.reciprocal(exp_inv[:, g % 2, :], exp_sum[:, g % 2, :]).then_inc(dve_step, 1)
            dve.wait_ge(dve_step, step())
            row = probs[:, g % 2, :].rearrange("p (j k) -> p j k", j=4)
            dve.tensor_tensor(row, row, exp_inv[:, g % 2, :].unsqueeze(2).to_broadcast([P, 4, P]),
                              ALU.mult).then_inc(probs_ready, 1)

        def split_attended(g):
            dve.wait_ge(attn_hi, g + 1)
            for h2 in range(2):
                rows = slice(64 * h2, 64 * h2 + 64)
                o = dve.tensor_tensor(attended_in(branch_lo[0], g, rows), attended_out(g, h2, rows),
                                      attended_in(branch_hi[0], g, rows).bitcast(F32), ALU.subtract)
            o.then_inc(frees(("attended", g)), 1)

        for u in range(U_MERGE):
            cast_lo(u + 2)
            if u < U_V and u % 2:
                glu(u // 2)
            if 19 <= u < 27:
                divide_probs(u - 19)
            if 18 <= u < 26:
                mask_scores(u - 18)
            if u == U_V + 3:
                dve.wait_ge(early_loaded, 16 * 5)
                for t in range(TT):
                    dve.wait_ge(*filled(("v", t)))
                    dve.tensor_tensor(vs[:, t, :], bank(("v", t))[:], bv[:],
                                      ALU.add).then_inc(frees(("v", t)), 1)
            if u == U_VSG + 3:
                dve.wait_ge(v_stored, 16 * TT)
                for t in range(TT):
                    dve.wait_ge(*filled(("vsg", t)))
                    dve.tensor_tensor(vs[:, t, :], bank(("vsg", t))[:], bvs[:], ALU.add).then_inc(
                        frees(("vsg", t)), 1)
            if U_VSG + 4 <= u < U_VSG + 8:
                t = u - U_VSG - 4
                dve.wait_ge(vsg_gelu, t + 1)
                row_stats(vs[:, t, :], t).then_inc(var_ready, 1)
            if U_VSG + 8 <= u < U_VSG + 12:
                dve.wait_ge(rstd_ready, 2)
                normalise(vs[:, u - U_VSG - 8, :], u - U_VSG - 8, sg_g[:], sg_b[:]).then_inc(vs_ready, 1)
            if u >= U_USG:
                c = u - U_USG
                dve.wait_ge(*filled(("spatial", c)))
                if c:
                    dve.wait_ge(gated, c)
                dve.tensor_tensor(bv[:].rearrange("p (t n) -> p t n", t=TT),
                                  bank(("spatial", c))[:].rearrange("p (t n) -> p t n", t=TT),
                                  b_s[:, c, :].unsqueeze(1).to_broadcast([P, TT, P]), ALU.add).then_inc(
                    frees(("spatial", c)), 1)
                dve.wait_ge(*drained(("spatial", c)))
                dve.wait_ge(*drained(("usg", c)))
                dve.tensor_tensor(tmp[:, c % 2, :], bv[:], tmp[:, c % 2, :], ALU.mult).then_inc(gated, 1)
                dve.wait_ge(gated_hi, c + 1)
                dve.tensor_tensor(branch_lo[1][:, c, :], tmp[:, c % 2, :], branch_hi[1][:, c, :].bitcast(F32),
                                  ALU.subtract).then_inc(gated_lo, 1)
            if 20 <= u < 28:
                split_attended(u - 20)
            convolve(0 if u < 1 else 5 if u < 8 else 3)
        convolve(len(taps))

        dve.wait_ge(*filled("conv_mean"))
        for c in range(WC):
            dve.scalar_tensor_tensor(out=conv[:, c, :], in0=bank("conv_mean")[:], scalar=-1.0 / W, in1=conv[:, c, :],
                                     op0=ALU.mult, op1=ALU.add).then_inc(centred, 1)
        dve.wait_ge(centred, WC)
        dve.sem_inc(frees("conv_mean"), 1)
        dve.wait_ge(*filled("conv_var"))
        dve.tensor_scalar(part[:, 0, :], bank("conv_var")[:], 1.0 / W, EPS, ALU.mult, ALU.add).then_inc(
            frees("conv_var"), 1)
        dve.wait_ge(conv_root, 1)
        dve.reciprocal(part[:, 1, :], part[:, 1, :]).then_inc(dve_step, 1)
        dve.wait_ge(dve_step, step())
        root, square = part[:, 1, :], merged[:, 0, :]
        dve.scalar_tensor_tensor(out=square, in0=root, scalar=-0.5, in1=root, op0=ALU.mult, op1=ALU.mult).then_inc(
            dve_step, 1)
        dve.wait_ge(dve_step, step())
        dve.tensor_tensor(square, square, part[:, 0, :], ALU.mult).then_inc(dve_step, 1)
        dve.wait_ge(dve_step, step())
        dve.scalar_tensor_tensor(out=root, in0=square, scalar=1.5, in1=root, op0=ALU.add, op1=ALU.mult).then_inc(
            dve_step, 1)
        dve.wait_ge(dve_step, step())
        for c in range(WC):
            dve.tensor_tensor(conv[:, c, :], conv[:, c, :], part[:, 1, :], ALU.mult).then_inc(conv_scaled, 1)
        for c in range(WC):
            dve.wait_ge(conv_hi, c + 1)
            dve.tensor_tensor(branch_lo[2][:, c, :], conv[:, c, :], branch_hi[2][:, c, :].bitcast(F32),
                              ALU.subtract).then_inc(conv_lo, 1)

        with dve.Fori(0, 2) as i:
            base = steps[0]
            steps[1:] = 4, i
            for r in range(2):
                u = U_MERGE + 9 * r
                for k in range(9):
                    cast_lo(u + k + 2, 18, i)
                    if k < 6:
                        continue
                    n = k - 6
                    if n == 2:
                        dve.wait_ge(dve_step, step(0))
                    for d in range(2):
                        name = ("branch", r, d, n)
                        dve.wait_ge(*filled(name, i))
                        dve.wait_ge(*drained(("gate", r, d, n), i))
                        out = merged[:, d, :] if n == 0 else part[:, d, :]
                        dve.tensor_tensor(out, gate[:, d, n, :], bank(name)[:], ALU.mult).then_inc(frees(name), 1)
                    for d in range(2):
                        dve.wait_ge(*drained(("branch", r, d, n), i))
                        if n == 1:
                            dve.tensor_tensor(merged[:, d, :], merged[:, d, :], part[:, d, :], ALU.add).then_inc(
                                dve_step, 1)
                            step()
                        if n == 2:
                            dve.tensor_tensor(merged[:, d, :], merged[:, d, :], part[:, d, :], ALU.add).then_inc(
                                merged_ready, 1)
                for d in range(2):
                    dve.wait_ge(merged_hi, i * 4 + (2 * r + d + 1))
                    chunk = bass.ds(i * 4 + (2 * r + d), 1)
                    dve.tensor_tensor(mT_lo[:, chunk, :].rearrange("p o n -> p (o n)"), merged[:, d, :],
                                      mT_hi[:, chunk, :].rearrange("p o n -> p (o n)").bitcast(F32),
                                      ALU.subtract).then_inc(merged_lo, 1)
            assert steps[0] - base == 4
        steps[:] = base + 8, 0, None

        for u in range(U_WO, U_MOE):
            cast_lo(u + 2)
            if u == U_WO + 2:
                dve.wait_ge(x0_reloaded, 16 * TT)
                dve.wait_ge(late_loaded, 16 * 7)
                for t in range(TT):
                    dve.scalar_tensor_tensor(out=x1[:, t, :], in0=x1[:, t, :], scalar=ALPHA, in1=b_o[:],
                                             op0=ALU.mult, op1=ALU.add).then_inc(dve_step, 1)
                step(TT)
            if u in (U_WO + 3, U_MOE - 1):
                n = (u - U_WO) // 4
                dve.wait_ge(dve_step, step(0))
                for t in range(TT):
                    name = ("mixed", n, t)
                    dve.wait_ge(*filled(name))
                    half = x1[:, t, n * 512:(n + 1) * 512]
                    dve.tensor_tensor(half, half, bank(name)[:], ALU.add).then_inc(frees(name), 1)
        for t in range(TT):
            dve.wait_ge(*drained(("mixed", 1, t)))
            row_stats(x1[:, t, :], t).then_inc(var_ready, 1)
        dve.wait_ge(rstd_ready, 3)
        for t in range(TT):
            normalise(x1[:, t, :], t, ln1_g[:], ln1_b[:]).then_inc(x1_ready, 1)

        def tt(out, a, b, op):
            dve.tensor_tensor(out, a, b, op).then_inc(dve_step, 1)
            dve.wait_ge(dve_step, step())

        def ranks(rank, ge, value):
            for d in range(1, 4):
                k = 4 - d
                tt(ge[..., 0:k], value[..., 0:k], value[..., d:4], ALU.is_ge)
                tt(rank[..., d:4], rank[..., d:4], ge[..., 0:k], ALU.add)
                tt(rank[..., 0:k], rank[..., 0:k], ge[..., 0:k], ALU.subtract)

        def per_tile(row16):
            return row16.rearrange("p (g e) -> p g e", g=4).unsqueeze(1).to_broadcast([P, TT, 4, 4])

        dve.wait_ge(*drained("router"))
        tt(r_sb[:], r_s[:], per_tile(b_router[:]), ALU.add)
        dve.tensor_copy(r_rank[:], per_tile(const[:, C_HIGHER:C_HIGHER + EXPERTS])).then_inc(dve_step, 1)
        dve.tensor_copy(g_rank[:], const[:, C_HIGHER:C_HIGHER + 4].unsqueeze(1).to_broadcast([P, TT, 4])).then_inc(
            dve_step, 1)
        dve.wait_ge(dve_step, step(2))
        ranks(r_rank[:], r_ge[:], r_sb[:])
        dve.tensor_scalar(r_sel[:], r_rank[:], 2.0, None, ALU.is_lt).then_inc(dve_step, 1)
        dve.wait_ge(dve_step, step())
        tt(r_tmp[:], r_sb[:], r_sel[:], ALU.mult)
        dve.tensor_reduce(g_sum[:], r_tmp[:], AX.X, ALU.add).then_inc(dve_step, 1)
        dve.wait_ge(dve_step, step())
        ranks(g_rank[:], g_ge[:], g_sum[:])
        dve.tensor_scalar(g_rank[:], g_rank[:], 1.0, None, ALU.is_lt).then_inc(dve_step, 1)
        dve.wait_ge(dve_step, step())
        dve.tensor_tensor(r_sel[:], r_sel[:], g_rank[:].unsqueeze(3).to_broadcast([P, TT, 4, 4]),
                          ALU.mult).then_inc(selected, 1)
        dve.wait_ge(selected, 1)
        tt(r_tmp[:], r_s[:], r_sel[:], ALU.mult)
        dve.tensor_reduce(w_sum[:], r_tmp[:].rearrange("p t g e -> p t (g e)"), AX.X, ALU.add).then_inc(dve_step, 1)
        dve.wait_ge(dve_step, step())
        dve.reciprocal(w_inv[:], w_sum[:]).then_inc(dve_step, 1)
        dve.memset(r_kth[..., 0:1], 0.0).then_inc(dve_step, 1)
        dve.tensor_copy(r_kth[..., 1:2], r_sel[..., 0:1]).then_inc(dve_step, 1)
        dve.wait_ge(dve_step, step(3))
        tt(r_kth[..., 2:3], r_kth[..., 1:2], r_sel[..., 1:2], ALU.add)
        tt(r_kth[..., 3:4], r_kth[..., 2:3], r_sel[..., 2:3], ALU.add)
        by_expert = [TT, EXPERTS]
        flat_kth = r_kth[:].rearrange("p t g e -> p t (g e)")
        tokens = token.unsqueeze(2).to_broadcast([P] + by_expert)
        dve.tensor_copy(info[..., 0], tokens).then_inc(dve_step, 1)
        dve.tensor_tensor(info[..., 2], r_tmp[:].rearrange("p t g e -> p t (g e)"),
                          w_inv[:].unsqueeze(2).to_broadcast([P] + by_expert), ALU.mult).then_inc(dve_step, 1)
        dve.memset(info[..., 3], 0.0).then_inc(dve_step, 1)
        dve.tensor_scalar(info[..., 1], flat_kth, float(T), 1.0, ALU.mult, ALU.add).then_inc(dve_step, 1)
        dve.wait_ge(dve_step, step(4))
        tt(info[..., 1], info[..., 1], tokens, ALU.add)
        dve.wait_ge(*filled("position"))
        flat_sel = r_sel[:].rearrange("p t g e -> p t (g e)")
        dve.tensor_reduce(most[:], bank("position")[:, 64:80], AX.X, ALU.max).then_inc(dve_step, 1)
        dve.scalar_tensor_tensor(out=position[:], in0=bank("position")[:, 0:64].rearrange("p (t e) -> p t e", t=TT),
                                 scalar=1.0, in1=flat_sel, op0=ALU.add, op1=ALU.mult).then_inc(frees("position"), 1)
        dve.wait_ge(dve_step, step())
        dve.wait_ge(*drained("position"))
        dve.tensor_scalar(overflow[:], most[:], float(SLOTS), None, ALU.is_gt).then_inc(flag_ready, 1)
        dve.tensor_scalar(position[:], position[:], -1.0, None, ALU.add).then_inc(routed, 1)
        dve.wait_ge(routed, 1)

        def make_onehot(e, b=0):
            slot = position[:, :, e if isinstance(e, int) else bass.ds(e, 1)]
            slot = slot.unsqueeze(2) if isinstance(e, int) else slot
            dve.scalar_tensor_tensor(out=onehot[:], in0=slot.to_broadcast([P, TT, SLOTS]), scalar=float(b * SLOTS),
                                     in1=iota.unsqueeze(1).to_broadcast([P, TT, SLOTS]),
                                     op0=ALU.subtract, op1=ALU.is_equal).then_inc(onehot_ready, 1)

        def slot_tokens(n, q, gathers):
            dve.wait_ge(*m_filled(M_INFO, n))
            if gathers is not None:
                dve.wait_ge(gathered[q], gathers * 16)
            dve.tensor_copy(slot_token[:, q:q + 1], psum[M_INFO][:, 0:1]).then_inc(token_ready, 1)

        def slot_rows(n, q, scatters):
            dve.wait_ge(*m_filled(M_INFO, n))
            if scatters is not None:
                dve.wait_ge(y_stored[q], scatters * 16)
            dve.tensor_scalar(slot_none[:], psum[M_INFO][:, 1:2], 0.0, 65536.0, ALU.is_equal, ALU.mult).then_inc(
                dve_step, 1)
            dve.wait_ge(dve_step, step())
            dve.scalar_tensor_tensor(out=slot_row[:, q:q + 1], in0=slot_none[:], scalar=-1.0,
                                     in1=psum[M_INFO][:, 1:2], op0=ALU.add, op1=ALU.add)
            dve.tensor_copy(slot_gate[:, q:q + 1], psum[M_INFO][:, 2:3]).then_inc(psum_free[M_INFO], 1)

        def split_xg(n, q):
            for half in range(2):
                dve.wait_ge(xg_hi, n * 2 + (half + 1))
                part_of = (slice(None), q, slice(4 * half, 4 * half + 4))
                dve.tensor_tensor(xgT_lo[part_of], psum[M_XT + half][:].rearrange("p (c n) -> p c n", c=4),
                                  xgT_hi[part_of].bitcast(F32), ALU.subtract).then_inc(psum_free[M_XT + half], 1)

        def gate_h(unit, n):
            dve.wait_ge(unit_used, unit + 1)
            dve.wait_ge(*m_drained(M_H1, n))
            dve.tensor_tensor(h[:], h_silu[:], psum[M_H3][:], ALU.mult).then_inc(psum_free[M_H3], 1)

        def split_hT(n):
            dve.wait_ge(hT_hi_done, n + 1)
            dve.tensor_tensor(hT_lo[:].rearrange("p c n -> p (c n)"), psum[M_HT][:],
                              hT_hi[:].rearrange("p c n -> p (c n)").bitcast(F32),
                              ALU.subtract).then_inc(psum_free[M_HT], 1)

        make_onehot(0)
        slot_tokens(0, 0, None)
        make_onehot(1)
        slot_rows(0, 0, None)
        slot_tokens(1, 1, None)
        split_xg(0, 0)
        for k in range(4):
            cast_lo(U_MOE + k + 2)

        def pair(j, per=0, i=None):
            for q in range(2):
                n = nth(q, 2, i)
                for k in range(12):
                    cast_lo(j + 12 * q + k + 2, per, i)
                    if k == 1:
                        split_xg(n + 1, 1 - q)
                    if k == 3:
                        gate_h(nth(j + 12 * q + 3, per, i), n)
                    if k == 4:
                        slot_rows(n + 1, 1 - q, q or None if i is None else i + q)
                    if k == 5:
                        split_hT(n)
                    if k == 7:
                        make_onehot(n + 2)
                    if k == 9:
                        slot_tokens(n + 2, q, nth(1, 1, i))

        pair(U_MOE + 4)
        with dve.Fori(0, 6) as i:
            base = steps[0]
            steps[1:] = 2, i
            pair(U_MOE + 4, 24, i + 1)
            assert steps[0] - base == 2
        steps[:] = base + 12, 0, None
        for n in (14, 15):
            j = U_MOE + 4 + 12 * n
            for k in range(12 if n == 14 else 8):
                if j + k + 2 < U_OVER:
                    cast_lo(j + k + 2)
                if k == 1 and n == 14:
                    split_xg(15, 1)
                if k == 3:
                    gate_h(j + 3, n)
                if k == 4 and n == 14:
                    slot_rows(15, 1, 7)
                if k == (5 if n == 14 else 3):
                    split_hT(n)

        with dve.register("over_dve") as reg:
            dve.reg_load(reg, overflow[0:1, 0:1])
            with dve.If(dve.snap(reg) > 0):
                with dve.Fori(0, EXPERTS) as e:
                    base = steps[0]
                    steps[1:] = 3, e
                    for b in range(3):
                        n, j = e * 3 + (EXPERTS + b), U_OVER + 12 * b
                        make_onehot(e, b + 1)
                        slot_tokens(n, 0, e * 3 + (EXPERTS // 2 + b))
                        slot_rows(n, 0, e * 3 + (EXPERTS // 2 + b))
                        split_xg(n, 0)
                        for k in range(8):
                            cast_lo(j + k, 36, e)
                        gate_h(nth(j + 7, 36, e), n)
                        split_hT(n)
                        for k in range(8, 12):
                            cast_lo(j + k, 36, e)
                    assert steps[0] - base == 3
                dve.nop()
            with dve.Else():
                dve.nop()

        for t in range(TT):
            row = x1[:, t, :]
            dve.wait_ge(y_loaded[t % 2], 32 * (t // 2 + 1))
            dve.scalar_tensor_tensor(out=row, in0=row, scalar=ALPHA, in1=y_in[:, t % 2, 0, :], op0=ALU.mult,
                                     op1=ALU.add).then_inc(final_step, 1)
            dve.wait_ge(final_step, 6 * t + 1)
            dve.tensor_tensor(row, row, y_in[:, t % 2, 1, :], ALU.add).then_inc(y_summed, 1)
            dve.wait_ge(y_summed, t + 1)
            for k in range(2):
                dve.bn_stats(stats[:, t, k, :], row[:, k * 512:(k + 1) * 512]).then_inc(final_step, 1)
            dve.wait_ge(final_step, 6 * t + 3)
            dve.bn_aggr(mv[:, t, :], stats[:, t, :, :].rearrange("p k s -> p (k s)")).then_inc(final_step, 1)
            dve.wait_ge(final_step, 6 * t + 4)
            dve.tensor_scalar(var_eps[:, t:t + 1], mv[:, t, 1:2], EPS, None, ALU.add).then_inc(var_ready, 1)
            dve.wait_ge(rstd_ready, 4 + t)
            dve.tensor_scalar(row, row, mv[:, t, 0:1], rstd[:, t:t + 1], ALU.subtract, ALU.mult).then_inc(
                final_step, 1)
            dve.wait_ge(final_step, 6 * t + 5)
            dve.tensor_tensor(row, row, ln2_g[:], ALU.mult).then_inc(final_step, 1)
            dve.wait_ge(final_step, 6 * t + 6)
            dve.tensor_tensor(row, row, ln2_b[:], ALU.add).then_inc(out_ready, 1)

    @block.gpsimd
    def _(pool):
        pool.dma_start(rpb_dram, A["rpb"][0].rearrange("h r c -> (h r c)").partition_broadcast(QCOLS)).then_inc(
            rpb_copied, 16)
        pool.memset(minus_half[:], -0.5).then_inc(pool_step, 1)
        pool.memset(conv_in[:], 0.0).then_inc(halo_zero, 1)
        pool.wait_ge(pool_step, 1)

        def power(tiles, waits):
            pool.wait_ge(var_ready, waits)
            pool.tensor_tensor(rstd[:, tiles], var_eps[:, tiles], minus_half[:, tiles], ALU.pow).then_inc(
                rstd_ready, 1)

        power(slice(0, TT), TT)
        for t in range(TT):
            pool.wait_ge(x0_ready, t + 1)
            pool.dma_start(x0_dram[tokens_of(t), :], x_in[:, t, :]).then_inc(x0_stored, 16)
        pool.wait_ge(x0_stored, 16 * TT)
        for t in range(TT):
            for half in range(2):
                pool.wait_ge(*filled(("x0T", t, half)))
        pool.wait_ge(*filled("w_s"))
        b_in = A["b_in"][0]
        pool.dma_start(bv[:], b_in[2 * W:3 * W].partition_broadcast(P)).then_inc(early_loaded, 16)
        pool.dma_start(bvs[:], b_in[4 * W:5 * W].partition_broadcast(P)).then_inc(early_loaded, 16)
        pool.dma_start(sg_g[:], A["sg_ln_g"][0].partition_broadcast(P)).then_inc(early_loaded, 16)
        pool.dma_start(sg_b[:], A["sg_ln_b"][0].partition_broadcast(P)).then_inc(early_loaded, 16)
        pool.dma_start(b_s[:].rearrange("p g t -> p (g t)"),
                       A["b_s"][0].rearrange("g t -> (g t)").partition_broadcast(P)).then_inc(early_loaded, 16)
        for t in range(TT):
            pool.wait_ge(*drained(("v", t)))
            pool.dma_start(v_dram[tokens_of(t), :], vs[:, t, :]).then_inc(v_stored, 16)
        pool.wait_ge(bias_loaded, 16 * 12 * 8)
        for n, j in enumerate((0, 2, 1, 3)):
            mask = const[:, C_MASK + KCOLS * PATTERN[j]:C_MASK + KCOLS * (PATTERN[j] + 1)]
            for hp in range(WC):
                o = pool.tensor_tensor(bias[:, hp, j, :].rearrange("p (r c) -> p r c", r=ROWS),
                                       bias[:, hp, 1 if j == 2 else j, :].rearrange("p (r c) -> p r c", r=ROWS),
                                       mask.unsqueeze(1).to_broadcast([P, ROWS, KCOLS]), ALU.add)
            o.then_inc(bias_ready, 1)
            if j == 2:
                pool.wait_ge(bias_ready, n + 1)

        c = WC - 1
        out = conv[:, c, :].rearrange("p (s t) -> p s t", s=2)

        def convolve(taps):
            for k in taps:
                shifted = conv_in[:, c, :, k:k + SEQ]
                if k:
                    pool.wait_ge(pool_conv, k)
                    pool.tensor_scalar(tap[:].rearrange("p (s t) -> p s t", s=2), shifted, conv_col[:, k, c:c + 1],
                                       None, ALU.mult).then_inc(pool_step, 1)
                    pool.wait_ge(pool_step, k + 1)
                    pool.tensor_tensor(conv[:, c, :], conv[:, c, :], tap[:], ALU.add).then_inc(pool_conv, 1)
                else:
                    pool.tensor_scalar(out, shifted, conv_col[:, k, c:c + 1], column(V_CONVB + c),
                                       ALU.mult, ALU.add).then_inc(pool_conv, 1)

        pool.wait_ge(*drained(("glu_a", c)))
        pool.wait_ge(*drained("vectors"))
        convolve(range(10))
        power(slice(0, TT), 2 * TT)
        convolve(range(10, TAPS))

        pool.wait_ge(unit_used, U_WO)
        for t in range(TT):
            pool.dma_start(x1[:, t, :], x0_dram[tokens_of(t), :]).then_inc(x0_reloaded, 16)
        for dst, a in ((b_o, A["b_o"][0]), (ln1_g, A["ln1_g"][0]), (ln1_b, A["ln1_b"][0]), (ln2_g, A["ln2_g"][0]),
                       (ln2_b, A["ln2_b"][0]), (b_router, A["b_router"])):
            pool.dma_start(dst[:], a.partition_broadcast(P)).then_inc(late_loaded, 16)
        pool.dma_start(w_router[:], A["w_router"].rearrange("(c p) e -> p c e", p=P)).then_inc(late_loaded, 16)
        power(slice(0, TT), 3 * TT)
        for t in range(TT):
            pool.wait_ge(x1_ready, t + 1)
            pool.dma_start(x1_dram[tokens_of(t), :], x1[:, t, :]).then_inc(x1_stored, 16)
        pool.wait_ge(x1_stored, 16 * TT)

        def gather(n, q):
            pool.wait_ge(token_ready, n + 1)
            pool.sem_inc(pool_go, 1)
            pool.indirect_dma_start(out=xg[:, q, :], out_offset=None, in_=x1_dram,
                                    in_offset=bass.IndirectOffsetOnAxis(ap=slot_token[:, q:q + 1], axis=0)).then_inc(
                gathered[q], 16)

        def scatter(n, q):
            for half in range(2):
                pool.wait_ge(*m_drained(M_Y + half, n))
                pool.sem_inc(pool_go, 1)
            pool.wait_ge(*m_drained(M_INFO, n))
            pool.sem_inc(pool_go, 1)
            pool.indirect_dma_start(out=y_dram, out_offset=bass.IndirectOffsetOnAxis(ap=slot_row[:, q:q + 1], axis=0),
                                    in_=y[:, q, :], in_offset=None, bounds_check=2 * T - 1,
                                    oob_is_err=False).then_inc(y_stored[q], 16)

        gather(0, 0)
        gather(1, 1)
        with pool.Fori(0, 7) as i:
            for q in range(2):
                pool.wait_ge(*m_filled(M_XT + 1, i * 2 + q))
                pool.sem_inc(pool_go, 1)
                gather(i * 2 + (q + 2), q)
                scatter(i * 2 + q, q)
        scatter(14, 0)
        scatter(15, 1)
        pool.wait_ge(flag_ready, 1)
        with pool.register("over_pool") as reg:
            pool.reg_load(reg, overflow[0:1, 0:1])
            with pool.If(pool.snap(reg) > 0):
                with pool.Fori(0, EXPERTS) as e:
                    for b in range(3):
                        n = e * 3 + (EXPERTS + b)
                        gather(n, 0)
                        scatter(n, 0)
                pool.wait_ge(y_stored[0], 16 * (EXPERTS // 2 + 3 * EXPERTS))
            with pool.Else():
                pool.wait_ge(y_stored[0], 16 * EXPERTS // 2)
        pool.wait_ge(y_stored[1], 16 * EXPERTS // 2)
        pool.sem_inc(all_stored, 1)
        for t in range(TT):
            power(slice(t, t + 1), 3 * TT + t + 1)

    @block.tensor
    def _(pe):
        def open_bank(name, i=None):
            if banks.at[name][1]:
                pe.wait_ge(*empty(name, i))

        def turn(name, tile, n=4):
            open_bank(name)
            for k in range(n):
                o = pe.transpose(bank(name)[:, k * P:(k + 1) * P], tile(k), ident)
            o.then_inc(fills(name), 1)

        def three(out, hi_l, lo_l, hi_r, lo_r, start, stop):
            pe.matmul(out, hi_l, hi_r, start=start, stop=False)
            pe.matmul(out, hi_l, lo_r, start=False, stop=False)
            return pe.matmul(out, lo_l, hi_r, start=False, stop=stop)

        def features(j, outs, x_hi, x_lo, per=0, i=None):
            pe.wait_ge(lo_cast, nth(j + 1, per, i))
            hi, lo = unit_of(w_hi, j, len(outs) * P), unit_of(w_lo, j, len(outs) * P)
            chunks = UNIT // (len(outs) * P)
            for d, name in enumerate(outs):
                open_bank(name, i)
                cols = slice(d * P, (d + 1) * P)
                for c in range(chunks):
                    o = three(bank(name)[:], hi[:, c, cols], lo[:, c, cols], x_hi[:, c, :], x_lo[:, c, :],
                              c == 0, c == chunks - 1)
            o.then_inc(unit_used, 1)

        def tokens(j, k, last, outs, x_hi, x_lo, choose, per=0, i=None):
            pe.wait_ge(lo_cast, nth(j + 1, per, i))
            hi, lo = unit_of(w_hi, j, 512), unit_of(w_lo, j, 512)
            for t, out in enumerate(outs):
                for c in range(2):
                    o = three(out, choose(x_hi[:, 2 * k + c, :], t), choose(x_lo[:, 2 * k + c, :], t), hi[:, c, :],
                              lo[:, c, :], k == 0 and c == 0, last and c == 1)
            o.then_inc(unit_used, 1)

        def scores(g):
            hp, seq = g // 2, g % 2
            open_bank(("scores", g))
            pe.wait_ge(*drained(("q", hp)))
            pe.wait_ge(*drained(("k", hp)))
            for h2 in range(2):
                rows = slice(64 * h2, 64 * h2 + 64)
                for j in range(4):
                    o = pe.matmul(bank(("scores", g))[rows, j * P:(j + 1) * P],
                                  qT[rows, hp, seq * SEQ + 64 * j:seq * SEQ + 64 * (j + 1)],
                                  grid(kT[rows, hp, :], seq, WINDOW[j], KCOLS), start=True, stop=True)
            o.then_inc(fills(("scores", g)), 1)

        def attend(g):
            hp, seq = g // 2, g % 2
            open_bank(("attended", g))
            pe.wait_ge(*drained(("probsT", g)))
            for j in range(4):
                o = pe.matmul(bank(("attended", g))[:, j * P:(j + 1) * P], v_win[:, seq, j, hp * P:(hp + 1) * P],
                              probsT[:, j * P:(j + 1) * P], start=True, stop=True)
            o.then_inc(fills(("attended", g)), 1)

        def in_row(x, t):
            return x[:, tokens_of(t)]

        pe.wait_ge(const_loaded, 16)
        pe.wait_ge(rows_loaded, 16 * 7)
        pe.transpose(bank("vectors")[:, 0:V_ALL], rows_v[0:V_ALL, :], ident[0:V_ALL, 0:V_ALL])
        pe.transpose(bank("vectors")[:, V_ALL:V_ALL + TAPS * WC], rows_c[0:TAPS * WC, :],
                     ident[0:TAPS * WC, 0:TAPS * WC]).then_inc(fills("vectors"), 1)
        turn("w_s", lambda k: w_s[:, k, :])
        for t in range(TT):
            pe.wait_ge(x0_ready, t + 1)
            for half in range(2):
                turn(("x0T", t, half), lambda k: x_in[:, t, (4 * half + k) * P:(4 * half + k + 1) * P])
        for t in (2, 3):
            for half in range(2):
                pe.wait_ge(*drained(("x0T", t, half)))

        for u in range(U_MERGE):
            if u < U_V:
                features(u, [("glu_g" if u % 2 else "glu_a", u // 2)], xT_hi, xT_lo)
            elif u < U_VSG:
                if u == U_V:
                    for t in range(TT):
                        open_bank(("v", t))
                tokens(u, u - U_V, u == U_V + 3, [bank(("v", t))[:] for t in range(TT)], xT_hi, xT_lo, in_row)
            elif u < U_QK:
                if u == U_VSG:
                    for t in range(TT):
                        open_bank(("vsg", t))
                tokens(u, u - U_VSG, u == U_VSG + 3, [bank(("vsg", t))[:] for t in range(TT)], xT_hi, xT_lo, in_row)
            elif u < U_USG:
                features(u, [("k" if u % 2 else "q", (u - U_QK) // 2)], xT_hi, xT_lo)
            else:
                c = u - U_USG
                features(u, [("usg", c)], xT_hi, xT_lo)
                open_bank(("spatial", c))
                pe.wait_ge(vs_ready, TT)
                pe.wait_ge(*drained("w_s"))
                for t in range(TT):
                    o = pe.matmul(bank(("spatial", c))[:, tokens_of(t)], vs[:, t, c * P:(c + 1) * P], w_sT[:, c, :],
                                  start=True, stop=True)
                o.then_inc(fills(("spatial", c)), 1)
            if 20 <= u < 28:
                if u == 20:
                    pe.wait_ge(v_windows, 16 * 8 * ROWS)
                attend(u - 20)
            if 19 <= u < 27:
                g = u - 19
                pe.wait_ge(probs_ready, g + 1)
                turn(("probsT", g), lambda k: probs[:, g % 2, k * P:(k + 1) * P])
            if 18 <= u < 26:
                scores(u - 18)

        pe.wait_ge(conv_ready, WC - 1)
        pe.wait_ge(pool_conv, TAPS)
        open_bank("conv_mean")
        for c in range(WC):
            o = pe.matmul(bank("conv_mean")[:], ones, conv[:, c, :], start=c == 0, stop=c == WC - 1)
        o.then_inc(fills("conv_mean"), 1)
        open_bank("conv_var")
        for c in range(WC):
            pe.wait_ge(squared, c + 1)
            o = pe.matmul(bank("conv_var")[:], ones, gate[:, c // 2, c % 2, :], start=c == 0, stop=c == WC - 1)
        o.then_inc(fills("conv_var"), 1)

        pe.wait_ge(*drained(("attended", 7)))
        pe.wait_ge(gated_lo, WC)
        with pe.Fori(0, 2) as i:
            for r in range(2):
                u = U_MERGE + 9 * r
                for d in range(2):
                    for n in range(3):
                        features(u, [("gate", r, d, n)], xT_hi, xT_lo, 18, i)
                        u += 1
                for n in range(3):
                    if n == 2:
                        pe.wait_ge(conv_lo, WC)
                    features(u, [("branch", r, d, n) for d in range(2)], branch_hi[n], branch_lo[n], 18, i)
                    u += 1
        pe.wait_ge(merged_lo, DC)
        for n in range(2):
            for t in range(TT):
                open_bank(("mixed", n, t))
            for k in range(4):
                tokens(U_WO + 4 * n + k, k, k == 3, [bank(("mixed", n, t))[:] for t in range(TT)], mT_hi, mT_lo,
                       in_row)

        for t in range(TT):
            pe.wait_ge(x1_ready, t + 1)
            for half in range(2):
                turn(("x1T", t, half), lambda k: x1[:, t, (4 * half + k) * P:(4 * half + k + 1) * P])
        for t in range(TT):
            for half in range(2):
                pe.wait_ge(*drained(("x1T", t, half)))
        pe.wait_ge(late_loaded, 16 * 7)
        for t in range(TT):
            for c in range(DC):
                o = pe.matmul(bank("router")[:, t * EXPERTS:(t + 1) * EXPERTS], x1T[:, c, tokens_of(t)],
                              w_router[:, c, :], start=c == 0, stop=c == DC - 1)
        o.then_inc(fills("router"), 1)
        pe.wait_ge(selected, 1)
        sel = r_sel[:].rearrange("p t g e -> p t (g e)")
        for t in range(TT + 1):
            out = bank("position")[:, t * EXPERTS:(t + 1) * EXPERTS]
            for k in range(min(t + 1, TT)):
                o = pe.matmul(out, before if k == t else ones, sel[:, k, :], start=k == 0, stop=k == min(t, TT - 1))
        o.then_inc(fills("position"), 1)

        def slots(n, e):
            pe.wait_ge(*m_empty(M_INFO, n))
            pe.wait_ge(onehot_ready, n + 1)
            for t in range(TT):
                row = info[:, t, e, :] if isinstance(e, int) else info[:, t, bass.ds(e, 1), :].rearrange(
                    "p e k -> p (e k)")
                o = pe.matmul(psum[M_INFO][:, 0:4], onehot[:, t, :], row, start=t == 0, stop=t == TT - 1)
            o.then_inc(psum_full[M_INFO], 1)

        def turn_xg(n, q, gathers):
            pe.wait_ge(gathered[q], gathers * 16 + 16)
            for half in range(2):
                pe.wait_ge(*m_empty(M_XT + half, n))
                for k in range(4):
                    c = 4 * half + k
                    o = pe.transpose(psum[M_XT + half][:, k * P:(k + 1) * P], xg[:, q, c * P:(c + 1) * P], ident)
                o.then_inc(psum_full[M_XT + half], 1)

        def hidden(b, n, q, j, k, per=0, i=None):
            if k == 0:
                pe.wait_ge(*m_empty(b, n))
                for half in range(2):
                    pe.wait_ge(*m_drained(M_XT + half, n))
            tokens(j, k, k == 3, [psum[b][:]], xgT_hi[:, q], xgT_lo[:, q], lambda x, t: x, per, i)

        def turn_h(n):
            pe.wait_ge(*m_empty(M_HT, n))
            pe.wait_ge(*m_drained(M_H3, n))
            for k in range(4):
                o = pe.transpose(psum[M_HT][:, k * P:(k + 1) * P], h[:, k * P:(k + 1) * P], ident)
            o.then_inc(psum_full[M_HT], 1)

        def output(n, j, k, per=0, i=None):
            if k == 0:
                pe.wait_ge(*m_drained(M_HT, n))
            if k % 2 == 0:
                pe.wait_ge(*m_empty(M_Y + k // 2, n))
            tokens(j, k % 2, k % 2 == 1, [psum[M_Y + k // 2][:]], hT_hi, hT_lo, lambda x, t: x, per, i)

        pe.wait_ge(routed, 1)
        slots(0, 0)
        slots(1, 1)
        turn_xg(0, 0, 0)
        for k in range(4):
            hidden(M_H1, 0, 0, U_MOE + k, k)
        with pe.Fori(0, 7) as i:
            for q in range(2):
                n, j = i * 2 + q, U_MOE + 4 + 12 * q
                for k in range(12):
                    if k < 4:
                        hidden(M_H3, n, q, j + k, k, 24, i)
                    elif k < 8:
                        hidden(M_H1, n + 1, 1 - q, j + k, k - 4, 24, i)
                    else:
                        output(n, j + k, k - 8, 24, i)
                    if k == 1:
                        turn_xg(n + 1, 1 - q, i + q)
                    if k == 5:
                        turn_h(n)
                    if k == 9:
                        slots(n + 2, n + 2)
        for n in (14, 15):
            j = U_MOE + 4 + 12 * n
            for k in range(4):
                hidden(M_H3, n, n % 2, j + k, k)
                if k == 1 and n == 14:
                    turn_xg(15, 1, 7)
            j += 4
            if n == 14:
                for k in range(4):
                    hidden(M_H1, 15, 1, j + k, k)
                    if k == 1:
                        turn_h(14)
                j += 4
            else:
                turn_h(15)
            for k in range(4):
                output(n, j + k, k)

        pe.wait_ge(flag_ready, 1)
        with pe.register("over_pe") as reg:
            pe.reg_load(reg, overflow[0:1, 0:1])
            with pe.If(pe.snap(reg) > 0):
                with pe.Fori(0, EXPERTS) as e:
                    for b in range(3):
                        n, j = e * 3 + (EXPERTS + b), U_OVER + 12 * b
                        slots(n, e)
                        turn_xg(n, 0, e * 3 + (EXPERTS // 2 + b))
                        for k in range(4):
                            hidden(M_H1, n, 0, j + k, k, 36, e)
                        for k in range(4):
                            hidden(M_H3, n, 0, j + 4 + k, k, 36, e)
                        turn_h(n)
                        for k in range(4):
                            output(n, j + 8 + k, k, 36, e)
                pe.nop()
            with pe.Else():
                pe.nop()

    moe.close()
    ctx.close()


_INS = ["x_prompt", "x_sample", "emb_ln_g", "emb_ln_b", "w_in", "b_in", "w_gate", "b_gate", "rpb", "w_a_o",
        "sg_ln_g", "sg_ln_b", "w_s", "b_s", "w_b_o", "conv_w", "conv_b", "cv_ln_g", "cv_ln_b", "w_c_o", "w_o", "b_o",
        "ln1_g", "ln1_b", "w_router", "b_router", "w_e1", "w_e3", "w_e2", "ln2_g", "ln2_b"]


def constants():
    import numpy as np

    c = np.zeros((P, C_ALL), np.float32)
    p = np.arange(P)
    c[:, C_IDENT:C_IDENT + P] = np.eye(P)
    c[:, C_BEFORE:C_BEFORE + P] = p[:, None] < p[None, :]
    c[:, C_IOTA:C_IOTA + P] = p
    c[:, C_ONES:C_ONES + P] = 1
    c[:, C_TOKEN:C_TOKEN + TT] = p[:, None] + P * np.arange(TT)
    c[:, C_HIGHER:C_HIGHER + EXPERTS] = 3 - np.arange(EXPERTS) % 4
    for pat, j in ((0, 0), (1, 1), (2, 3)):
        query = QCOLS * j + p % QCOLS
        start = np.clip(query - QCOLS // 2, 0, GRID - QCOLS)
        key = WINDOW[j] + np.arange(KCOLS)
        inside = (key >= start[:, None]) & (key < start[:, None] + QCOLS)
        c[:, C_MASK + KCOLS * pat:C_MASK + KCOLS * (pat + 1)] = np.where(inside, 0, -1e30)
    return c


def kernel(**inputs):
    import numpy as _np
    import concourse.bacc as _bacc
    from concourse import mybir as _mybir
    from concourse.bass_utils import run_bass_kernel_spmd as _run

    nc = _bacc.Bacc("TRN2", target_bir_lowering=False, num_devices=1)
    arrays, args = {}, {}
    for name in _INS + ["consts"]:
        a = constants() if name == "consts" else _np.ascontiguousarray(inputs[name])
        arrays[f"in_{name}_dram"] = a
        args[name] = nc.dram_tensor(f"in_{name}_dram", a.shape, _mybir.dt.from_np(a.dtype), kind="ExternalInput").ap()
    outs = [nc.dram_tensor(f"out_{i}_dram", (1, SEQ, D), F32, kind="ExternalOutput").ap() for i in range(2)]
    encoder_layer(nc, args, *outs)
    r = _run(nc, [arrays], core_ids=[0])
    return tuple(r.results[0][f"out_{i}_dram"] for i in range(2))
```

```python
from contextlib import ExitStack

import concourse.bass as bass
from concourse import mybir

P = 128
F32 = mybir.dt.float32
F32R = mybir.dt.float32r
I32 = mybir.dt.int32
ALU = mybir.AluOpType
ACT = mybir.ActivationFunctionType
AX = mybir.AxisListType

D = 1024
DC = D // P
T = 512
TT = T // P
SEQ = 256
W = 512
WC = W // P
GRID = 64
ROWS = SEQ // GRID
QCOLS = 16
KCOLS = 32
WINDOW = (0, 8, 24, 32)
PATTERN = (0, 1, 1, 2)
SHIFT = (0, -8, -16)
TAPS = 31
HALO = TAPS // 2
EXPERTS = 16
SLOTS = 128
FF = 512
ALPHA = 2.0 ** 0.25
EPS = 1e-5
QSCALE = 64 ** -0.5

RAW = 6
MORE = 6
SPLIT = 3
UNIT = 1024

C_IDENT, C_BEFORE, C_IOTA, C_ONES = 0, 128, 256, 384
C_TOKEN = 512
C_HIGHER = 516
C_MASK = 532
C_ALL = C_MASK + 3 * KCOLS

V_IN, V_GATE, V_CONVB, V_CVG, V_CVB, V_EMBG, V_EMBB, V_ALL = 0, 28, 52, 56, 60, 64, 72, 80

U_GLU, U_V, U_VSG, U_QK, U_USG = 0, 8, 12, 16, 24
U_MERGE = 28
U_WO = U_MERGE + 36
U_MOE = U_WO + 8
U_OVER = U_MOE + 12 * EXPERTS


class Banks:

    def __init__(self):
        self.used, self.full, self.at = [0] * 8, [0] * 8, {}

    def use(self, name, bank, unit=None):
        self.loop(1, 0, [(name, bank, unit)])

    def loop(self, times, units, uses):
        used, full = list(self.used), list(self.full)
        for name, bank, unit in uses:
            self.at[name] = [bank, used[bank], full[bank], unit, units]
            used[bank] += 1
            full[bank] += unit is None
        for name, bank, _ in uses:
            self.at[name] += [used[bank] - self.used[bank], full[bank] - self.full[bank]]
        self.used = [a + (b - a) * times for a, b in zip(self.used, used)]
        self.full = [a + (b - a) * times for a, b in zip(self.full, full)]


def plan_banks():
    b = Banks()
    b.use("vectors", 6)
    for c in range(DC):
        b.use(("x0T", c), c)
    b.use("w_s", 3)
    for c in range(WC):
        b.use(("glu_a", c), 4 + 2 * (c % 2), U_GLU + 2 * c)
        b.use(("glu_g", c), 5 + 2 * (c % 2), U_GLU + 2 * c + 1)
    for t in range(TT):
        b.use(("v", t), t, U_V + 3)
    for t in range(TT):
        b.use(("vsg", t), 4 + t, U_VSG + 3)
    for c in range(WC):
        b.use(("q", c), 4 + 2 * (c % 2), U_QK + 2 * c)
        b.use(("k", c), 5 + 2 * (c % 2), U_QK + 2 * c + 1)
    for g in range(8):
        b.use(("scores", g), g % 2)
        b.use(("probsT", g), 2)
        b.use(("attended", g), 3)
    for c in range(WC):
        b.use(("usg", c), 4 + c % 2, U_USG + c)
        b.use(("spatial", c), 6 + c % 2)
    b.use("conv_mean", 0)
    b.use("conv_var", 1)
    uses = []
    for r in range(2):
        for d in range(2):
            uses += [(("gate", r, d, n), 3 * d + n, U_MERGE + 9 * r + 3 * d + n) for n in range(3)]
        for n, bank in enumerate((6, 0, 2)):
            uses += [(("branch", r, d, n), bank + d, U_MERGE + 9 * r + 6 + n) for d in range(2)]
    b.loop(2, 18, uses)
    for n in range(2):
        for t in range(TT):
            b.use(("mixed", n, t), 4 * n + t, U_WO + 4 * n + 3)
    for t in range(TT):
        for h in range(2):
            b.use(("x1T", t, h), 2 * t + h)
    b.use("router", 0)
    b.use("r_s", 2)
    b.use("position", 1)
    return b


M_H1, M_H3, M_Y, M_XT, M_HT, M_INFO = 0, 1, 2, 4, 6, 7


def encoder_layer(nc, A, out_prompt, out_sample):
    banks = plan_banks()
    ctx = ExitStack()
    m_used, m_full = list(banks.used), list(banks.full)

    def sem(name):
        return ctx.enter_context(nc.semaphore(name))

    x0_dram = nc.dram_tensor("x0_scratch", (T, D), F32).ap()
    v_dram = nc.dram_tensor("v_scratch", (T, W), F32).ap()
    rpb_dram = nc.dram_tensor("rpb_scratch", (QCOLS, A["rpb"].shape[1] * A["rpb"].shape[2] * A["rpb"].shape[3]),
                              F32).ap()
    x1_dram = nc.dram_tensor("x1_scratch", (T, D), F32).ap()
    y_dram = nc.dram_tensor("y_scratch", (2 * T, D), F32).ap()

    def sb(stack, name, shape, dt=F32):
        return stack.enter_context(nc.sbuf_tensor(name, [P] + shape, dt))

    raw = sb(ctx, "raw", [RAW, UNIT])
    w_hi = sb(ctx, "w_hi", [SPLIT, UNIT], F32R)
    w_lo = sb(ctx, "w_lo", [SPLIT, UNIT], F32R)
    const = sb(ctx, "const", [C_ALL])
    vec = sb(ctx, "vec", [V_ALL])
    conv_col = sb(ctx, "conv_col", [TAPS, WC])
    stats = sb(ctx, "stats", [TT, 2, 6])
    mv = sb(ctx, "mv", [TT, 2])
    rstd = sb(ctx, "rstd", [TT])
    var_eps = sb(ctx, "var_eps", [TT])
    minus_half = sb(ctx, "minus_half", [TT])
    mu_rstd = sb(ctx, "mu_rstd", [TT])
    overflow = sb(ctx, "overflow", [1], I32)
    neg_max = sb(ctx, "neg_max", [2, 4])
    exp_sum = sb(ctx, "exp_sum", [2, 4])
    exp_inv = sb(ctx, "exp_inv", [2, 4])
    ident = const[:, C_IDENT:C_IDENT + P]
    before = const[:, C_BEFORE:C_BEFORE + P]
    iota = const[:, C_IOTA:C_IOTA + P]
    ones = const[:, C_ONES:C_ONES + P]
    token = const[:, C_TOKEN:C_TOKEN + TT]

    mix = ExitStack()
    xT_hi = sb(mix, "xT_hi", [DC, T], F32R)
    xT_lo = sb(mix, "xT_lo", [DC, T], F32R)
    branch_hi = [sb(mix, f"branch{n}_hi", [WC, T], F32R) for n in range(2)]
    branch_lo = [sb(mix, f"branch{n}_lo", [WC, T], F32R) for n in range(2)]
    conv_in = sb(mix, "conv_in", [WC, 2, SEQ + 2 * HALO])
    conv = sb(mix, "conv", [WC, T])
    early = ExitStack()
    qT = sb(early, "qT", [WC, T])
    kT = sb(early, "kT", [WC, T])
    v_win = sb(early, "v_win", [2, 4, W])
    bias = sb(early, "bias", [WC, 4, P])
    probs = sb(early, "probs", [2, W])
    probsT = sb(early, "probsT", [W])
    vs = sb(early, "vs", [TT, W])
    w_sT = sb(early, "w_sT", [4, P])
    b_s = sb(early, "b_s", [4, P])
    sg_g = sb(early, "sg_g", [W])
    sg_b = sb(early, "sg_b", [W])
    bv = sb(early, "bv", [W])
    bvs = sb(early, "bvs", [W])
    tmp = sb(early, "tmp", [2, W])
    conv_odd = sb(early, "conv_odd", [W])
    early.close()
    first = ExitStack()
    x_in = sb(first, "x_in", [TT, D])
    rows_v = sb(first, "rows_v", [P])
    rows_c = sb(first, "rows_c", [P])
    w_s = sb(first, "w_s_in", [4, P])
    first.close()
    late = ExitStack()
    branch_hi.append(sb(late, "branch2_hi", [WC, T], F32R))
    branch_lo.append(sb(late, "branch2_lo", [WC, T], F32R))
    mT_hi = sb(late, "mT_hi", [DC, T], F32R)
    mT_lo = sb(late, "mT_lo", [DC, T], F32R)
    gate = sb(late, "gate", [2, 3, T])
    part = sb(late, "part", [2, T])
    merged = sb(late, "merged", [2, T])
    late.close()
    mix.close()

    x1 = sb(ctx, "x1", [TT, D])
    ln1_g = sb(ctx, "ln1_g", [D])
    ln1_b = sb(ctx, "ln1_b", [D])
    b_o = sb(ctx, "b_o", [D])
    residual = ExitStack()
    emb_g = sb(residual, "emb_g", [D])
    emb_b = sb(residual, "emb_b", [D])
    residual.close()
    moe = ExitStack()
    ln2_g = sb(moe, "ln2_g", [D])
    ln2_b = sb(moe, "ln2_b", [D])
    tail = ExitStack()
    y_in = sb(tail, "y_in", [TT, 2, D])
    tail.close()
    raw_more = sb(moe, "raw_more", [MORE, UNIT])
    w_router = sb(moe, "w_router_in", [DC, EXPERTS])
    b_router = sb(moe, "b_router_in", [EXPERTS])
    scoresT = sb(moe, "scoresT", [T])
    r_s = sb(moe, "r_s", [TT, 4, 4])
    r_sb = sb(moe, "r_sb", [TT, 4, 4])
    r_ge = sb(moe, "r_ge", [TT, 4, 4])
    r_rank = sb(moe, "r_rank", [TT, 4, 4])
    r_sel = sb(moe, "r_sel", [TT + 1, 4, 4])
    r_tmp = sb(moe, "r_tmp", [TT, 4, 4])
    r_kth = sb(moe, "r_kth", [TT, 4, 4])
    g_sum = sb(moe, "g_sum", [TT, 4])
    g_ge = sb(moe, "g_ge", [TT, 4])
    g_rank = sb(moe, "g_rank", [TT, 4])
    w_sum = sb(moe, "w_sum", [TT])
    w_inv = sb(moe, "w_inv", [TT])
    position = sb(moe, "position", [TT, EXPERTS])
    info = sb(moe, "info", [TT, EXPERTS, 4])
    most = sb(moe, "most", [1])
    onehot = sb(moe, "onehot", [2, TT, SLOTS])
    slot_token = sb(moe, "slot_token", [2], I32)
    slot_row = sb(moe, "slot_row", [2], I32)
    slot_gate = sb(moe, "slot_gate", [2])
    slot_none = sb(moe, "slot_none", [1])
    xg = sb(moe, "xg", [2, D])
    xgT_hi = sb(moe, "xgT_hi", [2, DC, SLOTS], F32R)
    xgT_lo = sb(moe, "xgT_lo", [2, DC, SLOTS], F32R)
    h_silu = sb(moe, "h_silu", [FF])
    h = sb(moe, "h", [FF])
    hT_hi = sb(moe, "hT_hi", [4, SLOTS], F32R)
    hT_lo = sb(moe, "hT_lo", [4, SLOTS], F32R)
    y = sb(moe, "y", [2, D])
    routing = ExitStack()
    x1T = sb(routing, "x1T", [DC, T])
    routing.close()

    psum = [ctx.enter_context(nc.psum_tensor(f"bank{b}", [P, 512], F32)) for b in range(8)]

    const_loaded = sem("const_loaded")
    rows_loaded = sem("rows_loaded")
    x_loaded = [sem(f"x_loaded{t}") for t in range(TT)]
    early_loaded = sem("early_loaded")
    rpb_copied = sem("rpb_copied")
    bias_loaded = sem("bias_loaded")
    raw_loaded = [sem(f"raw_loaded{s}") for s in range(RAW + MORE)]
    hi_cast = sem("hi_cast")
    lo_cast = sem("lo_cast")
    unit_used = sem("unit_used")
    psum_full = [sem(f"psum_full{b}") for b in range(8)]
    psum_free = [sem(f"psum_free{b}") for b in range(8)]
    dve_step = sem("dve_step")
    pool_step = sem("pool_step")
    pool_go = sem("pool_go")
    halo_zero = sem("halo_zero")
    var_ready = sem("var_ready")
    rstd_ready = sem("rstd_ready")
    x0_normal = sem("x0_normal")
    x0T_full = sem("x0T_full")
    x0_stored = sem("x0_stored")
    x0T_hi_done = sem("x0T_hi_done")
    product_ready = sem("product_ready")
    pool_conv = sem("pool_conv")
    v_stored = sem("v_stored")
    v_windows = sem("v_windows")
    bias_ready = sem("bias_ready")
    max_ready = sem("max_ready")
    exp_done = sem("exp_done")
    probs_ready = sem("probs_ready")
    attn_hi = sem("attn_hi")
    vsg_gelu = sem("vsg_gelu")
    vs_ready = sem("vs_ready")
    gated = sem("gated")
    gated_hi = sem("gated_hi")
    gated_lo = sem("gated_lo")
    conv_ready = sem("conv_ready")
    centred = sem("centred")
    squared = sem("squared")
    conv_root = sem("conv_root")
    conv_scaled = sem("conv_scaled")
    conv_silu = sem("conv_silu")
    conv_hi = sem("conv_hi")
    conv_lo = sem("conv_lo")
    merged_ready = sem("merged_ready")
    merged_hi = sem("merged_hi")
    merged_lo = sem("merged_lo")
    x0_reloaded = sem("x0_reloaded")
    residual_loaded = sem("residual_loaded")
    late_loaded = sem("late_loaded")
    ln2_loaded = sem("ln2_loaded")
    x1_scaled = sem("x1_scaled")
    normalised = sem("normalised")
    scaled = sem("scaled")
    x1_ready = [sem(f"x1_ready{t}") for t in range(TT)]
    x1_stored = sem("x1_stored")
    scores_turned = sem("scores_turned")
    selected = sem("selected")
    routed = sem("routed")
    flag_ready = sem("flag_ready")
    onehot_ready = sem("onehot_ready")
    token_ready = sem("token_ready")
    gathered = [sem(f"gathered{q}") for q in range(2)]
    xg_hi = sem("xg_hi")
    hT_hi_done = sem("hT_hi_done")
    y_stored = [sem(f"y_stored{q}") for q in range(2)]
    all_stored = sem("all_stored")
    y_loaded = [sem(f"y_loaded{t}") for t in range(TT)]
    y_summed = sem("y_summed")
    final_step = sem("final_step")
    out_ready = sem("out_ready")
    out_stored = sem("out_stored")

    def nth(j, per=0, i=None):
        return j if i is None or not per else i * per + j

    def bank(name):
        return psum[banks.at[name][0]]

    def filled(name, i=None):
        b, _, full, unit, units, _, more = banks.at[name]
        if unit is None:
            return psum_full[b], nth(full + 1, more, i)
        return unit_used, nth(unit + 1, units, i)

    def empty(name, i=None):
        b, used, _, _, _, more, _ = banks.at[name]
        return psum_free[b], nth(used, more, i)

    def drained(name, i=None):
        b, used, _, _, _, more, _ = banks.at[name]
        return psum_free[b], nth(used + 1, more, i)

    def frees(name):
        return psum_free[banks.at[name][0]]

    def fills(name):
        return psum_full[banks.at[name][0]]

    def raw_slot(j):
        if j < U_MOE:
            return raw[:, j % RAW, :]
        s = (j - U_MOE) % (RAW + MORE)
        return raw_more[:, s, :] if s < MORE else raw[:, s - MORE, :]

    def raw_there(j, per=0, i=None):
        if j < U_MOE:
            return raw_loaded[j % RAW], nth(16 * (j // RAW + 1), 16 * per // RAW, i)
        s, turn = (j - U_MOE) % (RAW + MORE), (j - U_MOE) // (RAW + MORE) + 1
        if s < MORE:
            return raw_loaded[RAW + s], nth(16 * turn, 16 * per // (RAW + MORE), i)
        return raw_loaded[s - MORE], nth(16 * (turn + U_MOE // RAW), 16 * per // (RAW + MORE), i)

    def m_filled(b, n):
        return psum_full[b], n + (m_full[b] + 1)

    def m_empty(b, n):
        return psum_free[b], n + m_used[b]

    def m_drained(b, n):
        return psum_free[b], n + (m_used[b] + 1)

    def tokens_of(t):
        return slice(t * P, (t + 1) * P)

    def grid(row, seq, col, cols):
        return row[:, seq * SEQ:(seq + 1) * SEQ].rearrange("p (r c) -> p r c", c=GRID)[:, :, col:col + cols]

    products = {WC - 1: probs, WC - 2: tmp}

    def added(c, k):
        return k if c == WC - 1 else TAPS - 1 + k

    squares = (bvs[:], sg_g[:], sg_b[:], conv_odd[:])
    conv_vare, conv_rstd, conv_newton = bvs[:], sg_g[:], sg_b[:]

    def column(at):
        return vec[:, at:at + 1]

    def unit_of(tile, j, cols):
        return tile[:, j % SPLIT, :].rearrange("p (c n) -> p c n", n=cols)

    def attended_out(g, h2, rows):
        return bank(("attended", g))[rows, :].rearrange(
            "p (j q) -> p j q", j=4)[:, :, 64 * h2:64 * h2 + 64].rearrange("p j (r c) -> p j r c", r=ROWS)

    def attended_in(tile, g, rows):
        seq = g % 2
        return tile[rows, g // 2, seq * SEQ:(seq + 1) * SEQ].rearrange("p (r j c) -> p j r c", r=ROWS, j=4)

    w_in = A["w_in"][0].rearrange("(c p) n -> p c n", p=P)
    w_gate = A["w_gate"][0].rearrange("(c p) n -> p c n", p=P)
    w_branch = [A[n][0].rearrange("(c p) n -> p c n", p=P) for n in ("w_a_o", "w_b_o", "w_c_o")]
    w_o = A["w_o"][0].rearrange("(c p) n -> p c n", p=P)
    w_e1 = A["w_e1"][0].rearrange("e (c p) n -> p e c n", p=P)
    w_e3 = A["w_e3"][0].rearrange("e (c p) n -> p e c n", p=P)
    w_e2 = A["w_e2"][0].rearrange("e (c p) n -> p e c n", p=P)

    in_chunk = {}
    for c in range(WC):
        in_chunk |= {U_GLU + 2 * c: 20 + c, U_GLU + 2 * c + 1: 24 + c,
                     U_QK + 2 * c: c, U_QK + 2 * c + 1: 4 + c, U_USG + c: 12 + c}

    block = ctx.enter_context(nc.Block())

    @block.sync
    def _(sp):
        def load(j, source, n, per=0, i=None):
            if RAW <= j < U_MOE:
                sp.wait_ge(lo_cast, nth(j - RAW + 1, per, i))
            if j >= U_MOE + MORE or (j >= U_MOE and i is not None):
                sp.wait_ge(lo_cast, nth(j - RAW - MORE + 1, per, i))
            sp.dma_start(raw_slot(j).rearrange("p (c n) -> p c n", n=n), source).then_inc(
                raw_there(j)[0], 16)

        for t in range(TT):
            x = (A["x_prompt"], A["x_sample"])[t // 2][0]
            sp.dma_start(x_in[:, t, :], x[tokens_of(t % 2), :]).then_inc(x_loaded[t], 16)
        copy, heads, table_row = rpb_dram.shape[1], A["rpb"].shape[2] * A["rpb"].shape[3], A["rpb"].shape[3]

        def load_bias(h2, hp, qr):
            for pat, j in ((0, 0), (1, 1), (2, 3)):
                at = (2 * hp + h2) * heads + (7 - qr) * table_row + 15 + SHIFT[pat]
                source = bass.AP(tensor=rpb_dram.tensor, offset=rpb_dram.offset + at,
                                 ap=[[copy - 1, QCOLS], [table_row, ROWS], [1, KCOLS]])
                rows = slice(64 * h2 + QCOLS * qr, 64 * h2 + QCOLS * (qr + 1))
                sp.dma_start(bias[rows, hp, j, :].rearrange("p (r c) -> p r c", r=ROWS), source).then_inc(
                    bias_loaded, 16)

        sp.wait_ge(rows_loaded, 16 * 9)
        for u in range(U_MERGE):
            if u == 6:
                for t in range(TT):
                    sp.wait_ge(x0_normal, t + 1)
                    sp.dma_start(x0_dram[tokens_of(t), :], x_in[:, t, :]).then_inc(x0_stored, 16)
                sp.wait_ge(x0_stored, 16 * TT)
                sp.wait_ge(*drained("w_s"))
                sp.wait_ge(rpb_copied, 16)
            if 6 <= u < 14:
                for qr in range(ROWS):
                    load_bias((u - 6) % 2, (u - 6) // 2, qr)
            if u == 17:
                for t in range(TT):
                    sp.wait_ge(*drained(("v", t)))
                    sp.dma_start(v_dram[tokens_of(t), :], vs[:, t, :]).then_inc(v_stored, 16)
            if u in (18, 19):
                seq = u - 18
                sp.wait_ge(v_stored, 16 * TT)
                v_grid = v_dram[seq * SEQ:(seq + 1) * SEQ, :].rearrange("(r c) n -> r c n", c=GRID)
                for j in range(4):
                    sp.dma_start(v_win[:, seq, j, :], v_grid[:, WINDOW[j]:WINDOW[j] + KCOLS, :]).then_inc(
                        v_windows, 16)
            if u in in_chunk:
                f = in_chunk[u]
                load(u, w_in[:, :, f * P:(f + 1) * P], P)
            else:
                k, col = (u - U_V, 1024) if u < U_VSG else (u - U_VSG, 2048)
                load(u, w_in[:, 2 * k:2 * k + 2, col:col + W], W)
        with sp.Fori(0, 2) as i:
            for r in range(2):
                u = U_MERGE + 9 * r
                for d in range(2):
                    for n in range(3):
                        load(u, w_gate[:, :, bass.ds(i * 512 + (n * D + (2 * r + d) * P), P)], P, 18, i)
                        u += 1
                for n in range(3):
                    load(u, w_branch[n][:, :, bass.ds(i * 512 + 2 * r * P, 2 * P)], 2 * P, 18, i)
                    u += 1
        for n in range(2):
            for k in range(4):
                load(U_WO + 4 * n + k, w_o[:, 2 * k:2 * k + 2, n * 512:(n + 1) * 512], 512)

        def load_expert(kind, j, e, per=0, i=None):
            for k in range(4):
                if kind == 2:
                    source = w_e2[:, e, 2 * (k % 2):2 * (k % 2) + 2, (k // 2) * 512:(k // 2 + 1) * 512]
                else:
                    source = (w_e1 if kind == 1 else w_e3)[:, e, 2 * k:2 * k + 2, :]
                if i is not None:
                    source = source.rearrange("p e c n -> p (e c) n")
                load(j + k, source, 512, per, i)

        sp.wait_ge(unit_used, U_WO)
        load_expert(1, U_MOE, 0)
        load_expert(3, U_MOE + 4, 0)
        load_expert(1, U_MOE + 8, 1)
        for t in range(TT):
            sp.wait_ge(x1_ready[t], 1)
            sp.dma_start(x1_dram[tokens_of(t), :], x1[:, t, :]).then_inc(x1_stored, 16)
        with sp.Fori(0, 7) as i:
            for q in range(2):
                j = U_MOE + 12 + 12 * q
                load_expert(2, j, bass.ds(i * 2 + q, 1), 24, i)
                load_expert(3, j + 4, bass.ds(i * 2 + (q + 1), 1), 24, i)
                if q == 0:
                    load_expert(1, j + 8, bass.ds(i * 2 + 2, 1), 24, i)
                else:
                    load_expert(1, j + 8, bass.ds(i * 2 + 3, 1), 24, i)
        j = U_MOE + 12 + 12 * 14
        load_expert(2, j, 14)
        load_expert(3, j + 4, 15)
        load_expert(2, j + 8, 15)

        sp.wait_ge(flag_ready, 1)
        with sp.register("over_sp") as reg:
            sp.reg_load(reg, overflow[0:1, 0:1])
            with sp.If(sp.snap(reg) > 0):
                with sp.Fori(0, EXPERTS) as e:
                    for b in range(3):
                        j = U_OVER + 12 * b
                        load_expert(1, j, bass.ds(e, 1), 36, e)
                        load_expert(3, j + 4, bass.ds(e, 1), 36, e)
                        load_expert(2, j + 8, bass.ds(e, 1), 36, e)
                sp.nop()
            with sp.Else():
                sp.nop()

        sp.wait_ge(all_stored, 1)
        for t in range(TT):
            for k in range(2):
                sp.dma_start(y_in[:, t, k, :], y_dram[k * T + t * P:k * T + (t + 1) * P, :]).then_inc(
                    y_loaded[t], 16)
        for t in range(TT):
            sp.wait_ge(out_ready, t + 1)
            o = (out_prompt, out_sample)[t // 2][0]
            sp.dma_start(o[tokens_of(t % 2), :], x1[:, t, :]).then_inc(out_stored, 16)
        sp.wait_ge(out_stored, 16 * TT)

    @block.scalar
    def _(act):
        act.dma_start(const[:], A["consts"]).then_inc(const_loaded, 16)
        for at, n, a in ((V_IN, 28, "b_in"), (V_GATE, 24, "b_gate"), (V_CONVB, 4, "conv_b"),
                         (V_CVG, 4, "cv_ln_g"), (V_CVB, 4, "cv_ln_b")):
            act.dma_start(rows_v[at:at + n, :], A[a][0].rearrange("(r c) -> r c", c=P)).then_inc(rows_loaded, 16)
        for at, a in ((V_EMBG, "emb_ln_g"), (V_EMBB, "emb_ln_b")):
            act.dma_start(rows_v[at:at + DC, :], A[a].rearrange("(r c) -> r c", c=P)).then_inc(rows_loaded, 16)
        act.dma_start(rows_c[0:TAPS * WC, :], A["conv_w"][0].rearrange("t (c p) -> (t c) p", p=P)).then_inc(
            rows_loaded, 16)
        act.dma_start(w_s[:], A["w_s"][0].rearrange("g t s -> t g s")).then_inc(rows_loaded, 16)

        def cast_hi(j, per=0, i=None):
            act.wait_ge(*raw_there(j, per, i))
            if j >= SPLIT:
                act.wait_ge(unit_used, nth(j - SPLIT + 1, per, i))
            act.copy(w_hi[:, j % SPLIT, :], raw_slot(j)).then_inc(hi_cast, 1)

        for t in range(TT):
            act.wait_ge(rstd_ready, t + 1)
            act.activation(x_in[:, t, :], x_in[:, t, :], ACT.Identity, scale=rstd[:, t:t + 1],
                           bias=mu_rstd[:, t:t + 1]).then_inc(x0_normal, 1)
        cast_hi(0)
        act.wait_ge(*drained("vectors"))
        for c in range(DC + 1):
            if c < DC:
                if c >= WC:
                    act.wait_ge(*drained(("x0T", c - WC)))
                act.wait_ge(*filled(("x0T", c)))
                act.activation(conv[:, c % WC, :], bank(("x0T", c))[:], ACT.Identity, scale=column(V_EMBG + c),
                               bias=column(V_EMBB + c)).then_inc(x0T_full, 1)
            if c:
                act.wait_ge(x0T_full, c)
                act.copy(xT_hi[:, c - 1, :], conv[:, (c - 1) % WC, :]).then_inc(x0T_hi_done, 1)
        cast_hi(1)
        act.wait_ge(*filled("w_s"))
        act.wait_ge(x0_stored, 16 * TT)

        def glu(c):
            if c:
                act.wait_ge(*drained(("glu_a", c - 1)))
            act.wait_ge(*filled(("glu_g", c)))
            act.activation(tmp[:, 0, :], bank(("glu_g", c))[:], ACT.Sigmoid,
                           bias=column(V_IN + 24 + c)).then_inc(frees(("glu_g", c)), 1)

        def keys(c):
            act.wait_ge(*filled(("k", c)))
            act.activation(kT[:, c, :], bank(("k", c))[:], ACT.Identity,
                           bias=column(V_IN + 4 + c)).then_inc(frees(("k", c)), 1)

        def queries(c):
            act.wait_ge(*filled(("q", c)))
            for s in range(2):
                tokens = slice(s * SEQ, (s + 1) * SEQ)
                o = act.activation(qT[:, c, tokens].rearrange("p (j r c) -> p r j c", j=4, r=ROWS),
                                   bank(("q", c))[:, tokens].rearrange("p (r j c) -> p r j c", j=4, r=ROWS),
                                   ACT.Identity, bias=column(V_IN + c))
            o.then_inc(frees(("q", c)), 1)

        def exp_rows(g):
            act.wait_ge(max_ready, g + 1)
            for j in range(4):
                key = probs[:, g % 2, j * P:(j + 1) * P]
                o = act.activation(key, key, ACT.Exp, bias=neg_max[:, g % 2, j:j + 1],
                                   accum_out=exp_sum[:, g % 2, j:j + 1])
            o.then_inc(exp_done, 1)

        def copy_probsT(g):
            act.wait_ge(*filled(("probsT", g)))
            if g:
                act.wait_ge(*filled(("attended", g - 1)))
            act.copy(probsT[:], bank(("probsT", g))[:]).then_inc(frees(("probsT", g)), 1)

        def split_attended(g):
            act.wait_ge(*filled(("attended", g)))
            for h2 in range(2):
                rows = slice(64 * h2, 64 * h2 + 64)
                o = act.copy(attended_in(branch_hi[0], g, rows), attended_out(g, h2, rows))
            o.then_inc(attn_hi, 1)

        def product(c, k):
            if k == 0:
                act.wait_ge(*drained(("glu_a", c)))
            if k >= 3:
                act.wait_ge(pool_conv, added(c, k - 2))
            out = (products[c][:, k % 2, :] if k else conv[:, c, :]).rearrange("p (s t) -> p s t", s=2)
            act.activation(out, conv_in[:, c, :, k:k + SEQ], ACT.Identity, scale=conv_col[:, k, c:c + 1],
                           bias=column(V_CONVB + c) if k == 0 else 0.0).then_inc(product_ready, 1)

        def gated_chunk_hi(c):
            act.wait_ge(gated, c + 1)
            act.copy(branch_hi[1][:, c, :], tmp[:, c % 2, :]).then_inc(gated_hi, 1)

        for u in range(U_MERGE + 1):
            if u < U_MERGE:
                cast_hi(u + 2)
            if 20 <= u < 28:
                copy_probsT(u - 20)
            if 21 <= u < 29:
                split_attended(u - 21)
            if u > U_USG:
                gated_chunk_hi(u - U_USG - 1)
            if u == 25:
                for c in range(WC):
                    act.wait_ge(centred, c + 1)
                    act.activation(squares[c], conv[:, c, :], ACT.Square).then_inc(squared, 1)
            if u == 26:
                act.wait_ge(*drained("conv_var"))
                act.activation(conv_rstd, conv_vare, ACT.Sqrt).then_inc(conv_root, 1)
            if u < U_V and u % 2:
                glu(u // 2)
            if 8 <= u < 16:
                for k in range(4 * (u - 8), min(TAPS, 4 * (u - 7))):
                    product(WC - 1, k)
            if 16 <= u < 24:
                for k in range(4 * (u - 16), min(TAPS, 4 * (u - 15))):
                    product(WC - 2, k)
            if U_QK <= u < U_USG:
                c = (u - U_QK) // 2
                keys(c) if u % 2 else queries(c)
            if 18 <= u < 26:
                exp_rows(u - 18)
            if u == U_VSG + 3:
                for t in range(TT):
                    act.wait_ge(*drained(("vsg", t)))
                    act.activation(vs[:, t, :], vs[:, t, :], ACT.Gelu_apprx_tanh).then_inc(vsg_gelu, 1)
            if U_USG <= u < U_MERGE:
                c = u - U_USG
                if c == 0:
                    act.wait_ge(pool_conv, added(WC - 2, TAPS - 1))
                if c >= 2:
                    act.wait_ge(gated_lo, c - 1)
                act.wait_ge(*filled(("usg", c)))
                act.activation(tmp[:, c % 2, :], bank(("usg", c))[:], ACT.Gelu_apprx_tanh,
                               bias=column(V_IN + 12 + c)).then_inc(frees(("usg", c)), 1)

        for c in range(WC):
            act.wait_ge(conv_scaled, c + 1)
            act.activation(conv[:, c, :], conv[:, c, :], ACT.Silu, bias=column(V_CVB + c),
                           scale=column(V_CVG + c)).then_inc(conv_silu, 1)
        for c in range(WC):
            act.wait_ge(conv_silu, c + 1)
            act.copy(branch_hi[2][:, c, :], conv[:, c, :]).then_inc(conv_hi, 1)

        with act.Fori(0, 2) as i:
            for r in range(2):
                u = U_MERGE + 9 * r
                for d in range(2):
                    for n in range(3):
                        cast_hi(u + 2, 18, i)
                        name = ("gate", r, d, n)
                        if r:
                            act.wait_ge(*drained(("branch", r - 1, d, n), i))
                        else:
                            act.wait_ge(*drained(("branch", 1, d, n), i - 1))
                        act.wait_ge(*filled(name, i))
                        act.activation(gate[:, d, n, :], bank(name)[:], ACT.Sigmoid,
                                       bias=vec[:, bass.ds(i * 4 + (V_GATE + n * DC + 2 * r + d), 1)]).then_inc(
                            frees(name), 1)
                        u += 1
                for n in range(3):
                    cast_hi(u + 2, 18, i)
                    u += 1
                for d in range(2):
                    act.wait_ge(merged_ready, i * 4 + (2 * r + d + 1))
                    act.copy(mT_hi[:, bass.ds(i * 4 + (2 * r + d), 1), :].rearrange("p o n -> p (o n)"),
                             merged[:, d, :]).then_inc(merged_hi, 1)
        for u in range(U_WO, U_MOE):
            cast_hi(u + 2)

        for t in range(TT):
            act.wait_ge(rstd_ready, 6 + t)
            act.activation(x1[:, t, :], x1[:, t, :], ACT.Identity, scale=rstd[:, t:t + 1],
                           bias=mu_rstd[:, t:t + 1]).then_inc(normalised, 1)
        for t in range(TT):
            for half in range(2):
                name = ("x1T", t, half)
                act.wait_ge(*filled(name))
                act.copy(x1T[:, 4 * half:4 * half + 4, tokens_of(t)],
                         bank(name)[:].rearrange("p (c n) -> p c n", c=4)).then_inc(frees(name), 1)
        act.wait_ge(*filled("router"))
        act.activation(scoresT[0:EXPERTS, :], bank("router")[0:EXPERTS, :], ACT.Sigmoid).then_inc(frees("router"), 1)

        def split_xg(n, q):
            for half in range(2):
                act.wait_ge(*m_filled(M_XT + half, n))
                act.copy(xgT_hi[:, q, 4 * half:4 * half + 4, :],
                         psum[M_XT + half][:].rearrange("p (c n) -> p c n", c=4)).then_inc(xg_hi, 1)

        def silu(unit, n, h_before=None):
            act.wait_ge(unit_used, unit + 1)
            if h_before is not None:
                act.wait_ge(*m_drained(M_H3, h_before))
            act.activation(h_silu[:], psum[M_H1][:], ACT.Silu).then_inc(psum_free[M_H1], 1)

        def split_hT(n):
            act.wait_ge(*m_filled(M_HT, n))
            act.copy(hT_hi[:].rearrange("p c n -> p (c n)"), psum[M_HT][:]).then_inc(hT_hi_done, 1)

        def scale_y(unit, n, q, half):
            act.wait_ge(unit_used, unit + 1)
            act.wait_ge(*m_drained(M_INFO, n))
            act.activation(y[:, q, half * 512:(half + 1) * 512], psum[M_Y + half][:], ACT.Copy,
                           scale=slot_gate[:, q:q + 1]).then_inc(psum_free[M_Y + half], 1)

        def expert(n, q, j, per=0, i=None):
            for k in range(12):
                if j + k + 2 < U_OVER:
                    cast_hi(j + k + 2, per, i)
                if k == 1:
                    split_xg(n + 1, 1 - q)
                if k == 5:
                    split_hT(n)
                if k == 7:
                    silu(nth(j + 7, per, i), n + 1, n)
                if k == 9:
                    scale_y(nth(j + 9, per, i), n, q, 0)
                if k == 11:
                    scale_y(nth(j + 11, per, i), n, q, 1)

        split_xg(0, 0)
        for k in range(4):
            cast_hi(U_MOE + k + 2)
        silu(U_MOE + 3, 0)
        with act.Fori(0, 7) as i:
            for q in range(2):
                expert(i * 2 + q, q, U_MOE + 4 + 12 * q, 24, i)
        expert(14, 0, U_MOE + 4 + 12 * 14)
        j = U_MOE + 4 + 12 * 15
        for k in range(8):
            if j + k + 2 < U_OVER:
                cast_hi(j + k + 2)
            if k == 3:
                split_hT(15)
            if k == 5:
                scale_y(j + 5, 15, 1, 0)
            if k == 7:
                scale_y(j + 7, 15, 1, 1)

        act.wait_ge(flag_ready, 1)
        with act.register("over_act") as reg:
            act.reg_load(reg, overflow[0:1, 0:1])
            with act.If(act.snap(reg) > 0):
                with act.Fori(0, EXPERTS) as e:
                    for b in range(3):
                        n, j = e * 3 + (EXPERTS + b), U_OVER + 12 * b
                        split_xg(n, 0)
                        for k in range(4):
                            cast_hi(j + k, 36, e)
                        silu(nth(j + 3, 36, e), n)
                        for k in range(4, 8):
                            cast_hi(j + k, 36, e)
                        split_hT(n)
                        for k in range(8, 12):
                            cast_hi(j + k, 36, e)
                            if k % 2:
                                scale_y(nth(j + k, 36, e), n, 0, (k - 8) // 2)
                act.nop()
            with act.Else():
                act.nop()

        for t in range(TT):
            act.wait_ge(rstd_ready, 10 + t)
            act.activation(x1[:, t, :], x1[:, t, :], ACT.Identity, scale=rstd[:, t:t + 1],
                           bias=mu_rstd[:, t:t + 1]).then_inc(normalised, 1)

    @block.vector
    def _(dve):
        steps = [0, 0, None]

        def step(k=1):
            steps[0] += k
            return steps[0] if steps[2] is None else steps[2] * steps[1] + steps[0]

        def cast_lo(j, per=0, i=None):
            dve.wait_ge(hi_cast, nth(j + 1, per, i))
            dve.tensor_tensor(w_lo[:, j % SPLIT, :], raw_slot(j), w_hi[:, j % SPLIT, :].bitcast(F32),
                              ALU.subtract).then_inc(lo_cast, 1)

        def row_stats(x, t):
            halves = x.shape[-1] // 512
            for k in range(halves):
                dve.bn_stats(stats[:, t, k, :], x[:, k * 512:(k + 1) * 512]).then_inc(dve_step, 1)
            dve.wait_ge(dve_step, step(halves))
            dve.bn_aggr(mv[:, t, :], stats[:, t, 0:halves, :].rearrange("p k s -> p (k s)")).then_inc(dve_step, 1)
            dve.wait_ge(dve_step, step())
            return dve.tensor_scalar(var_eps[:, t:t + 1], mv[:, t, 1:2], EPS, None, ALU.add)

        def normalise(x, t, g, b):
            dve.tensor_scalar(x, x, mv[:, t, 0:1], rstd[:, t:t + 1], ALU.subtract, ALU.mult).then_inc(dve_step, 1)
            dve.wait_ge(dve_step, step())
            dve.tensor_tensor(x, x, g, ALU.mult).then_inc(dve_step, 1)
            dve.wait_ge(dve_step, step())
            return dve.tensor_tensor(x, x, b, ALU.add)

        for t in range(TT):
            dve.wait_ge(x_loaded[t], 16)
            row_stats(x_in[:, t, :], t).then_inc(var_ready, 1)
        dve.wait_ge(*filled("vectors"))
        dve.tensor_copy(conv_col[:].rearrange("p t c -> p (t c)"), bank("vectors")[:, V_ALL:V_ALL + TAPS * WC])
        dve.tensor_copy(vec[:], bank("vectors")[:, 0:V_ALL]).then_inc(frees("vectors"), 1)
        cast_lo(0)
        for c in range(DC):
            dve.wait_ge(x0T_hi_done, c + 1)
            dve.tensor_tensor(xT_lo[:, c, :], conv[:, c % WC, :], xT_hi[:, c, :].bitcast(F32),
                              ALU.subtract).then_inc(frees(("x0T", c)), 1)
        cast_lo(1)
        dve.wait_ge(*filled("w_s"))
        dve.wait_ge(x0_stored, 16 * TT)
        dve.tensor_copy(w_sT[:].rearrange("p g t -> p (g t)"), bank("w_s")[:]).then_inc(frees("w_s"), 1)
        dve.wait_ge(*drained("vectors"))

        last = {0: 0, 1: 0}

        conv_steps = (WC - 2) * (TAPS + 1)

        def convolve(start, end):
            for n in range(start, min(end, conv_steps)):
                c, k = divmod(n, TAPS + 1)
                shifted = None if k == TAPS else conv_in[:, c, :, k:k + SEQ]
                even = conv[:, c, :].rearrange("p (s t) -> p s t", s=2)
                odd = conv_odd[:].rearrange("p (s t) -> p s t", s=2)
                if k == 0:
                    dve.wait_ge(*drained(("glu_a", c)))
                    o = dve.tensor_scalar(even, shifted, conv_col[:, k, c:c + 1], column(V_CONVB + c),
                                          ALU.mult, ALU.add)
                elif k == TAPS:
                    dve.wait_ge(dve_step, steps[0])
                    dve.tensor_tensor(even, even, odd, ALU.add).then_inc(conv_ready, 1)
                    continue
                elif k == 1:
                    if c:
                        dve.wait_ge(conv_ready, c)
                    o = dve.tensor_scalar(odd, shifted, conv_col[:, k, c:c + 1], None, ALU.mult)
                else:
                    dve.wait_ge(dve_step, last[k % 2])
                    sum_ = odd if k % 2 else even
                    o = dve.scalar_tensor_tensor(out=sum_, in0=shifted, scalar=conv_col[:, k, c:c + 1], in1=sum_,
                                                 op0=ALU.mult, op1=ALU.add)
                o.then_inc(dve_step, 1)
                last[k % 2] = step()

        def glu(c):
            dve.wait_ge(*filled(("glu_a", c)))
            dve.wait_ge(*drained(("glu_g", c)))
            if c == 0:
                dve.wait_ge(halo_zero, 1)
            dve.scalar_tensor_tensor(
                out=conv_in[:, c, :, HALO:HALO + SEQ], in0=bank(("glu_a", c))[:].rearrange("p (s t) -> p s t", s=2),
                scalar=column(V_IN + 20 + c), in1=tmp[:, 0, :].rearrange("p (s t) -> p s t", s=2),
                op0=ALU.add, op1=ALU.mult).then_inc(frees(("glu_a", c)), 1)

        def mask_scores(g):
            dve.wait_ge(*filled(("scores", g)))
            if g == 0:
                dve.wait_ge(bias_ready, 4)
                dve.wait_ge(pool_conv, TAPS - 1)
            if g >= 2:
                dve.wait_ge(*filled(("probsT", g - 2)))
            row = probs[:, g % 2, :]
            dve.scalar_tensor_tensor(out=row, in0=bank(("scores", g))[:], scalar=QSCALE,
                                     in1=bias[:, g // 2, :, :].rearrange("p j k -> p (j k)"),
                                     op0=ALU.mult, op1=ALU.add).then_inc(frees(("scores", g)), 1)
            dve.wait_ge(*drained(("scores", g)))
            dve.tensor_reduce(neg_max[:, g % 2, :], row.rearrange("p (j k) -> p j k", j=4), AX.X,
                              ALU.max).then_inc(dve_step, 1)
            dve.wait_ge(dve_step, step())
            dve.tensor_scalar(neg_max[:, g % 2, :], neg_max[:, g % 2, :], -1.0, None, ALU.mult).then_inc(max_ready, 1)

        def divide_probs(g):
            dve.wait_ge(exp_done, g + 1)
            dve.reciprocal(exp_inv[:, g % 2, :], exp_sum[:, g % 2, :]).then_inc(dve_step, 1)
            dve.wait_ge(dve_step, step())
            row = probs[:, g % 2, :].rearrange("p (j k) -> p j k", j=4)
            dve.tensor_tensor(row, row, exp_inv[:, g % 2, :].unsqueeze(2).to_broadcast([P, 4, P]),
                              ALU.mult).then_inc(probs_ready, 1)

        def split_attended(g):
            dve.wait_ge(attn_hi, g + 1)
            for h2 in range(2):
                rows = slice(64 * h2, 64 * h2 + 64)
                o = dve.tensor_tensor(attended_in(branch_lo[0], g, rows), attended_out(g, h2, rows),
                                      attended_in(branch_hi[0], g, rows).bitcast(F32), ALU.subtract)
            o.then_inc(frees(("attended", g)), 1)

        def gated_chunk_lo(c):
            dve.wait_ge(gated_hi, c + 1)
            dve.tensor_tensor(branch_lo[1][:, c, :], tmp[:, c % 2, :], branch_hi[1][:, c, :].bitcast(F32),
                              ALU.subtract).then_inc(gated_lo, 1)

        for u in range(U_MERGE + 1):
            if u < U_MERGE:
                cast_lo(u + 2)
            if 19 <= u < 27:
                divide_probs(u - 19)
            if 21 <= u < 29:
                split_attended(u - 21)
            if u > U_USG:
                gated_chunk_lo(u - U_USG - 1)
            if u == 25:
                dve.wait_ge(*filled("conv_mean"))
                for c in range(WC):
                    dve.scalar_tensor_tensor(out=conv[:, c, :], in0=bank("conv_mean")[:], scalar=-1.0 / W,
                                             in1=conv[:, c, :], op0=ALU.mult, op1=ALU.add).then_inc(centred, 1)
                dve.wait_ge(centred, WC)
                dve.sem_inc(frees("conv_mean"), 1)
            if u == 26:
                dve.wait_ge(*filled("conv_var"))
                dve.tensor_scalar(conv_vare, bank("conv_var")[:], 1.0 / W, EPS, ALU.mult, ALU.add).then_inc(
                    frees("conv_var"), 1)
                dve.wait_ge(conv_root, 1)
                dve.reciprocal(conv_rstd, conv_rstd).then_inc(dve_step, 1)
                dve.wait_ge(dve_step, step())
                dve.scalar_tensor_tensor(out=conv_newton, in0=conv_rstd, scalar=-0.5, in1=conv_rstd, op0=ALU.mult,
                                         op1=ALU.mult).then_inc(dve_step, 1)
                dve.wait_ge(dve_step, step())
                dve.tensor_tensor(conv_newton, conv_newton, conv_vare, ALU.mult).then_inc(dve_step, 1)
                dve.wait_ge(dve_step, step())
                dve.scalar_tensor_tensor(out=conv_rstd, in0=conv_newton, scalar=1.5, in1=conv_rstd, op0=ALU.add,
                                         op1=ALU.mult).then_inc(dve_step, 1)
                dve.wait_ge(dve_step, step())
                for c in range(WC):
                    dve.tensor_tensor(conv[:, c, :], conv[:, c, :], conv_rstd, ALU.mult).then_inc(conv_scaled, 1)
            if u < U_V and u % 2:
                glu(u // 2)
            if u == 17:
                dve.wait_ge(bias_loaded, 16 * 12 * 8)
                for n, j in enumerate((0, 2, 1, 3)):
                    mask = const[:, C_MASK + KCOLS * PATTERN[j]:C_MASK + KCOLS * (PATTERN[j] + 1)]
                    if j == 1:
                        dve.wait_ge(bias_ready, n)
                    dve.tensor_tensor(bias[:, :, j, :].rearrange("p h (r c) -> p h r c", r=ROWS),
                                      bias[:, :, 1 if j == 2 else j, :].rearrange("p h (r c) -> p h r c", r=ROWS),
                                      mask.unsqueeze(1).unsqueeze(1).to_broadcast([P, WC, ROWS, KCOLS]),
                                      ALU.add).then_inc(bias_ready, 1)
            if u < U_V:
                convolve(5 * (u - 1) if u else 0, 5 * u)
            elif u < 16:
                convolve(35 + 4 * (u - 8), 35 + 4 * (u - 7))
            if 18 <= u < 26:
                mask_scores(u - 18)
            if u == U_V + 3:
                dve.wait_ge(early_loaded, 16 * 5)
                for t in range(TT):
                    dve.wait_ge(*filled(("v", t)))
                    dve.tensor_tensor(vs[:, t, :], bank(("v", t))[:], bv[:],
                                      ALU.add).then_inc(frees(("v", t)), 1)
            if u == U_VSG + 3:
                dve.wait_ge(v_stored, 16 * TT)
                for t in range(TT):
                    dve.wait_ge(*filled(("vsg", t)))
                    dve.tensor_tensor(vs[:, t, :], bank(("vsg", t))[:], bvs[:], ALU.add).then_inc(
                        frees(("vsg", t)), 1)
            if U_VSG + 4 <= u < U_VSG + 8:
                t = u - U_VSG - 4
                dve.wait_ge(vsg_gelu, t + 1)
                row_stats(vs[:, t, :], t).then_inc(var_ready, 1)
            if U_VSG + 8 <= u < U_VSG + 12:
                dve.wait_ge(rstd_ready, 5)
                normalise(vs[:, u - U_VSG - 8, :], u - U_VSG - 8, sg_g[:], sg_b[:]).then_inc(vs_ready, 1)
            if U_USG <= u < U_MERGE:
                c = u - U_USG
                dve.wait_ge(*filled(("spatial", c)))
                if c:
                    dve.wait_ge(gated, c)
                dve.tensor_tensor(bv[:].rearrange("p (t n) -> p t n", t=TT),
                                  bank(("spatial", c))[:].rearrange("p (t n) -> p t n", t=TT),
                                  b_s[:, c, :].unsqueeze(1).to_broadcast([P, TT, P]), ALU.add).then_inc(
                    frees(("spatial", c)), 1)
                dve.wait_ge(*drained(("spatial", c)))
                dve.wait_ge(*drained(("usg", c)))
                dve.tensor_tensor(tmp[:, c % 2, :], bv[:], tmp[:, c % 2, :], ALU.mult).then_inc(gated, 1)

        for c in range(WC):
            dve.wait_ge(conv_hi, c + 1)
            dve.tensor_tensor(branch_lo[2][:, c, :], conv[:, c, :], branch_hi[2][:, c, :].bitcast(F32),
                              ALU.subtract).then_inc(conv_lo, 1)

        with dve.Fori(0, 2) as i:
            base = steps[0]
            steps[1:] = 4, i
            for r in range(2):
                u = U_MERGE + 9 * r
                for k in range(9):
                    cast_lo(u + k + 2, 18, i)
                    if k < 6:
                        continue
                    n = k - 6
                    if n == 2:
                        dve.wait_ge(dve_step, step(0))
                    for d in range(2):
                        name = ("branch", r, d, n)
                        dve.wait_ge(*filled(name, i))
                        dve.wait_ge(*drained(("gate", r, d, n), i))
                        out = merged[:, d, :] if n == 0 else part[:, d, :]
                        dve.tensor_tensor(out, gate[:, d, n, :], bank(name)[:], ALU.mult).then_inc(frees(name), 1)
                    for d in range(2):
                        dve.wait_ge(*drained(("branch", r, d, n), i))
                        if n == 1:
                            dve.tensor_tensor(merged[:, d, :], merged[:, d, :], part[:, d, :], ALU.add).then_inc(
                                dve_step, 1)
                            step()
                        if n == 2:
                            dve.tensor_tensor(merged[:, d, :], merged[:, d, :], part[:, d, :], ALU.add).then_inc(
                                merged_ready, 1)
                for d in range(2):
                    dve.wait_ge(merged_hi, i * 4 + (2 * r + d + 1))
                    chunk = bass.ds(i * 4 + (2 * r + d), 1)
                    dve.tensor_tensor(mT_lo[:, chunk, :].rearrange("p o n -> p (o n)"), merged[:, d, :],
                                      mT_hi[:, chunk, :].rearrange("p o n -> p (o n)").bitcast(F32),
                                      ALU.subtract).then_inc(merged_lo, 1)
            assert steps[0] - base == 4
        steps[:] = base + 8, 0, None

        for u in range(U_WO, U_MOE):
            cast_lo(u + 2)
            if u == U_WO + 2:
                dve.wait_ge(x0_reloaded, 16 * TT)
                dve.wait_ge(residual_loaded, 16 * 3)
                dve.scalar_tensor_tensor(out=b_o[:], in0=emb_b[:], scalar=ALPHA, in1=b_o[:], op0=ALU.mult,
                                         op1=ALU.add).then_inc(dve_step, 1)
                for t in range(TT):
                    dve.scalar_tensor_tensor(out=x1[:, t, :], in0=x1[:, t, :], scalar=ALPHA, in1=emb_g[:],
                                             op0=ALU.mult, op1=ALU.mult).then_inc(dve_step, 1)
                dve.wait_ge(dve_step, step(TT + 1))
                for t in range(TT):
                    dve.tensor_tensor(x1[:, t, :], x1[:, t, :], b_o[:], ALU.add).then_inc(dve_step, 1)
                step(TT)
            if u in (U_WO + 3, U_MOE - 1):
                n = (u - U_WO) // 4
                dve.wait_ge(dve_step, step(0))
                for t in range(TT):
                    name = ("mixed", n, t)
                    dve.wait_ge(*filled(name))
                    half = x1[:, t, n * 512:(n + 1) * 512]
                    dve.tensor_tensor(half, half, bank(name)[:], ALU.add).then_inc(frees(name), 1)
                    dve.wait_ge(*drained(name))
                    dve.bn_stats(stats[:, t, n, :], half).then_inc(dve_step, 1)
                    step()
                    if n:
                        dve.wait_ge(dve_step, step(0))
                        dve.bn_aggr(mv[:, t, :], stats[:, t, :, :].rearrange("p k s -> p (k s)")).then_inc(
                            dve_step, 1)
                        dve.wait_ge(dve_step, step())
                        dve.tensor_scalar(var_eps[:, t:t + 1], mv[:, t, 1:2], EPS, None, ALU.add).then_inc(
                            var_ready, 1)
        dve.wait_ge(late_loaded, 16 * 4)
        for t in range(TT):
            dve.wait_ge(normalised, t + 1)
            dve.tensor_tensor(x1[:, t, :], x1[:, t, :], ln1_g[:], ALU.mult).then_inc(scaled, 1)
            if t % 2:
                dve.wait_ge(scaled, t + 1)
                dve.tensor_tensor(x1[:, t, :], x1[:, t, :], ln1_b[:], ALU.add).then_inc(x1_ready[t], 1)

        def tt(out, a, b, op):
            dve.tensor_tensor(out, a, b, op).then_inc(dve_step, 1)
            dve.wait_ge(dve_step, step())

        def ranks(rank, ge, value):
            for d in range(1, 4):
                k = 4 - d
                tt(ge[..., 0:k], value[..., 0:k], value[..., d:4], ALU.is_ge)
                tt(rank[..., d:4], rank[..., d:4], ge[..., 0:k], ALU.add)
                tt(rank[..., 0:k], rank[..., 0:k], ge[..., 0:k], ALU.subtract)

        def per_tile(row16):
            return row16.rearrange("p (g e) -> p g e", g=4).unsqueeze(1).to_broadcast([P, TT, 4, 4])

        dve.memset(r_sel[:, TT, :, :], 0.0).then_inc(dve_step, 1)
        dve.tensor_copy(r_rank[:], per_tile(const[:, C_HIGHER:C_HIGHER + EXPERTS])).then_inc(dve_step, 1)
        dve.tensor_copy(g_rank[:], const[:, C_HIGHER:C_HIGHER + 4].unsqueeze(1).to_broadcast([P, TT, 4])).then_inc(
            dve_step, 1)
        dve.wait_ge(dve_step, step(3))
        dve.wait_ge(*filled("r_s"))
        dve.tensor_copy(r_s[:].rearrange("p t g e -> p (t g e)"), bank("r_s")[:, 0:TT * EXPERTS]).then_inc(
            frees("r_s"), 1)
        dve.wait_ge(*drained("r_s"))
        tt(r_sb[:], r_s[:], per_tile(b_router[:]), ALU.add)
        ranks(r_rank[:], r_ge[:], r_sb[:])
        sel = r_sel[:, 0:TT]
        dve.tensor_scalar(sel, r_rank[:], 2.0, None, ALU.is_lt).then_inc(dve_step, 1)
        dve.wait_ge(dve_step, step())
        tt(r_tmp[:], r_sb[:], sel, ALU.mult)
        dve.tensor_reduce(g_sum[:], r_tmp[:], AX.X, ALU.add).then_inc(dve_step, 1)
        dve.wait_ge(dve_step, step())
        ranks(g_rank[:], g_ge[:], g_sum[:])
        dve.tensor_scalar(g_rank[:], g_rank[:], 1.0, None, ALU.is_lt).then_inc(dve_step, 1)
        dve.wait_ge(dve_step, step())
        dve.tensor_tensor(sel, sel, g_rank[:].unsqueeze(3).to_broadcast([P, TT, 4, 4]),
                          ALU.mult).then_inc(selected, 1)
        dve.wait_ge(selected, 1)
        tt(r_tmp[:], r_s[:], sel, ALU.mult)
        dve.tensor_reduce(w_sum[:], r_tmp[:].rearrange("p t g e -> p t (g e)"), AX.X, ALU.add).then_inc(dve_step, 1)
        dve.wait_ge(dve_step, step())
        dve.reciprocal(w_inv[:], w_sum[:]).then_inc(dve_step, 1)
        dve.memset(r_kth[..., 0:1], 0.0).then_inc(dve_step, 1)
        dve.tensor_copy(r_kth[..., 1:2], sel[..., 0:1]).then_inc(dve_step, 1)
        dve.wait_ge(dve_step, step(3))
        tt(r_kth[..., 2:3], r_kth[..., 1:2], sel[..., 1:2], ALU.add)
        tt(r_kth[..., 3:4], r_kth[..., 2:3], sel[..., 2:3], ALU.add)
        by_expert = [TT, EXPERTS]
        flat_kth = r_kth[:].rearrange("p t g e -> p t (g e)")
        tokens = token.unsqueeze(2).to_broadcast([P] + by_expert)
        dve.tensor_copy(info[..., 0], tokens).then_inc(dve_step, 1)
        dve.memset(info[..., 3], 0.0).then_inc(dve_step, 1)
        dve.tensor_tensor(info[..., 2], r_tmp[:].rearrange("p t g e -> p t (g e)"),
                          w_inv[:].unsqueeze(2).to_broadcast([P] + by_expert), ALU.mult).then_inc(dve_step, 1)
        dve.tensor_scalar(info[..., 1], flat_kth, float(T), 1.0, ALU.mult, ALU.add).then_inc(dve_step, 1)
        dve.wait_ge(dve_step, step(4))
        tt(info[..., 1], info[..., 1], tokens, ALU.add)
        dve.wait_ge(*filled("position"))
        flat_sel = sel.rearrange("p t g e -> p t (g e)")
        dve.tensor_reduce(most[:], bank("position")[:, 64:80], AX.X, ALU.max).then_inc(dve_step, 1)
        dve.scalar_tensor_tensor(out=position[:], in0=bank("position")[:, 0:64].rearrange("p (t e) -> p t e", t=TT),
                                 scalar=1.0, in1=flat_sel, op0=ALU.add, op1=ALU.mult).then_inc(frees("position"), 1)
        dve.wait_ge(dve_step, step())
        dve.wait_ge(*drained("position"))
        dve.tensor_scalar(overflow[:], most[:], float(SLOTS), None, ALU.is_gt).then_inc(flag_ready, 1)
        dve.tensor_scalar(position[:], position[:], -1.0, None, ALU.add).then_inc(routed, 1)
        dve.wait_ge(routed, 1)

        def make_onehot(e, q, b=0):
            slot = position[:, :, e if isinstance(e, int) else bass.ds(e, 1)]
            slot = slot.unsqueeze(2) if isinstance(e, int) else slot
            dve.scalar_tensor_tensor(out=onehot[:, q], in0=slot.to_broadcast([P, TT, SLOTS]), scalar=float(b * SLOTS),
                                     in1=iota.unsqueeze(1).to_broadcast([P, TT, SLOTS]),
                                     op0=ALU.subtract, op1=ALU.is_equal).then_inc(onehot_ready, 1)

        def slot_tokens(n, q, gathers):
            dve.wait_ge(*m_filled(M_INFO, n))
            if gathers is not None:
                dve.wait_ge(gathered[q], gathers * 16)
            dve.tensor_copy(slot_token[:, q:q + 1], psum[M_INFO][:, 0:1]).then_inc(token_ready, 1)

        def slot_rows(n, q, scatters):
            dve.wait_ge(*m_filled(M_INFO, n))
            if scatters is not None:
                dve.wait_ge(y_stored[q], scatters * 16)
            dve.tensor_scalar(slot_none[:], psum[M_INFO][:, 1:2], 0.0, 65536.0, ALU.is_equal, ALU.mult).then_inc(
                dve_step, 1)
            dve.wait_ge(dve_step, step())
            dve.scalar_tensor_tensor(out=slot_row[:, q:q + 1], in0=slot_none[:], scalar=-1.0,
                                     in1=psum[M_INFO][:, 1:2], op0=ALU.add, op1=ALU.add)
            dve.tensor_copy(slot_gate[:, q:q + 1], psum[M_INFO][:, 2:3]).then_inc(psum_free[M_INFO], 1)

        def split_xg(n, q):
            for half in range(2):
                dve.wait_ge(xg_hi, n * 2 + (half + 1))
                part_of = (slice(None), q, slice(4 * half, 4 * half + 4))
                dve.tensor_tensor(xgT_lo[part_of], psum[M_XT + half][:].rearrange("p (c n) -> p c n", c=4),
                                  xgT_hi[part_of].bitcast(F32), ALU.subtract).then_inc(psum_free[M_XT + half], 1)

        def gate_h(unit, n):
            dve.wait_ge(unit_used, unit + 1)
            dve.wait_ge(*m_drained(M_H1, n))
            dve.tensor_tensor(h[:], h_silu[:], psum[M_H3][:], ALU.mult).then_inc(psum_free[M_H3], 1)

        def split_hT(n):
            dve.wait_ge(hT_hi_done, n + 1)
            dve.tensor_tensor(hT_lo[:].rearrange("p c n -> p (c n)"), psum[M_HT][:],
                              hT_hi[:].rearrange("p c n -> p (c n)").bitcast(F32),
                              ALU.subtract).then_inc(psum_free[M_HT], 1)

        make_onehot(0, 0)
        make_onehot(1, 1)
        slot_tokens(0, 0, None)
        slot_rows(0, 0, None)
        slot_tokens(1, 1, None)
        split_xg(0, 0)
        for k in range(4):
            cast_lo(U_MOE + k + 2)

        def pair(j, per=0, i=None):
            for q in range(2):
                n = nth(q, 2, i)
                for k in range(12):
                    cast_lo(j + 12 * q + k + 2, per, i)
                    if k == 1:
                        split_xg(n + 1, 1 - q)
                    if k == 3:
                        gate_h(nth(j + 12 * q + 3, per, i), n)
                    if k == 4:
                        slot_rows(n + 1, 1 - q, q or None if i is None else i + q)
                    if k == 5:
                        split_hT(n)
                    if k == 7:
                        make_onehot(n + 2, q)
                    if k == 9:
                        slot_tokens(n + 2, q, nth(1, 1, i))

        pair(U_MOE + 4)
        with dve.Fori(0, 6) as i:
            base = steps[0]
            steps[1:] = 2, i
            pair(U_MOE + 4, 24, i + 1)
            assert steps[0] - base == 2
        steps[:] = base + 12, 0, None
        for n in (14, 15):
            j = U_MOE + 4 + 12 * n
            for k in range(12 if n == 14 else 8):
                if j + k + 2 < U_OVER:
                    cast_lo(j + k + 2)
                if k == 1 and n == 14:
                    split_xg(15, 1)
                if k == 3:
                    gate_h(j + 3, n)
                if k == 4 and n == 14:
                    slot_rows(15, 1, 7)
                if k == (5 if n == 14 else 3):
                    split_hT(n)

        with dve.register("over_dve") as reg:
            dve.reg_load(reg, overflow[0:1, 0:1])
            with dve.If(dve.snap(reg) > 0):
                with dve.Fori(0, EXPERTS) as e:
                    base = steps[0]
                    steps[1:] = 3, e
                    for b in range(3):
                        n, j = e * 3 + (EXPERTS + b), U_OVER + 12 * b
                        make_onehot(e, 0, b + 1)
                        slot_tokens(n, 0, e * 3 + (EXPERTS // 2 + b))
                        slot_rows(n, 0, e * 3 + (EXPERTS // 2 + b))
                        split_xg(n, 0)
                        for k in range(8):
                            cast_lo(j + k, 36, e)
                        gate_h(nth(j + 7, 36, e), n)
                        split_hT(n)
                        for k in range(8, 12):
                            cast_lo(j + k, 36, e)
                    assert steps[0] - base == 3
                dve.nop()
            with dve.Else():
                dve.nop()

        dve.wait_ge(x1_scaled, TT)
        for t in range(TT + 2):
            if t < TT:
                row = x1[:, t, :]
                dve.wait_ge(y_loaded[t], 32)
                dve.tensor_tensor(row, row, y_in[:, t, 0, :], ALU.add).then_inc(final_step, 1)
                dve.wait_ge(final_step, 4 * t + 1)
                dve.tensor_tensor(row, row, y_in[:, t, 1, :], ALU.add).then_inc(y_summed, 1)
                dve.wait_ge(y_summed, t + 1)
                for k in range(2):
                    dve.bn_stats(stats[:, t, k, :], row[:, k * 512:(k + 1) * 512]).then_inc(final_step, 1)
                dve.wait_ge(final_step, 4 * t + 3)
                dve.bn_aggr(mv[:, t, :], stats[:, t, :, :].rearrange("p k s -> p (k s)")).then_inc(final_step, 1)
                dve.wait_ge(final_step, 4 * t + 4)
                dve.tensor_scalar(var_eps[:, t:t + 1], mv[:, t, 1:2], EPS, None, ALU.add).then_inc(var_ready, 1)
            if t >= 2:
                dve.wait_ge(scaled, TT + t - 1)
                dve.tensor_tensor(x1[:, t - 2, :], x1[:, t - 2, :], ln2_b[:], ALU.add).then_inc(out_ready, 1)

    @block.gpsimd
    def _(pool):
        pool.dma_start(rpb_dram, A["rpb"][0].rearrange("h r c -> (h r c)").partition_broadcast(QCOLS)).then_inc(
            rpb_copied, 16)
        pool.memset(minus_half[:], -0.5).then_inc(pool_step, 1)
        pool.memset(conv_in[:], 0.0).then_inc(halo_zero, 1)
        pool.wait_ge(pool_step, 1)

        def root(n, t):
            pool.wait_ge(var_ready, (0, 2 * TT, 3 * TT)[n] + t + 1)
            pool.tensor_tensor(rstd[:, t:t + 1], var_eps[:, t:t + 1], minus_half[:, t:t + 1], ALU.pow).then_inc(
                pool_step, 1)
            pool.wait_ge(pool_step, n * TT + t + 2)
            pool.tensor_scalar(mu_rstd[:, t:t + 1], mv[:, t, 0:1], rstd[:, t:t + 1], -1.0, ALU.mult,
                               ALU.mult).then_inc(rstd_ready, 1)

        for t in range(TT):
            root(0, t)
        pool.wait_ge(x0_stored, 16 * TT)
        pool.wait_ge(*filled("w_s"))
        b_in = A["b_in"][0]
        pool.dma_start(bv[:], b_in[2 * W:3 * W].partition_broadcast(P)).then_inc(early_loaded, 16)
        pool.dma_start(bvs[:], b_in[4 * W:5 * W].partition_broadcast(P)).then_inc(early_loaded, 16)
        pool.dma_start(sg_g[:], A["sg_ln_g"][0].partition_broadcast(P)).then_inc(early_loaded, 16)
        pool.dma_start(sg_b[:], A["sg_ln_b"][0].partition_broadcast(P)).then_inc(early_loaded, 16)
        pool.dma_start(b_s[:].rearrange("p g t -> p (g t)"),
                       A["b_s"][0].rearrange("g t -> (g t)").partition_broadcast(P)).then_inc(early_loaded, 16)
        for c in (WC - 1, WC - 2):
            for k in range(1, TAPS):
                if c == WC - 2 and k == 14:
                    pool.wait_ge(var_ready, 2 * TT)
                    pool.tensor_tensor(rstd[:], var_eps[:], minus_half[:], ALU.pow).then_inc(rstd_ready, 1)
                pool.wait_ge(product_ready, (WC - 1 - c) * TAPS + k + 1)
                if k > 1:
                    pool.wait_ge(pool_conv, added(c, k - 1))
                pool.tensor_tensor(conv[:, c, :], conv[:, c, :], products[c][:, k % 2, :], ALU.add).then_inc(
                    pool_conv, 1)

        pool.wait_ge(unit_used, U_WO - 3)
        for t in range(TT):
            pool.dma_start(x1[:, t, :], x0_dram[tokens_of(t), :]).then_inc(x0_reloaded, 16)
        pool.dma_start(b_o[:], A["b_o"][0].partition_broadcast(P)).then_inc(residual_loaded, 16)
        pool.dma_start(emb_g[:], A["emb_ln_g"].partition_broadcast(P)).then_inc(residual_loaded, 16)
        pool.wait_ge(unit_used, U_WO)
        pool.dma_start(emb_b[:], A["emb_ln_b"].partition_broadcast(P)).then_inc(residual_loaded, 16)
        pool.wait_ge(unit_used, U_WO + 3)
        for dst, a in ((ln1_g, A["ln1_g"][0]), (ln1_b, A["ln1_b"][0]), (b_router, A["b_router"])):
            pool.dma_start(dst[:], a.partition_broadcast(P)).then_inc(late_loaded, 16)
        pool.dma_start(w_router[:], A["w_router"].rearrange("(c p) e -> p c e", p=P)).then_inc(late_loaded, 16)
        for t in range(TT):
            root(1, t)
        for t in range(0, TT, 2):
            pool.wait_ge(scaled, t + 1)
            pool.tensor_tensor(x1[:, t, :], x1[:, t, :], ln1_b[:], ALU.add).then_inc(x1_ready[t], 1)

        def gather(n, q):
            pool.wait_ge(token_ready, n + 1)
            pool.sem_inc(pool_go, 1)
            pool.indirect_dma_start(out=xg[:, q, :], out_offset=None, in_=x1_dram,
                                    in_offset=bass.IndirectOffsetOnAxis(ap=slot_token[:, q:q + 1], axis=0)).then_inc(
                gathered[q], 16)

        def scatter(n, q):
            for half in range(2):
                pool.wait_ge(*m_drained(M_Y + half, n))
                pool.sem_inc(pool_go, 1)
            pool.wait_ge(*m_drained(M_INFO, n))
            pool.sem_inc(pool_go, 1)
            pool.indirect_dma_start(out=y_dram, out_offset=bass.IndirectOffsetOnAxis(ap=slot_row[:, q:q + 1], axis=0),
                                    in_=y[:, q, :], in_offset=None, bounds_check=2 * T - 1,
                                    oob_is_err=False).then_inc(y_stored[q], 16)

        pool.wait_ge(x1_stored, 16 * TT)
        gather(0, 0)
        gather(1, 1)
        with pool.Fori(0, 7) as i:
            for q in range(2):
                pool.wait_ge(*m_filled(M_XT + 1, i * 2 + q))
                pool.sem_inc(pool_go, 1)
                gather(i * 2 + (q + 2), q)
                scatter(i * 2 + q, q)
        for dst, a in ((ln2_g, "ln2_g"), (ln2_b, "ln2_b")):
            pool.dma_start(dst[:], A[a][0].partition_broadcast(P)).then_inc(ln2_loaded, 16)
        for t in range(TT):
            pool.tensor_scalar(x1[:, t, :], x1[:, t, :], ALPHA, None, ALU.mult).then_inc(x1_scaled, 1)
        scatter(14, 0)
        scatter(15, 1)
        pool.wait_ge(flag_ready, 1)
        with pool.register("over_pool") as reg:
            pool.reg_load(reg, overflow[0:1, 0:1])
            with pool.If(pool.snap(reg) > 0):
                with pool.Fori(0, EXPERTS) as e:
                    for b in range(3):
                        n = e * 3 + (EXPERTS + b)
                        gather(n, 0)
                        scatter(n, 0)
                pool.wait_ge(y_stored[0], 16 * (EXPERTS // 2 + 3 * EXPERTS))
            with pool.Else():
                pool.wait_ge(y_stored[0], 16 * EXPERTS // 2)
        pool.wait_ge(y_stored[1], 16 * EXPERTS // 2)
        pool.sem_inc(all_stored, 1)
        pool.wait_ge(ln2_loaded, 32)
        for t in range(TT + 1):
            if t < TT:
                root(2, t)
            if t:
                pool.wait_ge(normalised, TT + t)
                pool.tensor_tensor(x1[:, t - 1, :], x1[:, t - 1, :], ln2_g[:], ALU.mult).then_inc(scaled, 1)

    @block.tensor
    def _(pe):
        def open_bank(name, i=None):
            if banks.at[name][1]:
                pe.wait_ge(*empty(name, i))

        def turn(name, tile, n=4):
            open_bank(name)
            for k in range(n):
                o = pe.transpose(bank(name)[:, k * P:(k + 1) * P], tile(k), ident)
            o.then_inc(fills(name), 1)

        def three(out, hi_l, lo_l, hi_r, lo_r, start, stop):
            pe.matmul(out, hi_l, hi_r, start=start, stop=False)
            pe.matmul(out, hi_l, lo_r, start=False, stop=False)
            return pe.matmul(out, lo_l, hi_r, start=False, stop=stop)

        def features(j, outs, x_hi, x_lo, per=0, i=None, chunk_there=None):
            pe.wait_ge(lo_cast, nth(j + 1, per, i))
            hi, lo = unit_of(w_hi, j, len(outs) * P), unit_of(w_lo, j, len(outs) * P)
            chunks = UNIT // (len(outs) * P)
            for d, name in enumerate(outs):
                open_bank(name, i)
                cols = slice(d * P, (d + 1) * P)
                for c in range(chunks):
                    if chunk_there is not None:
                        pe.wait_ge(*chunk_there(c))
                    o = three(bank(name)[:], hi[:, c, cols], lo[:, c, cols], x_hi[:, c, :], x_lo[:, c, :],
                              c == 0, c == chunks - 1)
            o.then_inc(unit_used, 1)

        def tokens(j, k, last, outs, x_hi, x_lo, choose, per=0, i=None):
            pe.wait_ge(lo_cast, nth(j + 1, per, i))
            hi, lo = unit_of(w_hi, j, 512), unit_of(w_lo, j, 512)
            for t, out in enumerate(outs):
                for c in range(2):
                    o = three(out, choose(x_hi[:, 2 * k + c, :], t), choose(x_lo[:, 2 * k + c, :], t), hi[:, c, :],
                              lo[:, c, :], k == 0 and c == 0, last and c == 1)
            o.then_inc(unit_used, 1)

        def scores(g):
            hp, seq = g // 2, g % 2
            open_bank(("scores", g))
            pe.wait_ge(*drained(("q", hp)))
            pe.wait_ge(*drained(("k", hp)))
            for h2 in range(2):
                rows = slice(64 * h2, 64 * h2 + 64)
                for j in range(4):
                    o = pe.matmul(bank(("scores", g))[rows, j * P:(j + 1) * P],
                                  qT[rows, hp, seq * SEQ + 64 * j:seq * SEQ + 64 * (j + 1)],
                                  grid(kT[rows, hp, :], seq, WINDOW[j], KCOLS), start=True, stop=True)
            o.then_inc(fills(("scores", g)), 1)

        def attend(g):
            hp, seq = g // 2, g % 2
            open_bank(("attended", g))
            pe.wait_ge(*drained(("probsT", g)))
            for j in range(4):
                o = pe.matmul(bank(("attended", g))[:, j * P:(j + 1) * P], v_win[:, seq, j, hp * P:(hp + 1) * P],
                              probsT[:, j * P:(j + 1) * P], start=True, stop=True)
            o.then_inc(fills(("attended", g)), 1)

        def in_row(x, t):
            return x[:, tokens_of(t)]

        pe.wait_ge(const_loaded, 16)
        pe.wait_ge(rows_loaded, 16 * 9)
        pe.transpose(bank("vectors")[:, 0:V_ALL], rows_v[0:V_ALL, :], ident[0:V_ALL, 0:V_ALL])
        pe.transpose(bank("vectors")[:, V_ALL:V_ALL + TAPS * WC], rows_c[0:TAPS * WC, :],
                     ident[0:TAPS * WC, 0:TAPS * WC]).then_inc(fills("vectors"), 1)
        for t in range(TT):
            pe.wait_ge(x0_normal, t + 1)
            for c in range(DC):
                name = ("x0T", c)
                if t == 0:
                    open_bank(name)
                o = pe.transpose(bank(name)[:, tokens_of(t)], x_in[:, t, c * P:(c + 1) * P], ident)
                if t == TT - 1:
                    o.then_inc(fills(name), 1)
        turn("w_s", lambda k: w_s[:, k, :])

        for u in range(U_MERGE):
            if u < U_V:
                features(u, [("glu_g" if u % 2 else "glu_a", u // 2)], xT_hi, xT_lo,
                         chunk_there=(lambda c: drained(("x0T", c))) if u == 0 else None)
            elif u < U_VSG:
                if u == U_V:
                    for t in range(TT):
                        open_bank(("v", t))
                tokens(u, u - U_V, u == U_V + 3, [bank(("v", t))[:] for t in range(TT)], xT_hi, xT_lo, in_row)
            elif u < U_QK:
                if u == U_VSG:
                    for t in range(TT):
                        open_bank(("vsg", t))
                tokens(u, u - U_VSG, u == U_VSG + 3, [bank(("vsg", t))[:] for t in range(TT)], xT_hi, xT_lo, in_row)
            elif u < U_USG:
                features(u, [("k" if u % 2 else "q", (u - U_QK) // 2)], xT_hi, xT_lo)
            else:
                c = u - U_USG
                features(u, [("usg", c)], xT_hi, xT_lo)
            if 18 <= u < 26:
                scores(u - 18)
            if u >= U_USG:
                c = u - U_USG
                open_bank(("spatial", c))
                pe.wait_ge(vs_ready, TT)
                pe.wait_ge(*drained("w_s"))
                for t in range(TT):
                    o = pe.matmul(bank(("spatial", c))[:, tokens_of(t)], vs[:, t, c * P:(c + 1) * P], w_sT[:, c, :],
                                  start=True, stop=True)
                o.then_inc(fills(("spatial", c)), 1)
            if 20 <= u < 28:
                if u == 20:
                    pe.wait_ge(v_windows, 16 * 8)
                attend(u - 20)
            if 19 <= u < 27:
                g = u - 19
                pe.wait_ge(probs_ready, g + 1)
                turn(("probsT", g), lambda k: probs[:, g % 2, k * P:(k + 1) * P])
            if u == 24:
                pe.wait_ge(conv_ready, WC - 2)
                pe.wait_ge(pool_conv, added(WC - 2, TAPS - 1))
                open_bank("conv_mean")
                for c in range(WC):
                    o = pe.matmul(bank("conv_mean")[:], ones, conv[:, c, :], start=c == 0, stop=c == WC - 1)
                o.then_inc(fills("conv_mean"), 1)
            if u == 25:
                open_bank("conv_var")
                for c in range(WC):
                    pe.wait_ge(squared, c + 1)
                    o = pe.matmul(bank("conv_var")[:], ones, squares[c], start=c == 0, stop=c == WC - 1)
                o.then_inc(fills("conv_var"), 1)

        with pe.Fori(0, 2) as i:
            for r in range(2):
                u = U_MERGE + 9 * r
                for d in range(2):
                    for n in range(3):
                        features(u, [("gate", r, d, n)], xT_hi, xT_lo, 18, i)
                        u += 1
                for n in range(3):
                    if n == 0:
                        pe.wait_ge(*drained(("attended", 7)))
                    elif n == 1:
                        pe.wait_ge(gated_lo, WC)
                    else:
                        pe.wait_ge(conv_lo, WC)
                    features(u, [("branch", r, d, n) for d in range(2)], branch_hi[n], branch_lo[n], 18, i)
                    u += 1
        for n in range(2):
            for t in range(TT):
                open_bank(("mixed", n, t))
            for k in range(4):
                pe.wait_ge(merged_lo, 2 * k + 2)
                tokens(U_WO + 4 * n + k, k, k == 3, [bank(("mixed", n, t))[:] for t in range(TT)], mT_hi, mT_lo,
                       in_row)

        pe.wait_ge(late_loaded, 16 * 4)
        for t in range(TT + 1):
            if t < TT:
                pe.wait_ge(x1_ready[t], 1)
                for half in range(2):
                    turn(("x1T", t, half), lambda k: x1[:, t, (4 * half + k) * P:(4 * half + k + 1) * P])
            if t:
                for half in range(2):
                    pe.wait_ge(*drained(("x1T", t - 1, half)))
                for c in range(DC):
                    o = pe.matmul(bank("router")[0:EXPERTS, tokens_of(t - 1)], w_router[:, c, :],
                                  x1T[:, c, tokens_of(t - 1)], start=c == 0, stop=c == DC - 1)
        o.then_inc(fills("router"), 1)
        pe.wait_ge(*drained("router"))
        open_bank("r_s")
        for t in range(TT):
            o = pe.transpose(bank("r_s")[:, t * EXPERTS:(t + 1) * EXPERTS], scoresT[0:EXPERTS, tokens_of(t)],
                             ident[0:EXPERTS, 0:EXPERTS])
        o.then_inc(fills("r_s"), 1)
        pe.wait_ge(selected, 1)
        open_bank("position")
        sel = r_sel[:].rearrange("p t g e -> p (t g e)")
        pe.matmul(bank("position")[:, 0:80], before, sel, start=True, stop=False)
        for k in range(1, TT + 1):
            at = EXPERTS * k
            o = pe.matmul(bank("position")[:, at:80], ones, sel[:, 0:80 - at], start=False, stop=k == TT)
        o.then_inc(fills("position"), 1)

        def slots(n, e, q):
            pe.wait_ge(onehot_ready, n + 1)
            pe.wait_ge(*m_empty(M_INFO, n))
            for t in range(TT):
                row = info[:, t, e, :] if isinstance(e, int) else info[:, t, bass.ds(e, 1), :].rearrange(
                    "p e k -> p (e k)")
                o = pe.matmul(psum[M_INFO][:, 0:4], onehot[:, q, t, :], row, start=t == 0, stop=t == TT - 1)
            o.then_inc(psum_full[M_INFO], 1)

        def turn_xg(n, q, gathers):
            pe.wait_ge(gathered[q], gathers * 16 + 16)
            for half in range(2):
                pe.wait_ge(*m_empty(M_XT + half, n))
                for k in range(4):
                    c = 4 * half + k
                    o = pe.transpose(psum[M_XT + half][:, k * P:(k + 1) * P], xg[:, q, c * P:(c + 1) * P], ident)
                o.then_inc(psum_full[M_XT + half], 1)

        def hidden(b, n, q, j, k, per=0, i=None):
            if k == 0:
                pe.wait_ge(*m_empty(b, n))
                for half in range(2):
                    pe.wait_ge(*m_drained(M_XT + half, n))
            tokens(j, k, k == 3, [psum[b][:]], xgT_hi[:, q], xgT_lo[:, q], lambda x, t: x, per, i)

        def turn_h(n):
            pe.wait_ge(*m_empty(M_HT, n))
            pe.wait_ge(*m_drained(M_H3, n))
            for k in range(4):
                o = pe.transpose(psum[M_HT][:, k * P:(k + 1) * P], h[:, k * P:(k + 1) * P], ident)
            o.then_inc(psum_full[M_HT], 1)

        def output(n, j, k, per=0, i=None):
            if k == 0:
                pe.wait_ge(*m_drained(M_HT, n))
            if k % 2 == 0:
                pe.wait_ge(*m_empty(M_Y + k // 2, n))
            tokens(j, k % 2, k % 2 == 1, [psum[M_Y + k // 2][:]], hT_hi, hT_lo, lambda x, t: x, per, i)

        pe.wait_ge(routed, 1)
        slots(0, 0, 0)
        slots(1, 1, 1)
        turn_xg(0, 0, 0)
        for k in range(4):
            hidden(M_H1, 0, 0, U_MOE + k, k)
        with pe.Fori(0, 7) as i:
            for q in range(2):
                n, j = i * 2 + q, U_MOE + 4 + 12 * q
                for k in range(12):
                    if k < 4:
                        hidden(M_H3, n, q, j + k, k, 24, i)
                    elif k < 8:
                        hidden(M_H1, n + 1, 1 - q, j + k, k - 4, 24, i)
                    else:
                        output(n, j + k, k - 8, 24, i)
                    if k == 1:
                        turn_xg(n + 1, 1 - q, i + q)
                    if k == 5:
                        turn_h(n)
                    if k == 9:
                        slots(n + 2, n + 2, q)
        for n in (14, 15):
            j = U_MOE + 4 + 12 * n
            for k in range(4):
                hidden(M_H3, n, n % 2, j + k, k)
                if k == 1 and n == 14:
                    turn_xg(15, 1, 7)
            j += 4
            if n == 14:
                for k in range(4):
                    hidden(M_H1, 15, 1, j + k, k)
                    if k == 1:
                        turn_h(14)
                j += 4
            else:
                turn_h(15)
            for k in range(4):
                output(n, j + k, k)

        pe.wait_ge(flag_ready, 1)
        with pe.register("over_pe") as reg:
            pe.reg_load(reg, overflow[0:1, 0:1])
            with pe.If(pe.snap(reg) > 0):
                with pe.Fori(0, EXPERTS) as e:
                    for b in range(3):
                        n, j = e * 3 + (EXPERTS + b), U_OVER + 12 * b
                        slots(n, e, 0)
                        turn_xg(n, 0, e * 3 + (EXPERTS // 2 + b))
                        for k in range(4):
                            hidden(M_H1, n, 0, j + k, k, 36, e)
                        for k in range(4):
                            hidden(M_H3, n, 0, j + 4 + k, k, 36, e)
                        turn_h(n)
                        for k in range(4):
                            output(n, j + 8 + k, k, 36, e)
                pe.nop()
            with pe.Else():
                pe.nop()

    moe.close()
    ctx.close()


_INS = ["x_prompt", "x_sample", "emb_ln_g", "emb_ln_b", "w_in", "b_in", "w_gate", "b_gate", "rpb", "w_a_o",
        "sg_ln_g", "sg_ln_b", "w_s", "b_s", "w_b_o", "conv_w", "conv_b", "cv_ln_g", "cv_ln_b", "w_c_o", "w_o", "b_o",
        "ln1_g", "ln1_b", "w_router", "b_router", "w_e1", "w_e3", "w_e2", "ln2_g", "ln2_b"]


def constants():
    import numpy as np

    c = np.zeros((P, C_ALL), np.float32)
    p = np.arange(P)
    c[:, C_IDENT:C_IDENT + P] = np.eye(P)
    c[:, C_BEFORE:C_BEFORE + P] = p[:, None] < p[None, :]
    c[:, C_IOTA:C_IOTA + P] = p
    c[:, C_ONES:C_ONES + P] = 1
    c[:, C_TOKEN:C_TOKEN + TT] = p[:, None] + P * np.arange(TT)
    c[:, C_HIGHER:C_HIGHER + EXPERTS] = 3 - np.arange(EXPERTS) % 4
    for pat, j in ((0, 0), (1, 1), (2, 3)):
        query = QCOLS * j + p % QCOLS
        start = np.clip(query - QCOLS // 2, 0, GRID - QCOLS)
        key = WINDOW[j] + np.arange(KCOLS)
        inside = (key >= start[:, None]) & (key < start[:, None] + QCOLS)
        c[:, C_MASK + KCOLS * pat:C_MASK + KCOLS * (pat + 1)] = np.where(inside, 0, -1e30)
    return c


def kernel(**inputs):
    import numpy as _np
    import concourse.bacc as _bacc
    from concourse import mybir as _mybir
    from concourse.bass_utils import run_bass_kernel_spmd as _run

    nc = _bacc.Bacc("TRN2", target_bir_lowering=False, num_devices=1)
    arrays, args = {}, {}
    for name in _INS + ["consts"]:
        a = constants() if name == "consts" else _np.ascontiguousarray(inputs[name])
        arrays[f"in_{name}_dram"] = a
        args[name] = nc.dram_tensor(f"in_{name}_dram", a.shape, _mybir.dt.from_np(a.dtype), kind="ExternalInput").ap()
    outs = [nc.dram_tensor(f"out_{i}_dram", (1, SEQ, D), F32, kind="ExternalOutput").ap() for i in range(2)]
    encoder_layer(nc, args, *outs)
    r = _run(nc, [arrays], core_ids=[0])
    return tuple(r.results[0][f"out_{i}_dram"] for i in range(2))
```

```python
from contextlib import ExitStack

import concourse.bass as bass
from concourse import mybir

P = 128
F32 = mybir.dt.float32
F32R = mybir.dt.float32r
I32 = mybir.dt.int32
ALU = mybir.AluOpType
ACT = mybir.ActivationFunctionType
AX = mybir.AxisListType

D = 1024
DC = D // P
T = 512
TT = T // P
SEQ = 256
W = 512
WC = W // P
GRID = 64
ROWS = SEQ // GRID
QCOLS = 16
KCOLS = 32
WINDOW = (0, 8, 24, 32)
PATTERN = (0, 1, 1, 2)
SHIFT = (0, -8, -16)
TAPS = 31
HALO = TAPS // 2
EXPERTS = 16
SLOTS = 128
FF = 512
ALPHA = 2.0 ** 0.25
EPS = 1e-5
QSCALE = 64 ** -0.5

RAW = 6
MORE = 6
RING = RAW + 3 * MORE
SPLIT = 3
M_SPLIT = 4
M_AHEAD = M_SPLIT - 1
UNIT = 1024

C_IDENT, C_BEFORE, C_IOTA, C_ONES = 0, 128, 256, 384
C_TOKEN = 512
C_HIGHER = 516
C_MASK = 532
C_ALL = C_MASK + 3 * KCOLS

V_IN, V_GATE, V_CONVB, V_CVG, V_CVB, V_EMBG, V_EMBB, V_ALL = 0, 28, 52, 56, 60, 64, 72, 80

U_GLU, U_V, U_VSG, U_QK, U_USG = 0, 8, 12, 16, 24
U_MERGE = 28
U_WO = U_MERGE + 36
U_MOE = U_WO + 8
U_OVER = U_MOE + 12 * EXPERTS


class Banks:

    def __init__(self):
        self.used, self.full, self.at = [0] * 8, [0] * 8, {}

    def use(self, name, bank, unit=None):
        self.loop(1, 0, [(name, bank, unit)])

    def loop(self, times, units, uses):
        used, full = list(self.used), list(self.full)
        for name, bank, unit in uses:
            self.at[name] = [bank, used[bank], full[bank], unit, units]
            used[bank] += 1
            full[bank] += unit is None
        for name, bank, _ in uses:
            self.at[name] += [used[bank] - self.used[bank], full[bank] - self.full[bank]]
        self.used = [a + (b - a) * times for a, b in zip(self.used, used)]
        self.full = [a + (b - a) * times for a, b in zip(self.full, full)]


def plan_banks():
    b = Banks()
    b.use("vectors", 6)
    for c in range(DC):
        b.use(("x0T", c), c)
    b.use("w_s", 3)
    for c in range(WC):
        b.use(("glu_a", c), 4 + 2 * (c % 2), U_GLU + 2 * c)
        b.use(("glu_g", c), 5 + 2 * (c % 2), U_GLU + 2 * c + 1)
    for t in range(TT):
        b.use(("v", t), t, U_V + 3)
    for t in range(TT):
        b.use(("vsg", t), 4 + t, U_VSG + 3)
    for c in range(WC):
        b.use(("q", c), 4 + 2 * (c % 2), U_QK + 2 * c)
        b.use(("k", c), 5 + 2 * (c % 2), U_QK + 2 * c + 1)
    for g in range(8):
        b.use(("scores", g), g % 2)
        b.use(("probsT", g), 2)
        b.use(("attended", g), 3)
    for c in range(WC):
        b.use(("usg", c), 4 + c % 2, U_USG + c)
        b.use(("spatial", c), 6 + c % 2)
    b.use("conv_mean", 0)
    b.use("conv_var", 1)
    uses = []
    for r in range(2):
        for d in range(2):
            uses += [(("gate", r, d, n), 3 * d + n, U_MERGE + 9 * r + 3 * d + n) for n in range(3)]
        for n, bank in enumerate((6, 0, 2)):
            uses += [(("branch", r, d, n), bank + d, U_MERGE + 9 * r + 6 + n) for d in range(2)]
    b.loop(2, 18, uses)
    for n in range(2):
        for t in range(TT):
            b.use(("mixed", n, t), 4 * n + t, U_WO + 4 * n + 3 if n == 0 or t == TT - 1 else None)
    for t in range(TT):
        for h in range(2):
            b.use(("x1T", t, h), 2 * t + h)
    b.use("router", 0)
    b.use("r_s", 2)
    b.use("position", 1)
    return b


M_H1, M_H3, M_Y, M_XT, M_HT, M_INFO = 0, 1, 2, 4, 6, 7


def encoder_layer(nc, A, out_prompt, out_sample):
    banks = plan_banks()
    ctx = ExitStack()
    m_used, m_full = list(banks.used), list(banks.full)

    def sem(name):
        return ctx.enter_context(nc.semaphore(name))

    x0_dram = nc.dram_tensor("x0_scratch", (T, D), F32).ap()
    v_dram = nc.dram_tensor("v_scratch", (T, W), F32).ap()
    rpb_dram = nc.dram_tensor("rpb_scratch", (QCOLS, A["rpb"].shape[1] * A["rpb"].shape[2] * A["rpb"].shape[3]),
                              F32).ap()
    x1_dram = nc.dram_tensor("x1_scratch", (T, D), F32).ap()
    y_dram = nc.dram_tensor("y_scratch", (2 * T, D), F32).ap()

    def sb(stack, name, shape, dt=F32):
        return stack.enter_context(nc.sbuf_tensor(name, [P] + shape, dt))

    raw = sb(ctx, "raw", [RAW, UNIT])
    w_hi = sb(ctx, "w_hi", [SPLIT, UNIT], F32R)
    w_lo = sb(ctx, "w_lo", [SPLIT, UNIT], F32R)
    const = sb(ctx, "const", [C_ALL])
    vec = sb(ctx, "vec", [V_ALL])
    conv_col = sb(ctx, "conv_col", [TAPS, WC])
    stats = sb(ctx, "stats", [TT, 2, 6])
    mv = sb(ctx, "mv", [TT, 2])
    rstd = sb(ctx, "rstd", [TT])
    var_eps = sb(ctx, "var_eps", [TT])
    minus_half = sb(ctx, "minus_half", [TT])
    mu_rstd = sb(ctx, "mu_rstd", [TT])
    overflow = sb(ctx, "overflow", [1], I32)
    neg_max = sb(ctx, "neg_max", [2, 4])
    exp_sum = sb(ctx, "exp_sum", [2, 4])
    exp_inv = sb(ctx, "exp_inv", [2, 4])
    ident = const[:, C_IDENT:C_IDENT + P]
    before = const[:, C_BEFORE:C_BEFORE + P]
    iota = const[:, C_IOTA:C_IOTA + P]
    ones = const[:, C_ONES:C_ONES + P]
    token = const[:, C_TOKEN:C_TOKEN + TT]

    mix = ExitStack()
    xT_hi = sb(mix, "xT_hi", [DC, T], F32R)
    xT_lo = sb(mix, "xT_lo", [DC, T], F32R)
    branch_hi = [sb(mix, f"branch{n}_hi", [WC, T], F32R) for n in range(2)]
    branch_lo = [sb(mix, f"branch{n}_lo", [WC, T], F32R) for n in range(2)]
    conv_in = sb(mix, "conv_in", [WC, 2, SEQ + 2 * HALO])
    conv = sb(mix, "conv", [WC, T])
    early = ExitStack()
    qT = sb(early, "qT", [WC, T])
    kT = sb(early, "kT", [WC, T])
    v_win = sb(early, "v_win", [2, 4, W])
    bias = sb(early, "bias", [WC, 4, P])
    probs = sb(early, "probs", [2, W])
    probsT = sb(early, "probsT", [W])
    vs = sb(early, "vs", [TT, W])
    w_sT = sb(early, "w_sT", [4, P])
    b_s = sb(early, "b_s", [4, P])
    sg_g = sb(early, "sg_g", [W])
    sg_b = sb(early, "sg_b", [W])
    bv = sb(early, "bv", [W])
    bvs = sb(early, "bvs", [W])
    tmp = sb(early, "tmp", [2, W])
    conv_odd = sb(early, "conv_odd", [W])
    early.close()
    first = ExitStack()
    x_in = sb(first, "x_in", [TT, D])
    rows_v = sb(first, "rows_v", [P])
    rows_c = sb(first, "rows_c", [P])
    w_s = sb(first, "w_s_in", [4, P])
    first.close()
    late = ExitStack()
    mT_hi = sb(late, "mT_hi", [DC, T], F32R)
    mT_lo = sb(late, "mT_lo", [DC, T], F32R)
    branch_hi.append(sb(late, "branch2_hi", [WC, T], F32R))
    branch_lo.append(sb(late, "branch2_lo", [WC, T], F32R))
    gate = sb(late, "gate", [2, 3, T])
    part = sb(late, "part", [2, T])
    merged = sb(late, "merged", [2, T])
    late.close()
    mix.close()

    x1 = sb(ctx, "x1", [TT, D])
    residual = ExitStack()
    ln1_g = sb(residual, "ln1_g", [D])
    ln1_b = sb(residual, "ln1_b", [D])
    b_o = sb(residual, "b_o", [D])
    emb_g = sb(residual, "emb_g", [D])
    emb_b = sb(residual, "emb_b", [D])
    residual.close()
    moe = ExitStack()
    raw_rows = sb(moe, "raw_rows", [MORE, UNIT])
    ln2_g = sb(moe, "ln2_g", [D])
    ln2_b = sb(moe, "ln2_b", [D])
    tail = ExitStack()
    y_first = sb(tail, "y_first", [TT, D])
    y_second = sb(tail, "y_second", [TT, D])
    tail.close()
    raw_more = sb(moe, "raw_more", [MORE, UNIT])
    w_router = sb(moe, "w_router_in", [DC, EXPERTS])
    b_router = sb(moe, "b_router_in", [EXPERTS])
    scoresT = sb(moe, "scoresT", [T])
    r_s = sb(moe, "r_s", [TT, 4, 4])
    r_sb = sb(moe, "r_sb", [TT, 4, 4])
    r_ge = sb(moe, "r_ge", [TT, 4, 4])
    r_rank = sb(moe, "r_rank", [TT, 4, 4])
    r_sel = sb(moe, "r_sel", [TT + 1, 4, 4])
    r_tmp = sb(moe, "r_tmp", [TT, 4, 4])
    r_kth = sb(moe, "r_kth", [TT, 4, 4])
    g_sum = sb(moe, "g_sum", [TT, 4])
    g_ge = sb(moe, "g_ge", [TT, 4])
    g_rank = sb(moe, "g_rank", [TT, 4])
    w_sum = sb(moe, "w_sum", [TT])
    w_inv = sb(moe, "w_inv", [TT])
    position = sb(moe, "position", [TT, EXPERTS])
    info = sb(moe, "info", [TT, EXPERTS, 4])
    most = sb(moe, "most", [1])
    onehot = sb(moe, "onehot", [2, TT, SLOTS])
    slot_token = sb(moe, "slot_token", [2], I32)
    slot_row = sb(moe, "slot_row", [2], I32)
    slot_gate = sb(moe, "slot_gate", [2])
    slot_none = sb(moe, "slot_none", [1])
    slot_info = sb(moe, "slot_info", [2, 2])
    slot_kept = sb(moe, "slot_kept", [2, 2])
    w_hi_more = sb(moe, "w_hi_more", [M_SPLIT - SPLIT, UNIT], F32R)
    w_lo_more = sb(moe, "w_lo_more", [M_SPLIT - SPLIT, UNIT], F32R)
    xg = sb(moe, "xg", [2, D])
    routing = ExitStack()
    x1T = sb(routing, "x1T", [DC, T])
    routing.close()
    xgT_hi = sb(moe, "xgT_hi", [2, DC, SLOTS], F32R)
    xgT_lo = sb(moe, "xgT_lo", [2, DC, SLOTS], F32R)
    h_silu = sb(moe, "h_silu", [FF])
    h = sb(moe, "h", [FF])
    hT_hi = sb(moe, "hT_hi", [4, SLOTS], F32R)
    hT_lo = sb(moe, "hT_lo", [4, SLOTS], F32R)
    y = sb(moe, "y", [2, D])
    raw_late = sb(moe, "raw_late", [MORE, UNIT])
    psum = [ctx.enter_context(nc.psum_tensor(f"bank{b}", [P, 512], F32)) for b in range(8)]

    const_loaded = sem("const_loaded")
    rows_loaded = sem("rows_loaded")
    x_loaded = [sem(f"x_loaded{t}") for t in range(TT)]
    early_loaded = sem("early_loaded")
    rpb_copied = sem("rpb_copied")
    bias_loaded = sem("bias_loaded")
    raw_loaded = [sem(f"raw_loaded{s}") for s in range(RING)]
    hi_cast = sem("hi_cast")
    lo_cast = sem("lo_cast")
    unit_used = sem("unit_used")
    psum_full = [sem(f"psum_full{b}") for b in range(8)]
    psum_free = [sem(f"psum_free{b}") for b in range(8)]
    dve_step = sem("dve_step")
    pool_step = sem("pool_step")
    pool_go = sem("pool_go")
    halo_zero = sem("halo_zero")
    var_ready = sem("var_ready")
    rstd_ready = sem("rstd_ready")
    x0_normal = sem("x0_normal")
    x0T_full = sem("x0T_full")
    x0_stored = sem("x0_stored")
    x0T_hi_done = sem("x0T_hi_done")
    product_ready = sem("product_ready")
    pool_conv = sem("pool_conv")
    v_stored = sem("v_stored")
    v_windows = sem("v_windows")
    bias_ready = sem("bias_ready")
    max_ready = sem("max_ready")
    exp_done = sem("exp_done")
    probs_ready = sem("probs_ready")
    attn_hi = sem("attn_hi")
    vsg_gelu = sem("vsg_gelu")
    vs_ready = sem("vs_ready")
    gated = sem("gated")
    gated_hi = sem("gated_hi")
    gated_lo = sem("gated_lo")
    conv_ready = sem("conv_ready")
    centred = sem("centred")
    squared = sem("squared")
    conv_root = sem("conv_root")
    conv_scaled = sem("conv_scaled")
    conv_silu = sem("conv_silu")
    conv_hi = sem("conv_hi")
    conv_lo = sem("conv_lo")
    merged_ready = sem("merged_ready")
    merged_hi = sem("merged_hi")
    merged_lo = sem("merged_lo")
    x0_reloaded = sem("x0_reloaded")
    residual_loaded = sem("residual_loaded")
    late_loaded = sem("late_loaded")
    ln2_loaded = sem("ln2_loaded")
    x1_scaled = sem("x1_scaled")
    normalised = sem("normalised")
    scaled = sem("scaled")
    x1_ready = [sem(f"x1_ready{t}") for t in range(TT)]
    x1_stored = sem("x1_stored")
    scores_turned = sem("scores_turned")
    selected = sem("selected")
    routed = sem("routed")
    flag_ready = sem("flag_ready")
    onehot_ready = sem("onehot_ready")
    token_ready = sem("token_ready")
    rows_ready = sem("rows_ready")
    gathered = [sem(f"gathered{q}") for q in range(2)]
    xg_hi = sem("xg_hi")
    hT_hi_done = sem("hT_hi_done")
    y_stored = [sem(f"y_stored{q}") for q in range(2)]
    all_stored = sem("all_stored")
    lower_stored = sem("lower_stored")
    first_loaded = [sem(f"first_loaded{t}") for t in range(TT)]
    second_loaded = [sem(f"second_loaded{t}") for t in range(TT)]
    y_summed = sem("y_summed")
    final_step = sem("final_step")
    last_centred = sem("last_centred")
    out_ready = sem("out_ready")
    out_stored = sem("out_stored")

    def nth(j, per=0, i=None):
        return j if i is None or not per else i * per + j

    def bank(name):
        return psum[banks.at[name][0]]

    def filled(name, i=None):
        b, _, full, unit, units, _, more = banks.at[name]
        if unit is None:
            return psum_full[b], nth(full + 1, more, i)
        return unit_used, nth(unit + 1, units, i)

    def empty(name, i=None):
        b, used, _, _, _, more, _ = banks.at[name]
        return psum_free[b], nth(used, more, i)

    def drained(name, i=None):
        b, used, _, _, _, more, _ = banks.at[name]
        return psum_free[b], nth(used + 1, more, i)

    def frees(name):
        return psum_free[banks.at[name][0]]

    def fills(name):
        return psum_full[banks.at[name][0]]

    def ring_slot(j):
        return (j - U_MOE) % RING if j < U_OVER else (j - U_OVER) % (RING // 2)

    def raw_slot(j):
        if j < U_MOE:
            return raw[:, j % RAW, :]
        s = ring_slot(j)
        return (raw_more, raw, raw_late, raw_rows)[s // MORE][:, s % MORE, :]

    def raw_there(j, per=0, i=None):
        if j < U_MOE:
            return raw_loaded[j % RAW], nth(16 * (j // RAW + 1), 16 * per // RAW, i)
        s = ring_slot(j)
        before = U_MOE // RAW if s // MORE == 1 else 0
        if j < U_OVER:
            turn, ring = (j - U_MOE) // RING, RING
        else:
            turn, ring = (U_OVER - U_MOE) // RING + (j - U_OVER) // (RING // 2), RING // 2
        at = s % MORE if s // MORE == 1 else RAW + (s if s < MORE else s - RAW)
        return raw_loaded[at], nth(16 * (before + turn + 1), 16 * per // ring, i)

    def m_filled(b, n):
        return psum_full[b], n + (m_full[b] + 1)

    def m_empty(b, n):
        return psum_free[b], n + m_used[b]

    def m_drained(b, n):
        return psum_free[b], n + (m_used[b] + 1)

    def tokens_of(t):
        return slice(t * P, (t + 1) * P)

    def grid(row, seq, col, cols):
        return row[:, seq * SEQ:(seq + 1) * SEQ].rearrange("p (r c) -> p r c", c=GRID)[:, :, col:col + cols]

    products = {WC - 1: probs, WC - 2: tmp}

    def added(c, k):
        return k if c == WC - 1 else TAPS - 1 + k

    squares = (bvs[:], sg_g[:], sg_b[:], conv_odd[:])
    conv_vare, conv_rstd, conv_newton = bvs[:], sg_g[:], sg_b[:]

    def column(at):
        return vec[:, at:at + 1]

    def hi_slot(j):
        s = j % SPLIT if j < U_MOE else (j - U_MOE) % M_SPLIT
        return w_hi[:, s, :] if s < SPLIT else w_hi_more[:, s - SPLIT, :]

    def lo_slot(j):
        s = j % SPLIT if j < U_MOE else (j - U_MOE) % M_SPLIT
        return w_lo[:, s, :] if s < SPLIT else w_lo_more[:, s - SPLIT, :]

    def unit_of(slot, cols):
        return slot.rearrange("p (c n) -> p c n", n=cols)

    def attended_out(g, h2, rows):
        return bank(("attended", g))[rows, :].rearrange(
            "p (j q) -> p j q", j=4)[:, :, 64 * h2:64 * h2 + 64].rearrange("p j (r c) -> p j r c", r=ROWS)

    def attended_in(tile, g, rows):
        seq = g % 2
        return tile[rows, g // 2, seq * SEQ:(seq + 1) * SEQ].rearrange("p (r j c) -> p j r c", r=ROWS, j=4)

    w_in = A["w_in"][0].rearrange("(c p) n -> p c n", p=P)
    w_gate = A["w_gate"][0].rearrange("(c p) n -> p c n", p=P)
    w_branch = [A[n][0].rearrange("(c p) n -> p c n", p=P) for n in ("w_a_o", "w_b_o", "w_c_o")]
    w_o = A["w_o"][0].rearrange("(c p) n -> p c n", p=P)
    w_e1 = A["w_e1"][0].rearrange("e (c p) n -> p e c n", p=P)
    w_e3 = A["w_e3"][0].rearrange("e (c p) n -> p e c n", p=P)
    w_e2 = A["w_e2"][0].rearrange("e (c p) n -> p e c n", p=P)

    in_chunk = {}
    for c in range(WC):
        in_chunk |= {U_GLU + 2 * c: 20 + c, U_GLU + 2 * c + 1: 24 + c,
                     U_QK + 2 * c: c, U_QK + 2 * c + 1: 4 + c, U_USG + c: 12 + c}

    block = ctx.enter_context(nc.Block())

    @block.sync
    def _(sp):
        def load(j, source, n, per=0, i=None):
            if RAW <= j < U_MOE:
                sp.wait_ge(lo_cast, nth(j - RAW + 1, per, i))
            if U_MOE + MORE <= j < U_MOE + 2 * MORE or j >= U_OVER:
                sp.wait_ge(lo_cast, nth(j - RAW - MORE + 1, per, i))
            elif j >= U_MOE + RING:
                sp.wait_ge(lo_cast, nth(j - RING + 1, per, i))
            elif j == U_MOE:
                sp.wait_ge(unit_used, U_WO)
            elif j == U_MOE + 2 * MORE:
                sp.wait_ge(unit_used, U_WO + 4)
            elif j == U_MOE + 3 * MORE:
                for t in range(TT):
                    sp.wait_ge(x1_ready[t], 1)
                    sp.dma_start(x1_dram[tokens_of(t), :], x1[:, t, :]).then_inc(x1_stored, 16)
            sp.dma_start(raw_slot(j).rearrange("p (c n) -> p c n", n=n), source).then_inc(
                raw_there(j)[0], 16)

        for t in range(TT):
            x = (A["x_prompt"], A["x_sample"])[t // 2][0]
            sp.dma_start(x_in[:, t, :], x[tokens_of(t % 2), :]).then_inc(x_loaded[t], 16)
        copy, heads, table_row = rpb_dram.shape[1], A["rpb"].shape[2] * A["rpb"].shape[3], A["rpb"].shape[3]

        def load_bias(h2, hp, qr):
            for pat, j in ((0, 0), (1, 1), (2, 3)):
                at = (2 * hp + h2) * heads + (7 - qr) * table_row + 15 + SHIFT[pat]
                source = bass.AP(tensor=rpb_dram.tensor, offset=rpb_dram.offset + at,
                                 ap=[[copy - 1, QCOLS], [table_row, ROWS], [1, KCOLS]])
                rows = slice(64 * h2 + QCOLS * qr, 64 * h2 + QCOLS * (qr + 1))
                sp.dma_start(bias[rows, hp, j, :].rearrange("p (r c) -> p r c", r=ROWS), source).then_inc(
                    bias_loaded, 16)

        sp.wait_ge(rows_loaded, 16 * 9)
        for u in range(U_MERGE):
            if u == 6:
                for t in range(TT):
                    sp.wait_ge(x0_normal, t + 1)
                    sp.dma_start(x0_dram[tokens_of(t), :], x_in[:, t, :]).then_inc(x0_stored, 16)
                sp.wait_ge(x0_stored, 16 * TT)
                sp.wait_ge(*drained("w_s"))
                sp.wait_ge(rpb_copied, 16)
            if 6 <= u < 14:
                for qr in range(ROWS):
                    load_bias((u - 6) % 2, (u - 6) // 2, qr)
            if u == 17:
                for t in range(TT):
                    sp.wait_ge(*drained(("v", t)))
                    sp.dma_start(v_dram[tokens_of(t), :], vs[:, t, :]).then_inc(v_stored, 16)
            if u in (18, 19):
                seq = u - 18
                sp.wait_ge(v_stored, 16 * TT)
                v_grid = v_dram[seq * SEQ:(seq + 1) * SEQ, :].rearrange("(r c) n -> r c n", c=GRID)
                for j in range(4):
                    sp.dma_start(v_win[:, seq, j, :], v_grid[:, WINDOW[j]:WINDOW[j] + KCOLS, :]).then_inc(
                        v_windows, 16)
            if u in in_chunk:
                f = in_chunk[u]
                load(u, w_in[:, :, f * P:(f + 1) * P], P)
            else:
                k, col = (u - U_V, 1024) if u < U_VSG else (u - U_VSG, 2048)
                load(u, w_in[:, 2 * k:2 * k + 2, col:col + W], W)
        with sp.Fori(0, 2) as i:
            for r in range(2):
                u = U_MERGE + 9 * r
                for d in range(2):
                    for n in range(3):
                        load(u, w_gate[:, :, bass.ds(i * 512 + (n * D + (2 * r + d) * P), P)], P, 18, i)
                        u += 1
                for n in range(3):
                    load(u, w_branch[n][:, :, bass.ds(i * 512 + 2 * r * P, 2 * P)], 2 * P, 18, i)
                    u += 1
        for n in range(2):
            for k in range(4):
                load(U_WO + 4 * n + k, w_o[:, 2 * k:2 * k + 2, n * 512:(n + 1) * 512], 512)

        def load_expert(kind, j, e, per=0, i=None):
            for k in range(4):
                if kind == 2:
                    source = w_e2[:, e, 2 * (k % 2):2 * (k % 2) + 2, (k // 2) * 512:(k // 2 + 1) * 512]
                else:
                    source = (w_e1 if kind == 1 else w_e3)[:, e, 2 * k:2 * k + 2, :]
                if i is not None:
                    source = source.rearrange("p e c n -> p (e c) n")
                load(j + k, source, 512, per, i)

        load_expert(1, U_MOE, 0)
        load_expert(3, U_MOE + 4, 0)
        load_expert(1, U_MOE + 8, 1)
        load_expert(2, U_MOE + 12, 0)
        load_expert(3, U_MOE + 16, 1)
        load_expert(1, U_MOE + 20, 2)
        with sp.Fori(0, 6) as i:
            for q in range(2):
                j = U_MOE + 24 + 12 * q
                load_expert(2, j, bass.ds(i * 2 + (q + 1), 1), 24, i)
                load_expert(3, j + 4, bass.ds(i * 2 + (q + 2), 1), 24, i)
                load_expert(1, j + 8, bass.ds(i * 2 + (q + 3), 1), 24, i)
        j = U_MOE + 24 + 12 * 12
        load_expert(2, j, 13)
        load_expert(3, j + 4, 14)
        load_expert(1, j + 8, 15)
        load_expert(2, j + 12, 14)
        load_expert(3, j + 16, 15)
        load_expert(2, j + 20, 15)

        def load_first():
            for t in range(TT):
                sp.dma_start(y_first[:, t, :], y_dram[tokens_of(t), :]).then_inc(first_loaded[t], 16)

        sp.wait_ge(flag_ready, 1)
        with sp.register("over_sp") as reg:
            sp.reg_load(reg, overflow[0:1, 0:1])
            with sp.If(sp.snap(reg) > 0):
                with sp.Fori(0, EXPERTS) as e:
                    for b in range(3):
                        j = U_OVER + 12 * b
                        load_expert(1, j, bass.ds(e, 1), 36, e)
                        load_expert(3, j + 4, bass.ds(e, 1), 36, e)
                        load_expert(2, j + 8, bass.ds(e, 1), 36, e)
                sp.wait_ge(all_stored, 1)
                load_first()
            with sp.Else():
                sp.wait_ge(lower_stored, 1)
                load_first()

        sp.wait_ge(all_stored, 1)
        for t in range(TT):
            sp.dma_start(y_second[:, t, :], y_dram[T + t * P:T + (t + 1) * P, :]).then_inc(second_loaded[t], 16)
        for t in range(TT):
            sp.wait_ge(out_ready, t + 1)
            o = (out_prompt, out_sample)[t // 2][0]
            sp.dma_start(o[tokens_of(t % 2), :], x1[:, t, :]).then_inc(out_stored, 16)
        sp.wait_ge(out_stored, 16 * TT)

    @block.scalar
    def _(act):
        act.dma_start(const[:], A["consts"]).then_inc(const_loaded, 16)
        for at, n, a in ((V_IN, 28, "b_in"), (V_GATE, 24, "b_gate"), (V_CONVB, 4, "conv_b"),
                         (V_CVG, 4, "cv_ln_g"), (V_CVB, 4, "cv_ln_b")):
            act.dma_start(rows_v[at:at + n, :], A[a][0].rearrange("(r c) -> r c", c=P)).then_inc(rows_loaded, 16)
        for at, a in ((V_EMBG, "emb_ln_g"), (V_EMBB, "emb_ln_b")):
            act.dma_start(rows_v[at:at + DC, :], A[a].rearrange("(r c) -> r c", c=P)).then_inc(rows_loaded, 16)
        act.dma_start(rows_c[0:TAPS * WC, :], A["conv_w"][0].rearrange("t (c p) -> (t c) p", p=P)).then_inc(
            rows_loaded, 16)
        act.dma_start(w_s[:], A["w_s"][0].rearrange("g t s -> t g s")).then_inc(rows_loaded, 16)

        def cast_hi(j, per=0, i=None):
            act.wait_ge(*raw_there(j, per, i))
            if U_MOE <= j < U_MOE + M_SPLIT:
                act.wait_ge(unit_used, U_MOE)
            elif j >= U_MOE:
                act.wait_ge(unit_used, nth(j - M_SPLIT + 1, per, i))
            elif j >= SPLIT:
                act.wait_ge(unit_used, nth(j - SPLIT + 1, per, i))
            act.copy(hi_slot(j), raw_slot(j)).then_inc(hi_cast, 1)

        for t in range(TT):
            act.wait_ge(rstd_ready, t + 1)
            act.activation(x_in[:, t, :], x_in[:, t, :], ACT.Identity, scale=rstd[:, t:t + 1],
                           bias=mu_rstd[:, t:t + 1]).then_inc(x0_normal, 1)
        cast_hi(0)
        act.wait_ge(*drained("vectors"))
        for c in range(DC + 1):
            if c < DC:
                if c >= WC:
                    act.wait_ge(*drained(("x0T", c - WC)))
                act.wait_ge(*filled(("x0T", c)))
                act.activation(conv[:, c % WC, :], bank(("x0T", c))[:], ACT.Identity, scale=column(V_EMBG + c),
                               bias=column(V_EMBB + c)).then_inc(x0T_full, 1)
            if c:
                act.wait_ge(x0T_full, c)
                act.copy(xT_hi[:, c - 1, :], conv[:, (c - 1) % WC, :]).then_inc(x0T_hi_done, 1)
        cast_hi(1)
        act.wait_ge(*filled("w_s"))
        act.wait_ge(x0_stored, 16 * TT)

        def glu(c):
            if c:
                act.wait_ge(*drained(("glu_a", c - 1)))
            act.wait_ge(*filled(("glu_g", c)))
            act.activation(tmp[:, 0, :], bank(("glu_g", c))[:], ACT.Sigmoid,
                           bias=column(V_IN + 24 + c)).then_inc(frees(("glu_g", c)), 1)

        def keys(c):
            act.wait_ge(*filled(("k", c)))
            act.activation(kT[:, c, :], bank(("k", c))[:], ACT.Identity,
                           bias=column(V_IN + 4 + c)).then_inc(frees(("k", c)), 1)

        def queries(c):
            act.wait_ge(*filled(("q", c)))
            for s in range(2):
                tokens = slice(s * SEQ, (s + 1) * SEQ)
                o = act.activation(qT[:, c, tokens].rearrange("p (j r c) -> p r j c", j=4, r=ROWS),
                                   bank(("q", c))[:, tokens].rearrange("p (r j c) -> p r j c", j=4, r=ROWS),
                                   ACT.Identity, bias=column(V_IN + c))
            o.then_inc(frees(("q", c)), 1)

        def exp_rows(g):
            act.wait_ge(max_ready, g + 1)
            for j in range(4):
                key = probs[:, g % 2, j * P:(j + 1) * P]
                o = act.activation(key, key, ACT.Exp, bias=neg_max[:, g % 2, j:j + 1],
                                   accum_out=exp_sum[:, g % 2, j:j + 1])
            o.then_inc(exp_done, 1)

        def copy_probsT(g):
            act.wait_ge(*filled(("probsT", g)))
            if g:
                act.wait_ge(*filled(("attended", g - 1)))
            act.copy(probsT[:], bank(("probsT", g))[:]).then_inc(frees(("probsT", g)), 1)

        def split_attended(g):
            act.wait_ge(*filled(("attended", g)))
            for h2 in range(2):
                rows = slice(64 * h2, 64 * h2 + 64)
                o = act.copy(attended_in(branch_hi[0], g, rows), attended_out(g, h2, rows))
            o.then_inc(attn_hi, 1)

        def product(c, k):
            if k == 0:
                act.wait_ge(*drained(("glu_a", c)))
            if k >= 3:
                act.wait_ge(pool_conv, added(c, k - 2))
            out = (products[c][:, k % 2, :] if k else conv[:, c, :]).rearrange("p (s t) -> p s t", s=2)
            act.activation(out, conv_in[:, c, :, k:k + SEQ], ACT.Identity, scale=conv_col[:, k, c:c + 1],
                           bias=column(V_CONVB + c) if k == 0 else 0.0).then_inc(product_ready, 1)

        def gated_chunk_hi(c):
            act.wait_ge(gated, c + 1)
            act.copy(branch_hi[1][:, c, :], tmp[:, c % 2, :]).then_inc(gated_hi, 1)

        for u in range(U_MERGE + 1):
            if u < U_MERGE:
                cast_hi(u + 2)
            if 20 <= u < 28:
                copy_probsT(u - 20)
            if 21 <= u < 29:
                split_attended(u - 21)
            if u > U_USG:
                gated_chunk_hi(u - U_USG - 1)
            if u == 25:
                for c in range(WC):
                    act.wait_ge(centred, c + 1)
                    act.activation(squares[c], conv[:, c, :], ACT.Square).then_inc(squared, 1)
            if u == 26:
                act.wait_ge(*drained("conv_var"))
                act.activation(conv_rstd, conv_vare, ACT.Sqrt).then_inc(conv_root, 1)
            if u < U_V and u % 2:
                glu(u // 2)
            if 8 <= u < 16:
                for k in range(4 * (u - 8), min(TAPS, 4 * (u - 7))):
                    product(WC - 1, k)
            if 16 <= u < 24:
                for k in range(4 * (u - 16), min(TAPS, 4 * (u - 15))):
                    product(WC - 2, k)
            if U_QK <= u < U_USG:
                c = (u - U_QK) // 2
                keys(c) if u % 2 else queries(c)
            if 18 <= u < 26:
                exp_rows(u - 18)
            if u == U_VSG + 3:
                for t in range(TT):
                    act.wait_ge(*drained(("vsg", t)))
                    act.activation(vs[:, t, :], vs[:, t, :], ACT.Gelu_apprx_tanh).then_inc(vsg_gelu, 1)
            if U_USG <= u < U_MERGE:
                c = u - U_USG
                if c == 0:
                    act.wait_ge(pool_conv, added(WC - 2, TAPS - 1))
                if c >= 2:
                    act.wait_ge(gated_lo, c - 1)
                act.wait_ge(*filled(("usg", c)))
                act.activation(tmp[:, c % 2, :], bank(("usg", c))[:], ACT.Gelu_apprx_tanh,
                               bias=column(V_IN + 12 + c)).then_inc(frees(("usg", c)), 1)

        for c in range(WC):
            act.wait_ge(conv_scaled, c + 1)
            act.activation(conv[:, c, :], conv[:, c, :], ACT.Silu, bias=column(V_CVB + c),
                           scale=column(V_CVG + c)).then_inc(conv_silu, 1)
        for c in range(WC):
            act.wait_ge(conv_silu, c + 1)
            act.copy(branch_hi[2][:, c, :], conv[:, c, :]).then_inc(conv_hi, 1)

        with act.Fori(0, 2) as i:
            for r in range(2):
                u = U_MERGE + 9 * r
                for d in range(2):
                    for n in range(3):
                        cast_hi(u + 2, 18, i)
                        name = ("gate", r, d, n)
                        if r:
                            act.wait_ge(*drained(("branch", r - 1, d, n), i))
                        else:
                            act.wait_ge(*drained(("branch", 1, d, n), i - 1))
                        act.wait_ge(*filled(name, i))
                        act.activation(gate[:, d, n, :], bank(name)[:], ACT.Sigmoid,
                                       bias=vec[:, bass.ds(i * 4 + (V_GATE + n * DC + 2 * r + d), 1)]).then_inc(
                            frees(name), 1)
                        u += 1
                for n in range(3):
                    cast_hi(u + 2, 18, i)
                    u += 1
                for d in range(2):
                    act.wait_ge(merged_ready, i * 4 + (2 * r + d + 1))
                    act.copy(mT_hi[:, bass.ds(i * 4 + (2 * r + d), 1), :].rearrange("p o n -> p (o n)"),
                             merged[:, d, :]).then_inc(merged_hi, 1)
        for u in range(U_WO + 2, U_MOE):
            cast_hi(u)

        for t in range(TT):
            act.wait_ge(rstd_ready, 6 + t)
            act.activation(x1[:, t, :], x1[:, t, :], ACT.Identity, scale=rstd[:, t:t + 1],
                           bias=mu_rstd[:, t:t + 1]).then_inc(normalised, 1)
        for t in range(TT):
            for half in range(2):
                name = ("x1T", t, half)
                act.wait_ge(*filled(name))
                act.copy(x1T[:, 4 * half:4 * half + 4, tokens_of(t)],
                         bank(name)[:].rearrange("p (c n) -> p c n", c=4)).then_inc(frees(name), 1)
            cast_hi(U_MOE + t)
        act.wait_ge(*filled("router"))
        act.activation(scoresT[0:EXPERTS, :], bank("router")[0:EXPERTS, :], ACT.Sigmoid).then_inc(frees("router"), 1)

        def split_xg(n, q):
            for half in range(2):
                act.wait_ge(*m_filled(M_XT + half, n))
                act.copy(xgT_hi[:, q, 4 * half:4 * half + 4, :],
                         psum[M_XT + half][:].rearrange("p (c n) -> p c n", c=4)).then_inc(xg_hi, 1)

        def silu(unit, n, h_before=None):
            act.wait_ge(unit_used, unit + 1)
            if h_before is not None:
                act.wait_ge(*m_drained(M_H3, h_before))
            act.activation(h_silu[:], psum[M_H1][:], ACT.Silu).then_inc(psum_free[M_H1], 1)

        def split_hT(n):
            act.wait_ge(*m_filled(M_HT, n))
            act.copy(hT_hi[:].rearrange("p c n -> p (c n)"), psum[M_HT][:]).then_inc(hT_hi_done, 1)

        def scale_y(unit, n, q, half):
            act.wait_ge(unit_used, unit + 1)
            act.wait_ge(rows_ready, n + 1)
            act.activation(y[:, q, half * 512:(half + 1) * 512], psum[M_Y + half][:], ACT.Copy,
                           scale=slot_gate[:, q:q + 1]).then_inc(psum_free[M_Y + half], 1)

        def expert(n, q, j, per=0, i=None):
            for k in range(12):
                if j + k + M_AHEAD < U_OVER:
                    cast_hi(j + k + M_AHEAD, per, i)
                if k == 1:
                    split_xg(n + 1, 1 - q)
                if k == 5:
                    split_hT(n)
                if k == 7:
                    silu(nth(j + 7, per, i), n + 1, n)
                if k == 9:
                    scale_y(nth(j + 9, per, i), n, q, 0)
                if k == 11:
                    scale_y(nth(j + 11, per, i), n, q, 1)

        split_xg(0, 0)
        for u in range(U_MOE + TT, U_MOE + 4 + M_AHEAD):
            cast_hi(u)
        silu(U_MOE + 3, 0)
        with act.Fori(0, 7) as i:
            for q in range(2):
                expert(i * 2 + q, q, U_MOE + 4 + 12 * q, 24, i)
        expert(14, 0, U_MOE + 4 + 12 * 14)
        j = U_MOE + 4 + 12 * 15
        for k in range(8):
            if j + k + M_AHEAD < U_OVER:
                cast_hi(j + k + M_AHEAD)
            if k == 3:
                split_hT(15)
            if k == 5:
                scale_y(j + 5, 15, 1, 0)
            if k == 7:
                scale_y(j + 7, 15, 1, 1)

        act.wait_ge(flag_ready, 1)
        with act.register("over_act") as reg:
            act.reg_load(reg, overflow[0:1, 0:1])
            with act.If(act.snap(reg) > 0):
                with act.Fori(0, EXPERTS) as e:
                    for b in range(3):
                        n, j = e * 3 + (EXPERTS + b), U_OVER + 12 * b
                        split_xg(n, 0)
                        for k in range(4):
                            cast_hi(j + k, 36, e)
                        silu(nth(j + 3, 36, e), n)
                        for k in range(4, 8):
                            cast_hi(j + k, 36, e)
                        split_hT(n)
                        for k in range(8, 12):
                            cast_hi(j + k, 36, e)
                            if k % 2:
                                scale_y(nth(j + k, 36, e), n, 0, (k - 8) // 2)
                act.nop()
            with act.Else():
                act.nop()

        for t in range(TT - 2):
            act.wait_ge(rstd_ready, 10 + t)
            act.activation(x1[:, t, :], x1[:, t, :], ACT.Identity, scale=rstd[:, t:t + 1],
                           bias=mu_rstd[:, t:t + 1]).then_inc(normalised, 1)

    @block.vector
    def _(dve):
        steps = [0, 0, None]

        def step(k=1):
            steps[0] += k
            return steps[0] if steps[2] is None else steps[2] * steps[1] + steps[0]

        def cast_lo(j, per=0, i=None):
            dve.wait_ge(hi_cast, nth(j + 1, per, i))
            dve.tensor_tensor(lo_slot(j), raw_slot(j), hi_slot(j).bitcast(F32),
                              ALU.subtract).then_inc(lo_cast, 1)

        def row_stats(x, t):
            halves = x.shape[-1] // 512
            for k in range(halves):
                dve.bn_stats(stats[:, t, k, :], x[:, k * 512:(k + 1) * 512]).then_inc(dve_step, 1)
            dve.wait_ge(dve_step, step(halves))
            dve.bn_aggr(mv[:, t, :], stats[:, t, 0:halves, :].rearrange("p k s -> p (k s)")).then_inc(dve_step, 1)
            dve.wait_ge(dve_step, step())
            return dve.tensor_scalar(var_eps[:, t:t + 1], mv[:, t, 1:2], EPS, None, ALU.add)

        def normalise(x, t, g, b):
            dve.tensor_scalar(x, x, mv[:, t, 0:1], rstd[:, t:t + 1], ALU.subtract, ALU.mult).then_inc(dve_step, 1)
            dve.wait_ge(dve_step, step())
            dve.tensor_tensor(x, x, g, ALU.mult).then_inc(dve_step, 1)
            dve.wait_ge(dve_step, step())
            return dve.tensor_tensor(x, x, b, ALU.add)

        for t in range(TT):
            dve.wait_ge(x_loaded[t], 16)
            row_stats(x_in[:, t, :], t).then_inc(var_ready, 1)
        dve.wait_ge(*filled("vectors"))
        dve.tensor_copy(conv_col[:].rearrange("p t c -> p (t c)"), bank("vectors")[:, V_ALL:V_ALL + TAPS * WC])
        dve.tensor_copy(vec[:], bank("vectors")[:, 0:V_ALL]).then_inc(frees("vectors"), 1)
        cast_lo(0)
        for c in range(DC):
            dve.wait_ge(x0T_hi_done, c + 1)
            dve.tensor_tensor(xT_lo[:, c, :], conv[:, c % WC, :], xT_hi[:, c, :].bitcast(F32),
                              ALU.subtract).then_inc(frees(("x0T", c)), 1)
        cast_lo(1)
        dve.wait_ge(*filled("w_s"))
        dve.wait_ge(x0_stored, 16 * TT)
        dve.tensor_copy(w_sT[:].rearrange("p g t -> p (g t)"), bank("w_s")[:]).then_inc(frees("w_s"), 1)
        dve.wait_ge(*drained("vectors"))

        last = {0: 0, 1: 0}

        conv_steps = (WC - 2) * (TAPS + 1)

        def convolve(start, end):
            for n in range(start, min(end, conv_steps)):
                c, k = divmod(n, TAPS + 1)
                shifted = None if k == TAPS else conv_in[:, c, :, k:k + SEQ]
                even = conv[:, c, :].rearrange("p (s t) -> p s t", s=2)
                odd = conv_odd[:].rearrange("p (s t) -> p s t", s=2)
                if k == 0:
                    dve.wait_ge(*drained(("glu_a", c)))
                    o = dve.tensor_scalar(even, shifted, conv_col[:, k, c:c + 1], column(V_CONVB + c),
                                          ALU.mult, ALU.add)
                elif k == TAPS:
                    dve.wait_ge(dve_step, steps[0])
                    dve.tensor_tensor(even, even, odd, ALU.add).then_inc(conv_ready, 1)
                    continue
                elif k == 1:
                    if c:
                        dve.wait_ge(conv_ready, c)
                    o = dve.tensor_scalar(odd, shifted, conv_col[:, k, c:c + 1], None, ALU.mult)
                else:
                    dve.wait_ge(dve_step, last[k % 2])
                    sum_ = odd if k % 2 else even
                    o = dve.scalar_tensor_tensor(out=sum_, in0=shifted, scalar=conv_col[:, k, c:c + 1], in1=sum_,
                                                 op0=ALU.mult, op1=ALU.add)
                o.then_inc(dve_step, 1)
                last[k % 2] = step()

        def glu(c):
            dve.wait_ge(*filled(("glu_a", c)))
            dve.wait_ge(*drained(("glu_g", c)))
            if c == 0:
                dve.wait_ge(halo_zero, 1)
            dve.scalar_tensor_tensor(
                out=conv_in[:, c, :, HALO:HALO + SEQ], in0=bank(("glu_a", c))[:].rearrange("p (s t) -> p s t", s=2),
                scalar=column(V_IN + 20 + c), in1=tmp[:, 0, :].rearrange("p (s t) -> p s t", s=2),
                op0=ALU.add, op1=ALU.mult).then_inc(frees(("glu_a", c)), 1)

        def mask_scores(g):
            dve.wait_ge(*filled(("scores", g)))
            if g == 0:
                dve.wait_ge(bias_ready, 4)
                dve.wait_ge(pool_conv, TAPS - 1)
            if g >= 2:
                dve.wait_ge(*filled(("probsT", g - 2)))
            row = probs[:, g % 2, :]
            dve.scalar_tensor_tensor(out=row, in0=bank(("scores", g))[:], scalar=QSCALE,
                                     in1=bias[:, g // 2, :, :].rearrange("p j k -> p (j k)"),
                                     op0=ALU.mult, op1=ALU.add).then_inc(frees(("scores", g)), 1)
            dve.wait_ge(*drained(("scores", g)))
            dve.tensor_reduce(neg_max[:, g % 2, :], row.rearrange("p (j k) -> p j k", j=4), AX.X,
                              ALU.max).then_inc(dve_step, 1)
            dve.wait_ge(dve_step, step())
            dve.tensor_scalar(neg_max[:, g % 2, :], neg_max[:, g % 2, :], -1.0, None, ALU.mult).then_inc(max_ready, 1)

        def divide_probs(g):
            dve.wait_ge(exp_done, g + 1)
            dve.reciprocal(exp_inv[:, g % 2, :], exp_sum[:, g % 2, :]).then_inc(dve_step, 1)
            dve.wait_ge(dve_step, step())
            row = probs[:, g % 2, :].rearrange("p (j k) -> p j k", j=4)
            dve.tensor_tensor(row, row, exp_inv[:, g % 2, :].unsqueeze(2).to_broadcast([P, 4, P]),
                              ALU.mult).then_inc(probs_ready, 1)

        def split_attended(g):
            dve.wait_ge(attn_hi, g + 1)
            for h2 in range(2):
                rows = slice(64 * h2, 64 * h2 + 64)
                o = dve.tensor_tensor(attended_in(branch_lo[0], g, rows), attended_out(g, h2, rows),
                                      attended_in(branch_hi[0], g, rows).bitcast(F32), ALU.subtract)
            o.then_inc(frees(("attended", g)), 1)

        def gated_chunk_lo(c):
            dve.wait_ge(gated_hi, c + 1)
            dve.tensor_tensor(branch_lo[1][:, c, :], tmp[:, c % 2, :], branch_hi[1][:, c, :].bitcast(F32),
                              ALU.subtract).then_inc(gated_lo, 1)

        for u in range(U_MERGE + 1):
            if u < U_MERGE:
                cast_lo(u + 2)
            if 19 <= u < 27:
                divide_probs(u - 19)
            if 21 <= u < 29:
                split_attended(u - 21)
            if u > U_USG:
                gated_chunk_lo(u - U_USG - 1)
            if u == 25:
                dve.wait_ge(*filled("conv_mean"))
                for c in range(WC):
                    dve.scalar_tensor_tensor(out=conv[:, c, :], in0=bank("conv_mean")[:], scalar=-1.0 / W,
                                             in1=conv[:, c, :], op0=ALU.mult, op1=ALU.add).then_inc(centred, 1)
                dve.wait_ge(centred, WC)
                dve.sem_inc(frees("conv_mean"), 1)
            if u == 26:
                dve.wait_ge(*filled("conv_var"))
                dve.tensor_scalar(conv_vare, bank("conv_var")[:], 1.0 / W, EPS, ALU.mult, ALU.add).then_inc(
                    frees("conv_var"), 1)
                dve.wait_ge(conv_root, 1)
                dve.reciprocal(conv_rstd, conv_rstd).then_inc(dve_step, 1)
                dve.wait_ge(dve_step, step())
                dve.scalar_tensor_tensor(out=conv_newton, in0=conv_rstd, scalar=-0.5, in1=conv_rstd, op0=ALU.mult,
                                         op1=ALU.mult).then_inc(dve_step, 1)
                dve.wait_ge(dve_step, step())
                dve.tensor_tensor(conv_newton, conv_newton, conv_vare, ALU.mult).then_inc(dve_step, 1)
                dve.wait_ge(dve_step, step())
                dve.scalar_tensor_tensor(out=conv_rstd, in0=conv_newton, scalar=1.5, in1=conv_rstd, op0=ALU.add,
                                         op1=ALU.mult).then_inc(dve_step, 1)
                dve.wait_ge(dve_step, step())
                for c in range(WC):
                    dve.tensor_tensor(conv[:, c, :], conv[:, c, :], conv_rstd, ALU.mult).then_inc(conv_scaled, 1)
            if u < U_V and u % 2:
                glu(u // 2)
            if u == 17:
                dve.wait_ge(bias_loaded, 16 * 12 * 8)
                for n, j in enumerate((0, 2, 1, 3)):
                    mask = const[:, C_MASK + KCOLS * PATTERN[j]:C_MASK + KCOLS * (PATTERN[j] + 1)]
                    if j == 1:
                        dve.wait_ge(bias_ready, n)
                    dve.tensor_tensor(bias[:, :, j, :].rearrange("p h (r c) -> p h r c", r=ROWS),
                                      bias[:, :, 1 if j == 2 else j, :].rearrange("p h (r c) -> p h r c", r=ROWS),
                                      mask.unsqueeze(1).unsqueeze(1).to_broadcast([P, WC, ROWS, KCOLS]),
                                      ALU.add).then_inc(bias_ready, 1)
            if u < U_V:
                convolve(5 * (u - 1) if u else 0, 5 * u)
            elif u < 16:
                convolve(35 + 4 * (u - 8), 35 + 4 * (u - 7))
            if 18 <= u < 26:
                mask_scores(u - 18)
            if u == U_V + 3:
                dve.wait_ge(early_loaded, 16 * 5)
                for t in range(TT):
                    dve.wait_ge(*filled(("v", t)))
                    dve.tensor_tensor(vs[:, t, :], bank(("v", t))[:], bv[:],
                                      ALU.add).then_inc(frees(("v", t)), 1)
            if u == U_VSG + 3:
                dve.wait_ge(v_stored, 16 * TT)
                for t in range(TT):
                    dve.wait_ge(*filled(("vsg", t)))
                    dve.tensor_tensor(vs[:, t, :], bank(("vsg", t))[:], bvs[:], ALU.add).then_inc(
                        frees(("vsg", t)), 1)
            if U_VSG + 4 <= u < U_VSG + 8:
                t = u - U_VSG - 4
                dve.wait_ge(vsg_gelu, t + 1)
                row_stats(vs[:, t, :], t).then_inc(var_ready, 1)
            if U_VSG + 8 <= u < U_VSG + 12:
                dve.wait_ge(rstd_ready, 5)
                normalise(vs[:, u - U_VSG - 8, :], u - U_VSG - 8, sg_g[:], sg_b[:]).then_inc(vs_ready, 1)
            if U_USG <= u < U_MERGE:
                c = u - U_USG
                dve.wait_ge(*filled(("spatial", c)))
                if c:
                    dve.wait_ge(gated, c)
                dve.tensor_tensor(bv[:].rearrange("p (t n) -> p t n", t=TT),
                                  bank(("spatial", c))[:].rearrange("p (t n) -> p t n", t=TT),
                                  b_s[:, c, :].unsqueeze(1).to_broadcast([P, TT, P]), ALU.add).then_inc(
                    frees(("spatial", c)), 1)
                dve.wait_ge(*drained(("spatial", c)))
                dve.wait_ge(*drained(("usg", c)))
                dve.tensor_tensor(tmp[:, c % 2, :], bv[:], tmp[:, c % 2, :], ALU.mult).then_inc(gated, 1)

        for c in range(WC):
            dve.wait_ge(conv_hi, c + 1)
            dve.tensor_tensor(branch_lo[2][:, c, :], conv[:, c, :], branch_hi[2][:, c, :].bitcast(F32),
                              ALU.subtract).then_inc(conv_lo, 1)

        with dve.Fori(0, 2) as i:
            base = steps[0]
            steps[1:] = 4, i
            for r in range(2):
                u = U_MERGE + 9 * r
                for k in range(9):
                    cast_lo(u + k + 2, 18, i)
                    if k < 6:
                        continue
                    n = k - 6
                    if n == 2:
                        dve.wait_ge(dve_step, step(0))
                    for d in range(2):
                        name = ("branch", r, d, n)
                        dve.wait_ge(*filled(name, i))
                        dve.wait_ge(*drained(("gate", r, d, n), i))
                        out = merged[:, d, :] if n == 0 else part[:, d, :]
                        dve.tensor_tensor(out, gate[:, d, n, :], bank(name)[:], ALU.mult).then_inc(frees(name), 1)
                    for d in range(2):
                        dve.wait_ge(*drained(("branch", r, d, n), i))
                        if n == 1:
                            dve.tensor_tensor(merged[:, d, :], merged[:, d, :], part[:, d, :], ALU.add).then_inc(
                                dve_step, 1)
                            step()
                        if n == 2:
                            dve.tensor_tensor(merged[:, d, :], merged[:, d, :], part[:, d, :], ALU.add).then_inc(
                                merged_ready, 1)
                for d in range(2):
                    dve.wait_ge(merged_hi, i * 4 + (2 * r + d + 1))
                    chunk = bass.ds(i * 4 + (2 * r + d), 1)
                    dve.tensor_tensor(mT_lo[:, chunk, :].rearrange("p o n -> p (o n)"), merged[:, d, :],
                                      mT_hi[:, chunk, :].rearrange("p o n -> p (o n)").bitcast(F32),
                                      ALU.subtract).then_inc(merged_lo, 1)
            assert steps[0] - base == 4
        steps[:] = base + 8, 0, None

        def add_mixed(n, t):
            name = ("mixed", n, t)
            dve.wait_ge(*filled(name))
            half = x1[:, t, n * 512:(n + 1) * 512]
            dve.tensor_tensor(half, half, bank(name)[:], ALU.add).then_inc(frees(name), 1)
            dve.wait_ge(*drained(name))
            dve.bn_stats(stats[:, t, n, :], half).then_inc(dve_step, 1)
            step()

        def scale_x1(t):
            dve.wait_ge(normalised, t + 1)
            dve.tensor_tensor(x1[:, t, :], x1[:, t, :], ln1_g[:], ALU.mult).then_inc(scaled, 1)
            if t % 2:
                dve.wait_ge(scaled, t + 1)
                dve.tensor_tensor(x1[:, t, :], x1[:, t, :], ln1_b[:], ALU.add).then_inc(x1_ready[t], 1)

        for u in range(U_WO + 2, U_MOE):
            cast_lo(u)
            if u == U_WO + 4:
                dve.wait_ge(x0_reloaded, 16 * TT)
                dve.wait_ge(residual_loaded, 16 * 3)
                dve.scalar_tensor_tensor(out=b_o[:], in0=emb_b[:], scalar=ALPHA, in1=b_o[:], op0=ALU.mult,
                                         op1=ALU.add).then_inc(dve_step, 1)
                for t in range(TT):
                    dve.scalar_tensor_tensor(out=x1[:, t, :], in0=x1[:, t, :], scalar=ALPHA, in1=emb_g[:],
                                             op0=ALU.mult, op1=ALU.mult).then_inc(dve_step, 1)
                step(TT + 1)
            if u == U_WO + 5:
                dve.wait_ge(dve_step, step(0))
                for t in range(TT):
                    dve.tensor_tensor(x1[:, t, :], x1[:, t, :], b_o[:], ALU.add).then_inc(dve_step, 1)
                dve.wait_ge(dve_step, step(TT))
        for t in range(TT):
            add_mixed(0, t)
        dve.wait_ge(late_loaded, 16 * 4)
        for t in range(TT):
            add_mixed(1, t)
            dve.wait_ge(dve_step, step(0))
            dve.bn_aggr(mv[:, t, :], stats[:, t, :, :].rearrange("p k s -> p (k s)")).then_inc(dve_step, 1)
            dve.wait_ge(dve_step, step())
            dve.tensor_scalar(var_eps[:, t:t + 1], mv[:, t, 1:2], EPS, None, ALU.add).then_inc(var_ready, 1)
            if t:
                scale_x1(t - 1)
        scale_x1(TT - 1)

        def tt(out, a, b, op):
            dve.tensor_tensor(out, a, b, op).then_inc(dve_step, 1)
            dve.wait_ge(dve_step, step())

        def ranks(rank, ge, value):
            for d in range(1, 4):
                k = 4 - d
                tt(ge[..., 0:k], value[..., 0:k], value[..., d:4], ALU.is_ge)
                tt(rank[..., d:4], rank[..., d:4], ge[..., 0:k], ALU.add)
                tt(rank[..., 0:k], rank[..., 0:k], ge[..., 0:k], ALU.subtract)

        def per_tile(row16):
            return row16.rearrange("p (g e) -> p g e", g=4).unsqueeze(1).to_broadcast([P, TT, 4, 4])

        for t in range(TT):
            cast_lo(U_MOE + t)
        dve.memset(r_sel[:, TT, :, :], 0.0).then_inc(dve_step, 1)
        dve.tensor_copy(r_rank[:], per_tile(const[:, C_HIGHER:C_HIGHER + EXPERTS])).then_inc(dve_step, 1)
        dve.tensor_copy(g_rank[:], const[:, C_HIGHER:C_HIGHER + 4].unsqueeze(1).to_broadcast([P, TT, 4])).then_inc(
            dve_step, 1)
        dve.wait_ge(dve_step, step(3))
        dve.wait_ge(*filled("r_s"))
        dve.tensor_copy(r_s[:].rearrange("p t g e -> p (t g e)"), bank("r_s")[:, 0:TT * EXPERTS]).then_inc(
            frees("r_s"), 1)
        dve.wait_ge(*drained("r_s"))
        tt(r_sb[:], r_s[:], per_tile(b_router[:]), ALU.add)
        ranks(r_rank[:], r_ge[:], r_sb[:])
        sel = r_sel[:, 0:TT]
        dve.tensor_scalar(sel, r_rank[:], 2.0, None, ALU.is_lt).then_inc(dve_step, 1)
        dve.wait_ge(dve_step, step())
        tt(r_tmp[:], r_sb[:], sel, ALU.mult)
        dve.tensor_reduce(g_sum[:], r_tmp[:], AX.X, ALU.add).then_inc(dve_step, 1)
        dve.wait_ge(dve_step, step())
        ranks(g_rank[:], g_ge[:], g_sum[:])
        dve.tensor_scalar(g_rank[:], g_rank[:], 1.0, None, ALU.is_lt).then_inc(dve_step, 1)
        dve.wait_ge(dve_step, step())
        dve.tensor_tensor(sel, sel, g_rank[:].unsqueeze(3).to_broadcast([P, TT, 4, 4]),
                          ALU.mult).then_inc(selected, 1)
        dve.wait_ge(selected, 1)
        tt(r_tmp[:], r_s[:], sel, ALU.mult)
        dve.tensor_reduce(w_sum[:], r_tmp[:].rearrange("p t g e -> p t (g e)"), AX.X, ALU.add).then_inc(dve_step, 1)
        dve.wait_ge(dve_step, step())
        dve.reciprocal(w_inv[:], w_sum[:]).then_inc(dve_step, 1)
        dve.memset(r_kth[..., 0:1], 0.0).then_inc(dve_step, 1)
        dve.tensor_copy(r_kth[..., 1:2], sel[..., 0:1]).then_inc(dve_step, 1)
        dve.wait_ge(dve_step, step(3))
        tt(r_kth[..., 2:3], r_kth[..., 1:2], sel[..., 1:2], ALU.add)
        tt(r_kth[..., 3:4], r_kth[..., 2:3], sel[..., 2:3], ALU.add)
        by_expert = [TT, EXPERTS]
        flat_kth = r_kth[:].rearrange("p t g e -> p t (g e)")
        tokens = token.unsqueeze(2).to_broadcast([P] + by_expert)
        dve.tensor_copy(info[..., 0], tokens).then_inc(dve_step, 1)
        dve.memset(info[..., 3], 0.0).then_inc(dve_step, 1)
        dve.tensor_tensor(info[..., 2], r_tmp[:].rearrange("p t g e -> p t (g e)"),
                          w_inv[:].unsqueeze(2).to_broadcast([P] + by_expert), ALU.mult).then_inc(dve_step, 1)
        dve.tensor_scalar(info[..., 1], flat_kth, float(T), 1.0, ALU.mult, ALU.add).then_inc(dve_step, 1)
        dve.wait_ge(dve_step, step(4))
        tt(info[..., 1], info[..., 1], tokens, ALU.add)
        dve.wait_ge(*filled("position"))
        flat_sel = sel.rearrange("p t g e -> p t (g e)")
        dve.tensor_reduce(most[:], bank("position")[:, 64:80], AX.X, ALU.max).then_inc(dve_step, 1)
        dve.scalar_tensor_tensor(out=position[:], in0=bank("position")[:, 0:64].rearrange("p (t e) -> p t e", t=TT),
                                 scalar=1.0, in1=flat_sel, op0=ALU.add, op1=ALU.mult).then_inc(frees("position"), 1)
        dve.wait_ge(dve_step, step())
        dve.wait_ge(*drained("position"))
        dve.tensor_scalar(overflow[:], most[:], float(SLOTS), None, ALU.is_gt).then_inc(flag_ready, 1)
        dve.tensor_scalar(position[:], position[:], -1.0, None, ALU.add).then_inc(routed, 1)
        dve.wait_ge(routed, 1)

        def make_onehot(e, q, b=0):
            slot = position[:, :, e if isinstance(e, int) else bass.ds(e, 1)]
            slot = slot.unsqueeze(2) if isinstance(e, int) else slot
            dve.scalar_tensor_tensor(out=onehot[:, q], in0=slot.to_broadcast([P, TT, SLOTS]), scalar=float(b * SLOTS),
                                     in1=iota.unsqueeze(1).to_broadcast([P, TT, SLOTS]),
                                     op0=ALU.subtract, op1=ALU.is_equal).then_inc(onehot_ready, 1)

        def slot_tokens(n, q, gathers, lists=None, keep=True):
            dve.wait_ge(*m_filled(M_INFO, n))
            if gathers is not None:
                dve.wait_ge(gathered[q], gathers * 16)
            if lists is not None:
                dve.wait_ge(rows_ready, lists)
            if keep:
                dve.tensor_copy(slot_kept[:, q, :], slot_info[:, q, :]).then_inc(dve_step, 1)
                dve.wait_ge(dve_step, step())
            dve.tensor_scalar(slot_none[:], psum[M_INFO][:, 1:2], 0.0, 65536.0, ALU.is_equal, ALU.mult).then_inc(
                dve_step, 1)
            dve.wait_ge(dve_step, step())
            dve.tensor_tensor(slot_token[:, q:q + 1], slot_none[:], psum[M_INFO][:, 0:1], ALU.add).then_inc(
                token_ready, 1)
            dve.scalar_tensor_tensor(out=slot_info[:, q, 0:1], in0=slot_none[:], scalar=-1.0,
                                     in1=psum[M_INFO][:, 1:2], op0=ALU.add, op1=ALU.add)
            dve.tensor_copy(slot_info[:, q, 1:2], psum[M_INFO][:, 2:3]).then_inc(psum_free[M_INFO], 1)

        def slot_rows(n, q, scatters, source):
            dve.wait_ge(*m_drained(M_INFO, n))
            if scatters is not None:
                dve.wait_ge(y_stored[q], scatters * 16)
            dve.tensor_copy(slot_row[:, q:q + 1], source[:, q, 0:1])
            dve.tensor_copy(slot_gate[:, q:q + 1], source[:, q, 1:2]).then_inc(rows_ready, 1)

        def split_xg(n, q):
            for half in range(2):
                dve.wait_ge(xg_hi, n * 2 + (half + 1))
                part_of = (slice(None), q, slice(4 * half, 4 * half + 4))
                dve.tensor_tensor(xgT_lo[part_of], psum[M_XT + half][:].rearrange("p (c n) -> p c n", c=4),
                                  xgT_hi[part_of].bitcast(F32), ALU.subtract).then_inc(psum_free[M_XT + half], 1)

        def gate_h(unit, n):
            dve.wait_ge(unit_used, unit + 1)
            dve.wait_ge(*m_drained(M_H1, n))
            dve.tensor_tensor(h[:], h_silu[:], psum[M_H3][:], ALU.mult).then_inc(psum_free[M_H3], 1)

        def split_hT(n):
            dve.wait_ge(hT_hi_done, n + 1)
            dve.tensor_tensor(hT_lo[:].rearrange("p c n -> p (c n)"), psum[M_HT][:],
                              hT_hi[:].rearrange("p c n -> p (c n)").bitcast(F32),
                              ALU.subtract).then_inc(psum_free[M_HT], 1)

        make_onehot(0, 0)
        make_onehot(1, 1)
        slot_tokens(0, 0, None, keep=False)
        slot_tokens(1, 1, None, keep=False)
        make_onehot(2, 0)
        split_xg(0, 0)
        for u in range(U_MOE + TT, U_MOE + 4 + M_AHEAD):
            cast_lo(u)
        slot_tokens(2, 0, 1)

        def expert(n, q, j, scatters, more=True, per=0, i=None):
            last = isinstance(n, int) and n == EXPERTS - 1
            for k in range(8 if last else 12):
                if j + k + M_AHEAD < U_OVER:
                    cast_lo(j + k + M_AHEAD, per, i)
                if k == 1 and not last:
                    split_xg(n + 1, 1 - q)
                if k == 3:
                    gate_h(nth(j + 3, per, i), n)
                    if last:
                        split_hT(n)
                if k == 5 and not last:
                    split_hT(n)
                if k == 7 and more:
                    make_onehot(n + 3, 1 - q)
                if k == (3 if last else 7):
                    kept = i is not None or n < EXPERTS - 2
                    slot_rows(n, q, scatters, slot_kept if kept else slot_info)
                if k == 10 and more:
                    slot_tokens(n + 3, 1 - q, nth(q + 1, 1, i) if i is not None else (n + 3) // 2,
                                None if scatters is None else n)

        expert(0, 0, U_MOE + 4, None)
        expert(1, 1, U_MOE + 16, None)
        with dve.Fori(0, 5) as i:
            base = steps[0]
            steps[1:] = 4, i
            for q in range(2):
                expert(i * 2 + (2 + q), q, U_MOE + 4 + 12 * q, i + 1, True, 24, i + 1)
            assert steps[0] - base == 4
        steps[:] = base + 20, 0, None
        for n in range(12, EXPERTS):
            expert(n, n % 2, U_MOE + 4 + 12 * n, n // 2, n == 12)

        with dve.register("over_dve") as reg:
            dve.reg_load(reg, overflow[0:1, 0:1])
            with dve.If(dve.snap(reg) > 0):
                with dve.Fori(0, EXPERTS) as e:
                    base = steps[0]
                    steps[1:] = 3, e
                    for b in range(3):
                        n, j = e * 3 + (EXPERTS + b), U_OVER + 12 * b
                        make_onehot(e, 0, b + 1)
                        slot_tokens(n, 0, e * 3 + (EXPERTS // 2 + b), n, False)
                        slot_rows(n, 0, e * 3 + (EXPERTS // 2 + b), slot_info)
                        split_xg(n, 0)
                        for k in range(8):
                            cast_lo(j + k, 36, e)
                        gate_h(nth(j + 7, 36, e), n)
                        split_hT(n)
                        for k in range(8, 12):
                            cast_lo(j + k, 36, e)
                    assert steps[0] - base == 3
                dve.nop()
            with dve.Else():
                dve.nop()

        dve.wait_ge(x1_scaled, TT)
        for t in range(TT):
            dve.wait_ge(first_loaded[t], 16)
            dve.tensor_tensor(x1[:, t, :], x1[:, t, :], y_first[:, t, :], ALU.add).then_inc(final_step, 1)
        for t in range(TT):
            row = x1[:, t, :]
            dve.wait_ge(second_loaded[t], 16)
            dve.wait_ge(final_step, max(t + 1, 3 * t + TT))
            dve.tensor_tensor(row, row, y_second[:, t, :], ALU.add).then_inc(y_summed, 1)
            dve.wait_ge(y_summed, t + 1)
            for k in range(2):
                dve.bn_stats(stats[:, t, k, :], row[:, k * 512:(k + 1) * 512]).then_inc(final_step, 1)
            dve.wait_ge(final_step, TT + 3 * t + 2)
            dve.bn_aggr(mv[:, t, :], stats[:, t, :, :].rearrange("p k s -> p (k s)")).then_inc(final_step, 1)
            dve.wait_ge(final_step, TT + 3 * t + 3)
            dve.tensor_scalar(var_eps[:, t:t + 1], mv[:, t, 1:2], EPS, None, ALU.add).then_inc(var_ready, 1)
            if t >= 2:
                dve.wait_ge(ln2_loaded, 32)
                dve.scalar_tensor_tensor(out=row, in0=row, scalar=mv[:, t, 0:1], in1=ln2_g[:], op0=ALU.subtract,
                                         op1=ALU.mult).then_inc(last_centred, 1)
                dve.wait_ge(scaled, TT + t - 1)
                dve.tensor_tensor(x1[:, t - 2, :], x1[:, t - 2, :], ln2_b[:], ALU.add).then_inc(out_ready, 1)
        for t in (TT - 2, TT - 1):
            dve.wait_ge(last_centred, t - TT + 3)
            dve.wait_ge(rstd_ready, 10 + t)
            dve.scalar_tensor_tensor(out=x1[:, t, :], in0=x1[:, t, :], scalar=rstd[:, t:t + 1], in1=ln2_b[:],
                                     op0=ALU.mult, op1=ALU.add).then_inc(out_ready, 1)

    @block.gpsimd
    def _(pool):
        pool.dma_start(rpb_dram, A["rpb"][0].rearrange("h r c -> (h r c)").partition_broadcast(QCOLS)).then_inc(
            rpb_copied, 16)
        pool.memset(minus_half[:], -0.5).then_inc(pool_step, 1)
        pool.memset(conv_in[:], 0.0).then_inc(halo_zero, 1)
        pool.wait_ge(pool_step, 1)

        def root(n, t):
            pool.wait_ge(var_ready, (0, 2 * TT, 3 * TT)[n] + t + 1)
            pool.tensor_tensor(rstd[:, t:t + 1], var_eps[:, t:t + 1], minus_half[:, t:t + 1], ALU.pow).then_inc(
                pool_step, 1)
            pool.wait_ge(pool_step, n * TT + t + (3 if n == 2 else 2))
            pool.tensor_scalar(mu_rstd[:, t:t + 1], mv[:, t, 0:1], rstd[:, t:t + 1], -1.0, ALU.mult,
                               ALU.mult).then_inc(rstd_ready, 1)

        for t in range(TT):
            root(0, t)
        pool.wait_ge(x0_stored, 16 * TT)
        pool.wait_ge(*filled("w_s"))
        b_in = A["b_in"][0]
        pool.dma_start(bv[:], b_in[2 * W:3 * W].partition_broadcast(P)).then_inc(early_loaded, 16)
        pool.dma_start(bvs[:], b_in[4 * W:5 * W].partition_broadcast(P)).then_inc(early_loaded, 16)
        pool.dma_start(sg_g[:], A["sg_ln_g"][0].partition_broadcast(P)).then_inc(early_loaded, 16)
        pool.dma_start(sg_b[:], A["sg_ln_b"][0].partition_broadcast(P)).then_inc(early_loaded, 16)
        pool.dma_start(b_s[:].rearrange("p g t -> p (g t)"),
                       A["b_s"][0].rearrange("g t -> (g t)").partition_broadcast(P)).then_inc(early_loaded, 16)
        for c in (WC - 1, WC - 2):
            for k in range(1, TAPS):
                if c == WC - 2 and k == 14:
                    pool.wait_ge(var_ready, 2 * TT)
                    pool.tensor_tensor(rstd[:], var_eps[:], minus_half[:], ALU.pow).then_inc(rstd_ready, 1)
                pool.wait_ge(product_ready, (WC - 1 - c) * TAPS + k + 1)
                if k > 1:
                    pool.wait_ge(pool_conv, added(c, k - 1))
                pool.tensor_tensor(conv[:, c, :], conv[:, c, :], products[c][:, k % 2, :], ALU.add).then_inc(
                    pool_conv, 1)

        pool.wait_ge(unit_used, U_WO - 3)
        for t in range(TT):
            pool.dma_start(x1[:, t, :], x0_dram[tokens_of(t), :]).then_inc(x0_reloaded, 16)
        pool.dma_start(b_o[:], A["b_o"][0].partition_broadcast(P)).then_inc(residual_loaded, 16)
        pool.dma_start(emb_g[:], A["emb_ln_g"].partition_broadcast(P)).then_inc(residual_loaded, 16)
        pool.wait_ge(unit_used, U_WO)
        pool.dma_start(emb_b[:], A["emb_ln_b"].partition_broadcast(P)).then_inc(residual_loaded, 16)
        pool.wait_ge(unit_used, U_WO + 3)
        for dst, a in ((ln1_g, A["ln1_g"][0]), (ln1_b, A["ln1_b"][0]), (b_router, A["b_router"])):
            pool.dma_start(dst[:], a.partition_broadcast(P)).then_inc(late_loaded, 16)
        pool.dma_start(w_router[:], A["w_router"].rearrange("(c p) e -> p c e", p=P)).then_inc(late_loaded, 16)
        for t in range(TT):
            root(1, t)
            if t % 2:
                pool.wait_ge(scaled, t)
                pool.tensor_tensor(x1[:, t - 1, :], x1[:, t - 1, :], ln1_b[:], ALU.add).then_inc(x1_ready[t - 1], 1)

        def gather(n, q):
            pool.wait_ge(token_ready, n + 1)
            pool.sem_inc(pool_go, 1)
            pool.indirect_dma_start(out=xg[:, q, :], out_offset=None, in_=x1_dram,
                                    in_offset=bass.IndirectOffsetOnAxis(ap=slot_token[:, q:q + 1], axis=0),
                                    bounds_check=T - 1, oob_is_err=False).then_inc(gathered[q], 16)

        def scatter(n, q):
            for half in range(2):
                pool.wait_ge(*m_drained(M_Y + half, n))
                pool.sem_inc(pool_go, 1)
            pool.wait_ge(rows_ready, n + 1)
            pool.sem_inc(pool_go, 1)
            pool.indirect_dma_start(out=y_dram, out_offset=bass.IndirectOffsetOnAxis(ap=slot_row[:, q:q + 1], axis=0),
                                    in_=y[:, q, :], in_offset=None, bounds_check=2 * T - 1,
                                    oob_is_err=False).then_inc(y_stored[q], 16)

        pool.memset(xg[:], 0.0).then_inc(pool_step, 1)
        pool.wait_ge(pool_step, 2 * TT + 2)
        pool.wait_ge(x1_stored, 16 * TT)
        gather(0, 0)
        gather(1, 1)
        pool.wait_ge(*m_filled(M_XT + 1, 0))
        gather(2, 0)
        with pool.Fori(0, 6) as i:
            for q in range(2):
                pool.wait_ge(*m_filled(M_XT + 1, i * 2 + (q + 1)))
                pool.sem_inc(pool_go, 1)
                gather(i * 2 + (q + 3), 1 - q)
                scatter(i * 2 + q, q)
        pool.wait_ge(*m_filled(M_XT + 1, 13))
        gather(15, 1)
        scatter(12, 0)
        scatter(13, 1)
        for dst, a in ((ln2_g, "ln2_g"), (ln2_b, "ln2_b")):
            pool.dma_start(dst[:], A[a][0].partition_broadcast(P)).then_inc(ln2_loaded, 16)
        for t in range(TT):
            pool.tensor_scalar(x1[:, t, :], x1[:, t, :], ALPHA, None, ALU.mult).then_inc(x1_scaled, 1)
        scatter(14, 0)
        pool.wait_ge(y_stored[0], 16 * EXPERTS // 2)
        pool.wait_ge(y_stored[1], 16 * (EXPERTS // 2 - 1))
        pool.sem_inc(lower_stored, 1)
        scatter(15, 1)
        pool.wait_ge(flag_ready, 1)
        with pool.register("over_pool") as reg:
            pool.reg_load(reg, overflow[0:1, 0:1])
            with pool.If(pool.snap(reg) > 0):
                with pool.Fori(0, EXPERTS) as e:
                    for b in range(3):
                        n = e * 3 + (EXPERTS + b)
                        gather(n, 0)
                        scatter(n, 0)
                pool.wait_ge(y_stored[0], 16 * (EXPERTS // 2 + 3 * EXPERTS))
            with pool.Else():
                pool.wait_ge(y_stored[0], 16 * EXPERTS // 2)
        pool.wait_ge(y_stored[1], 16 * EXPERTS // 2)
        pool.sem_inc(all_stored, 1)
        pool.wait_ge(ln2_loaded, 32)
        for t in range(TT):
            root(2, t)
            if 1 <= t < TT - 1:
                pool.wait_ge(normalised, TT + t)
                pool.tensor_tensor(x1[:, t - 1, :], x1[:, t - 1, :], ln2_g[:], ALU.mult).then_inc(scaled, 1)

    @block.tensor
    def _(pe):
        def open_bank(name, i=None):
            if banks.at[name][1]:
                pe.wait_ge(*empty(name, i))

        def turn(name, tile, n=4):
            open_bank(name)
            for k in range(n):
                o = pe.transpose(bank(name)[:, k * P:(k + 1) * P], tile(k), ident)
            o.then_inc(fills(name), 1)

        def three(out, hi_l, lo_l, hi_r, lo_r, start, stop):
            pe.matmul(out, hi_l, hi_r, start=start, stop=False)
            pe.matmul(out, hi_l, lo_r, start=False, stop=False)
            return pe.matmul(out, lo_l, hi_r, start=False, stop=stop)

        def features(j, outs, x_hi, x_lo, per=0, i=None, chunk_there=None):
            pe.wait_ge(lo_cast, nth(j + 1, per, i))
            hi, lo = unit_of(hi_slot(j), len(outs) * P), unit_of(lo_slot(j), len(outs) * P)
            chunks = UNIT // (len(outs) * P)
            for d, name in enumerate(outs):
                open_bank(name, i)
                cols = slice(d * P, (d + 1) * P)
                for c in range(chunks):
                    if chunk_there is not None:
                        pe.wait_ge(*chunk_there(c))
                    o = three(bank(name)[:], hi[:, c, cols], lo[:, c, cols], x_hi[:, c, :], x_lo[:, c, :],
                              c == 0, c == chunks - 1)
            o.then_inc(unit_used, 1)

        def tokens(j, k, last, outs, x_hi, x_lo, choose, per=0, i=None):
            pe.wait_ge(lo_cast, nth(j + 1, per, i))
            hi, lo = unit_of(hi_slot(j), 512), unit_of(lo_slot(j), 512)
            for t, out in enumerate(outs):
                for c in range(2):
                    o = three(out, choose(x_hi[:, 2 * k + c, :], t), choose(x_lo[:, 2 * k + c, :], t), hi[:, c, :],
                              lo[:, c, :], k == 0 and c == 0, last and c == 1)
            o.then_inc(unit_used, 1)

        def scores(g):
            hp, seq = g // 2, g % 2
            open_bank(("scores", g))
            pe.wait_ge(*drained(("q", hp)))
            pe.wait_ge(*drained(("k", hp)))
            for h2 in range(2):
                rows = slice(64 * h2, 64 * h2 + 64)
                for j in range(4):
                    o = pe.matmul(bank(("scores", g))[rows, j * P:(j + 1) * P],
                                  qT[rows, hp, seq * SEQ + 64 * j:seq * SEQ + 64 * (j + 1)],
                                  grid(kT[rows, hp, :], seq, WINDOW[j], KCOLS), start=True, stop=True)
            o.then_inc(fills(("scores", g)), 1)

        def attend(g):
            hp, seq = g // 2, g % 2
            open_bank(("attended", g))
            pe.wait_ge(*drained(("probsT", g)))
            for j in range(4):
                o = pe.matmul(bank(("attended", g))[:, j * P:(j + 1) * P], v_win[:, seq, j, hp * P:(hp + 1) * P],
                              probsT[:, j * P:(j + 1) * P], start=True, stop=True)
            o.then_inc(fills(("attended", g)), 1)

        def in_row(x, t):
            return x[:, tokens_of(t)]

        pe.wait_ge(const_loaded, 16)
        pe.wait_ge(rows_loaded, 16 * 9)
        pe.transpose(bank("vectors")[:, 0:V_ALL], rows_v[0:V_ALL, :], ident[0:V_ALL, 0:V_ALL])
        pe.transpose(bank("vectors")[:, V_ALL:V_ALL + TAPS * WC], rows_c[0:TAPS * WC, :],
                     ident[0:TAPS * WC, 0:TAPS * WC]).then_inc(fills("vectors"), 1)
        for t in range(TT):
            pe.wait_ge(x0_normal, t + 1)
            for c in range(DC):
                name = ("x0T", c)
                if t == 0:
                    open_bank(name)
                o = pe.transpose(bank(name)[:, tokens_of(t)], x_in[:, t, c * P:(c + 1) * P], ident)
                if t == TT - 1:
                    o.then_inc(fills(name), 1)
        turn("w_s", lambda k: w_s[:, k, :])

        for u in range(U_MERGE):
            if u < U_V:
                features(u, [("glu_g" if u % 2 else "glu_a", u // 2)], xT_hi, xT_lo,
                         chunk_there=(lambda c: drained(("x0T", c))) if u == 0 else None)
            elif u < U_VSG:
                if u == U_V:
                    for t in range(TT):
                        open_bank(("v", t))
                tokens(u, u - U_V, u == U_V + 3, [bank(("v", t))[:] for t in range(TT)], xT_hi, xT_lo, in_row)
            elif u < U_QK:
                if u == U_VSG:
                    for t in range(TT):
                        open_bank(("vsg", t))
                tokens(u, u - U_VSG, u == U_VSG + 3, [bank(("vsg", t))[:] for t in range(TT)], xT_hi, xT_lo, in_row)
            elif u < U_USG:
                features(u, [("k" if u % 2 else "q", (u - U_QK) // 2)], xT_hi, xT_lo)
            else:
                c = u - U_USG
                features(u, [("usg", c)], xT_hi, xT_lo)
            if 18 <= u < 26:
                scores(u - 18)
            if u >= U_USG:
                c = u - U_USG
                open_bank(("spatial", c))
                pe.wait_ge(vs_ready, TT)
                pe.wait_ge(*drained("w_s"))
                for t in range(TT):
                    o = pe.matmul(bank(("spatial", c))[:, tokens_of(t)], vs[:, t, c * P:(c + 1) * P], w_sT[:, c, :],
                                  start=True, stop=True)
                o.then_inc(fills(("spatial", c)), 1)
            if 20 <= u < 28:
                if u == 20:
                    pe.wait_ge(v_windows, 16 * 8)
                attend(u - 20)
            if 19 <= u < 27:
                g = u - 19
                pe.wait_ge(probs_ready, g + 1)
                turn(("probsT", g), lambda k: probs[:, g % 2, k * P:(k + 1) * P])
            if u == 24:
                pe.wait_ge(conv_ready, WC - 2)
                pe.wait_ge(pool_conv, added(WC - 2, TAPS - 1))
                open_bank("conv_mean")
                for c in range(WC):
                    o = pe.matmul(bank("conv_mean")[:], ones, conv[:, c, :], start=c == 0, stop=c == WC - 1)
                o.then_inc(fills("conv_mean"), 1)
            if u == 25:
                open_bank("conv_var")
                for c in range(WC):
                    pe.wait_ge(squared, c + 1)
                    o = pe.matmul(bank("conv_var")[:], ones, squares[c], start=c == 0, stop=c == WC - 1)
                o.then_inc(fills("conv_var"), 1)

        with pe.Fori(0, 2) as i:
            for r in range(2):
                u = U_MERGE + 9 * r
                for d in range(2):
                    for n in range(3):
                        features(u, [("gate", r, d, n)], xT_hi, xT_lo, 18, i)
                        u += 1
                for n in range(3):
                    if n == 0:
                        pe.wait_ge(*drained(("attended", 7)))
                    elif n == 1:
                        pe.wait_ge(gated_lo, WC)
                    else:
                        pe.wait_ge(conv_lo, WC)
                    features(u, [("branch", r, d, n) for d in range(2)], branch_hi[n], branch_lo[n], 18, i)
                    u += 1
        for n in range(2):
            for t in range(TT):
                open_bank(("mixed", n, t))
            for k in range(1 if n else 4):
                pe.wait_ge(merged_lo, 2 * k + 2)
                tokens(U_WO + 4 * n + k, k, k == 3, [bank(("mixed", n, t))[:] for t in range(TT)], mT_hi, mT_lo,
                       in_row)
        for t in range(TT):
            name = ("mixed", 1, t)
            for k in range(1, 4):
                j = U_WO + 4 + k
                pe.wait_ge(lo_cast, j + 1)
                hi, lo = unit_of(hi_slot(j), 512), unit_of(lo_slot(j), 512)
                for c in range(2):
                    o = three(bank(name)[:], in_row(mT_hi[:, 2 * k + c, :], t), in_row(mT_lo[:, 2 * k + c, :], t),
                              hi[:, c, :], lo[:, c, :], False, k == 3 and c == 1)
            if t < TT - 1:
                o.then_inc(fills(name), 1)
            else:
                o.then_inc(unit_used, 3)

        pe.wait_ge(late_loaded, 16 * 4)
        for t in range(TT + 1):
            if t < TT:
                pe.wait_ge(x1_ready[t], 1)
                for half in range(2):
                    turn(("x1T", t, half), lambda k: x1[:, t, (4 * half + k) * P:(4 * half + k + 1) * P])
            if t:
                for half in range(2):
                    pe.wait_ge(*drained(("x1T", t - 1, half)))
                for c in range(DC):
                    o = pe.matmul(bank("router")[0:EXPERTS, tokens_of(t - 1)], w_router[:, c, :],
                                  x1T[:, c, tokens_of(t - 1)], start=c == 0, stop=c == DC - 1)
        o.then_inc(fills("router"), 1)
        pe.wait_ge(*drained("router"))
        open_bank("r_s")
        for t in range(TT):
            o = pe.transpose(bank("r_s")[:, t * EXPERTS:(t + 1) * EXPERTS], scoresT[0:EXPERTS, tokens_of(t)],
                             ident[0:EXPERTS, 0:EXPERTS])
        o.then_inc(fills("r_s"), 1)
        pe.wait_ge(selected, 1)
        open_bank("position")
        sel = r_sel[:].rearrange("p t g e -> p (t g e)")
        pe.matmul(bank("position")[:, 0:80], before, sel, start=True, stop=False)
        for k in range(1, TT + 1):
            at = EXPERTS * k
            o = pe.matmul(bank("position")[:, at:80], ones, sel[:, 0:80 - at], start=False, stop=k == TT)
        o.then_inc(fills("position"), 1)

        def slots(n, e, q):
            pe.wait_ge(onehot_ready, n + 1)
            pe.wait_ge(*m_empty(M_INFO, n))
            for t in range(TT):
                row = info[:, t, e, :] if isinstance(e, int) else info[:, t, bass.ds(e, 1), :].rearrange(
                    "p e k -> p (e k)")
                o = pe.matmul(psum[M_INFO][:, 0:4], onehot[:, q, t, :], row, start=t == 0, stop=t == TT - 1)
            o.then_inc(psum_full[M_INFO], 1)

        def turn_xg(n, q, gathers):
            pe.wait_ge(gathered[q], gathers * 16 + 16)
            for half in range(2):
                pe.wait_ge(*m_empty(M_XT + half, n))
                for k in range(4):
                    c = 4 * half + k
                    o = pe.transpose(psum[M_XT + half][:, k * P:(k + 1) * P], xg[:, q, c * P:(c + 1) * P], ident)
                o.then_inc(psum_full[M_XT + half], 1)

        def hidden(b, n, q, j, k, per=0, i=None):
            if k == 0:
                pe.wait_ge(*m_empty(b, n))
                for half in range(2):
                    pe.wait_ge(*m_drained(M_XT + half, n))
            tokens(j, k, k == 3, [psum[b][:]], xgT_hi[:, q], xgT_lo[:, q], lambda x, t: x, per, i)

        def turn_h(n):
            pe.wait_ge(*m_empty(M_HT, n))
            pe.wait_ge(*m_drained(M_H3, n))
            for k in range(4):
                o = pe.transpose(psum[M_HT][:, k * P:(k + 1) * P], h[:, k * P:(k + 1) * P], ident)
            o.then_inc(psum_full[M_HT], 1)

        def output(n, j, k, per=0, i=None):
            if k == 0:
                pe.wait_ge(*m_drained(M_HT, n))
            if k % 2 == 0:
                pe.wait_ge(*m_empty(M_Y + k // 2, n))
            tokens(j, k % 2, k % 2 == 1, [psum[M_Y + k // 2][:]], hT_hi, hT_lo, lambda x, t: x, per, i)

        pe.wait_ge(routed, 1)
        slots(0, 0, 0)
        slots(1, 1, 1)
        turn_xg(0, 0, 0)
        for k in range(4):
            hidden(M_H1, 0, 0, U_MOE + k, k)
        slots(2, 2, 0)

        def expert(n, q, j, gathers, more=True, per=0, i=None):
            for k in range(4):
                hidden(M_H3, n, q, j + k, k, per, i)
                if k == 1:
                    turn_xg(n + 1, 1 - q, gathers)
            for k in range(4):
                hidden(M_H1, n + 1, 1 - q, j + 4 + k, k, per, i)
                if k == 1:
                    turn_h(n)
            for k in range(4):
                output(n, j + 8 + k, k, per, i)
                if k == 1 and more:
                    slots(n + 3, n + 3, 1 - q)

        with pe.Fori(0, 6) as i:
            for q in range(2):
                expert(i * 2 + q, q, U_MOE + 4 + 12 * q, i + q, True, 24, i)
        for n in (12, 13, 14):
            expert(n, n % 2, U_MOE + 4 + 12 * n, (n + 1) // 2, n == 12)
        j = U_MOE + 4 + 12 * 15
        for k in range(4):
            hidden(M_H3, 15, 1, j + k, k)
        turn_h(15)
        for k in range(4):
            output(15, j + 4 + k, k)

        pe.wait_ge(flag_ready, 1)
        with pe.register("over_pe") as reg:
            pe.reg_load(reg, overflow[0:1, 0:1])
            with pe.If(pe.snap(reg) > 0):
                with pe.Fori(0, EXPERTS) as e:
                    for b in range(3):
                        n, j = e * 3 + (EXPERTS + b), U_OVER + 12 * b
                        slots(n, e, 0)
                        turn_xg(n, 0, e * 3 + (EXPERTS // 2 + b))
                        for k in range(4):
                            hidden(M_H1, n, 0, j + k, k, 36, e)
                        for k in range(4):
                            hidden(M_H3, n, 0, j + 4 + k, k, 36, e)
                        turn_h(n)
                        for k in range(4):
                            output(n, j + 8 + k, k, 36, e)
                pe.nop()
            with pe.Else():
                pe.nop()

    moe.close()
    ctx.close()


_INS = ["x_prompt", "x_sample", "emb_ln_g", "emb_ln_b", "w_in", "b_in", "w_gate", "b_gate", "rpb", "w_a_o",
        "sg_ln_g", "sg_ln_b", "w_s", "b_s", "w_b_o", "conv_w", "conv_b", "cv_ln_g", "cv_ln_b", "w_c_o", "w_o", "b_o",
        "ln1_g", "ln1_b", "w_router", "b_router", "w_e1", "w_e3", "w_e2", "ln2_g", "ln2_b"]


def constants():
    import numpy as np

    c = np.zeros((P, C_ALL), np.float32)
    p = np.arange(P)
    c[:, C_IDENT:C_IDENT + P] = np.eye(P)
    c[:, C_BEFORE:C_BEFORE + P] = p[:, None] < p[None, :]
    c[:, C_IOTA:C_IOTA + P] = p
    c[:, C_ONES:C_ONES + P] = 1
    c[:, C_TOKEN:C_TOKEN + TT] = p[:, None] + P * np.arange(TT)
    c[:, C_HIGHER:C_HIGHER + EXPERTS] = 3 - np.arange(EXPERTS) % 4
    for pat, j in ((0, 0), (1, 1), (2, 3)):
        query = QCOLS * j + p % QCOLS
        start = np.clip(query - QCOLS // 2, 0, GRID - QCOLS)
        key = WINDOW[j] + np.arange(KCOLS)
        inside = (key >= start[:, None]) & (key < start[:, None] + QCOLS)
        c[:, C_MASK + KCOLS * pat:C_MASK + KCOLS * (pat + 1)] = np.where(inside, 0, -1e30)
    return c


def kernel(**inputs):
    import numpy as _np
    import concourse.bacc as _bacc
    from concourse import mybir as _mybir
    from concourse.bass_utils import run_bass_kernel_spmd as _run

    nc = _bacc.Bacc("TRN2", target_bir_lowering=False, num_devices=1)
    arrays, args = {}, {}
    for name in _INS + ["consts"]:
        a = constants() if name == "consts" else _np.ascontiguousarray(inputs[name])
        arrays[f"in_{name}_dram"] = a
        args[name] = nc.dram_tensor(f"in_{name}_dram", a.shape, _mybir.dt.from_np(a.dtype), kind="ExternalInput").ap()
    outs = [nc.dram_tensor(f"out_{i}_dram", (1, SEQ, D), F32, kind="ExternalOutput").ap() for i in range(2)]
    encoder_layer(nc, args, *outs)
    r = _run(nc, [arrays], core_ids=[0])
    return tuple(r.results[0][f"out_{i}_dram"] for i in range(2))
```
